# Optimizing a Trainium2 kernel written in Bass

```python
import math
import jax, jax.numpy as jnp
from jax import lax
import numpy as np

D_MODEL = 1024
BATCH = 1
SEQ = 256
DEPTH = 2

HEAD_DIM = 64
Q_BLOCK = 128
A_HEADS = 8
A_KV_HEADS = 2
A_WINDOW = 128
B_HEADS = 8
C_HEADS = 8
C_BLOCK = 256
C_TOPK = 3
MOBA_Q_CHUNK = 16
D_HEADS = 8
D_KV_HEADS = 2
NSA_CMP_LEN = 32
NSA_CMP_STRIDE = 16
NSA_SLC_BLOCK = 64
NSA_TOPN = 16
NSA_WINDOW = 512
NSA_Q_CHUNK = 64
FORCE_BONUS = 1000.0
N_GROUPS = 4
EXPERTS_PER_GROUP = 8
N_EXPERTS = N_GROUPS * EXPERTS_PER_GROUP
EXPERT_FF = 256
TOP_K_IN_GROUP = 2

EPS = 1e-6
NEG = -1e30
MIX_WIDTH = (A_HEADS + B_HEADS) * HEAD_DIM
EVEN_WIDTHS = (A_HEADS * HEAD_DIM, A_KV_HEADS * HEAD_DIM, A_KV_HEADS * HEAD_DIM,
               B_HEADS * HEAD_DIM, B_HEADS * HEAD_DIM, B_HEADS * HEAD_DIM)
ODD_WIDTHS = (C_HEADS * HEAD_DIM, C_HEADS * HEAD_DIM, C_HEADS * HEAD_DIM,
              D_HEADS * HEAD_DIM) + (D_KV_HEADS * HEAD_DIM,) * 6 + (D_HEADS * 3,)
EVEN_IN = sum(EVEN_WIDTHS)
ODD_IN = sum(ODD_WIDTHS)

kernel_name = 'hybrid_swa_sink_stickbreak_moba_nsa_hmoe'

def rms_norm(x, g):
    xf = x.astype(jnp.float32)
    y = xf * lax.rsqrt(jnp.mean(xf * xf, axis=-1, keepdims=True) + EPS)
    return (y * g.astype(jnp.float32)).astype(x.dtype)

def _split(x, widths):
    offs = np.cumsum([0] + list(widths))
    return [x[..., int(offs[i]):int(offs[i + 1])] for i in range(len(widths))]

def _alibi_slopes(n_heads):
    return jnp.asarray(2.0 ** (-8.0 * np.arange(1, n_heads + 1) / n_heads), dtype=jnp.float32)

def banded_attention(q, k, v, window, slopes, sink=None):
    b, s, h, d = q.shape
    hkv = k.shape[2]
    g = h // hkv
    nb = s // Q_BLOCK
    npre = window // Q_BLOCK
    pad = ((0, 0), (npre * Q_BLOCK, 0), (0, 0), (0, 0))
    kp = jnp.pad(k, pad).reshape(b, nb + npre, Q_BLOCK, hkv, d)
    vp = jnp.pad(v, pad).reshape(b, nb + npre, Q_BLOCK, hkv, d)
    kw = jnp.concatenate([kp[:, j:j + nb] for j in range(npre + 1)], axis=2)
    vw = jnp.concatenate([vp[:, j:j + nb] for j in range(npre + 1)], axis=2)
    qb = q.reshape(b, nb, Q_BLOCK, hkv, g, d)
    sc = jnp.einsum('bnqhgd,bnkhd->bnhgqk', qb, kw).astype(jnp.float32) / math.sqrt(d)
    qpos = jnp.arange(nb)[:, None] * Q_BLOCK + jnp.arange(Q_BLOCK)[None, :]
    kpos = (jnp.arange(nb)[:, None] - npre) * Q_BLOCK + jnp.arange((npre + 1) * Q_BLOCK)[None, :]
    diff = qpos[:, :, None] - kpos[:, None, :]
    mask = (diff >= 0) & (diff < window) & (kpos[:, None, :] >= 0)
    m_h = slopes.reshape(hkv, g)[:, :, None, None]
    diff_f = diff.astype(jnp.float32)[None, :, None, None]
    sc = jnp.where(mask[None, :, None, None], sc - m_h * diff_f, NEG)
    if sink is None:
        p = jax.nn.softmax(sc, axis=-1)
    else:
        sk = sink.astype(jnp.float32).reshape(hkv, g)[None, None, :, :, None, None]
        mx = jnp.maximum(sc.max(axis=-1, keepdims=True), sk)
        e = jnp.exp(sc - mx)
        p = e / (e.sum(axis=-1, keepdims=True) + jnp.exp(sk - mx))
    o = jnp.einsum('bnhgqk,bnkhd->bnqhgd', p, vw.astype(jnp.float32))
    return o.reshape(b, s, h, d).astype(q.dtype)

def stick_breaking_attention(q, k, v):
    b, s, h, d = q.shape
    nb = s // Q_BLOCK
    qb = q.reshape(b, nb, Q_BLOCK, h, d).transpose(1, 0, 2, 3, 4)
    kpos = jnp.arange(s)
    vf = v.astype(jnp.float32)

    def block(args):
        qi, i = args
        z = jnp.einsum('bqhd,bkhd->bhqk', qi, k).astype(jnp.float32) / math.sqrt(d)
        qpos = i * Q_BLOCK + jnp.arange(Q_BLOCK)
        mask = kpos[None, :] < qpos[:, None]
        log_keep = jnp.where(mask, jax.nn.log_sigmoid(-z), 0.0)
        suffix = lax.cumsum(log_keep, axis=3, reverse=True) - log_keep
        a = jnp.where(mask, jnp.exp(jax.nn.log_sigmoid(z) + suffix), 0.0)
        return jnp.einsum('bhqk,bkhd->bqhd', a, vf)

    o = lax.map(block, (qb, jnp.arange(nb)))
    return o.transpose(1, 0, 2, 3, 4).reshape(b, s, h, d).astype(q.dtype)

def moba_attention(q, k, v, slopes):
    b, s, h, d = q.shape
    nblk = -(-s // C_BLOCK)
    s_pad = nblk * C_BLOCK
    pad = ((0, 0), (0, s_pad - s), (0, 0), (0, 0))
    q, k, v = jnp.pad(q, pad), jnp.pad(k, pad), jnp.pad(v, pad)
    kb = k.reshape(b, nblk, C_BLOCK, h, d).transpose(0, 3, 1, 2, 4)
    vb = v.reshape(b, nblk, C_BLOCK, h, d).transpose(0, 3, 1, 2, 4)
    gate = jnp.einsum('bshd,bhnd->bhsn', q, kb.mean(axis=3)).astype(jnp.float32)
    own = jnp.arange(s_pad) // C_BLOCK
    past = jnp.arange(nblk)[None, :] < own[:, None]
    gate = jnp.where(past, gate, NEG)
    _, top_idx = lax.top_k(gate, min(C_TOPK, nblk))
    top_valid = top_idx < own[:, None]
    idx = jnp.concatenate([top_idx, jnp.broadcast_to(own[:, None], (b, h, s_pad, 1))], axis=-1)
    valid = jnp.concatenate([top_valid, jnp.ones((b, h, s_pad, 1), dtype=bool)], axis=-1)
    nc = s_pad // MOBA_Q_CHUNK

    def to_chunks(a):
        return jnp.moveaxis(a.reshape(b, h, nc, MOBA_Q_CHUNK, *a.shape[3:]), 2, 0)

    bi = jnp.arange(b)[:, None, None, None]
    hi = jnp.arange(h)[None, :, None, None]

    def chunk(args):
        qi, ii, vi, ci = args
        ks = kb[bi, hi, ii]
        vs = vb[bi, hi, ii]
        sc = jnp.einsum('bhqd,bhqnkd->bhqnk', qi, ks).astype(jnp.float32) / math.sqrt(d)
        qpos = ci * MOBA_Q_CHUNK + jnp.arange(MOBA_Q_CHUNK)
        kpos = ii[..., None] * C_BLOCK + jnp.arange(C_BLOCK)
        diff = (qpos[:, None, None] - kpos).astype(jnp.float32)
        mask = vi[..., None] & (diff >= 0)
        sc = jnp.where(mask, sc - slopes[:, None, None, None] * diff, NEG)
        p = jax.nn.softmax(sc.reshape(b, h, MOBA_Q_CHUNK, -1), axis=-1).reshape(sc.shape)
        return jnp.einsum('bhqnk,bhqnkd->bhqd', p, vs.astype(jnp.float32))

    o = lax.map(chunk, (to_chunks(q.transpose(0, 2, 1, 3)), to_chunks(idx), to_chunks(valid), jnp.arange(nc)))
    o = jnp.moveaxis(o, 0, 2).reshape(b, h, s_pad, d).transpose(0, 2, 1, 3)[:, :s]
    return o.astype(q.dtype)

def compress_blocks(x, pos_emb, w):
    s = x.shape[1]
    n_cmp = (s - NSA_CMP_LEN) // NSA_CMP_STRIDE + 1
    idx = np.arange(n_cmp)[:, None] * NSA_CMP_STRIDE + np.arange(NSA_CMP_LEN)[None, :]
    blocks = x[:, idx] + pos_emb[None, None, :, None, :]
    return jnp.einsum('bnlhd,lde->bnhe', blocks, w)

def nsa_attention(q, k_cmp, v_cmp, k_slc, v_slc, k_win, v_win, gates, slopes):
    b, s, h, d = q.shape
    hkv = k_slc.shape[2]
    g = h // hkv
    n_cmp = k_cmp.shape[1]
    pos = jnp.arange(s)
    m_h = slopes.reshape(hkv, g)
    qg = q.reshape(b, s, hkv, g, d)
    cmp_end = jnp.arange(n_cmp) * NSA_CMP_STRIDE + NSA_CMP_LEN - 1
    diff_c = (pos[:, None] - cmp_end[None, :]).astype(jnp.float32)
    mask_c = diff_c >= 0
    sc = jnp.einsum('bshgd,bnhd->bhgsn', qg, k_cmp).astype(jnp.float32) / math.sqrt(d)
    sc = jnp.where(mask_c, sc - m_h[:, :, None, None] * diff_c, NEG)
    e = jnp.where(mask_c, jnp.exp(sc - sc.max(axis=-1, keepdims=True)), 0.0)
    den = e.sum(axis=-1, keepdims=True)
    p_cmp = e / jnp.where(den > 0, den, 1.0)
    o_cmp = jnp.einsum('bhgsn,bnhd->bshgd', p_cmp, v_cmp.astype(jnp.float32)).reshape(b, s, h, d)
    n_slc = s // NSA_SLC_BLOCK
    cst = np.arange(n_cmp)[:, None] * NSA_CMP_STRIDE
    sst = np.arange(n_slc)[None, :] * NSA_SLC_BLOCK
    overlap = jnp.asarray(((cst < sst + NSA_SLC_BLOCK) & (cst + NSA_CMP_LEN > sst)).astype(np.float32))
    p_slc = jnp.einsum('bhgsn,nj->bhsj', p_cmp, overlap)
    cur = pos // NSA_SLC_BLOCK
    j = jnp.arange(n_slc)[None, :]
    forced = (j == 0) | (j == cur[:, None]) | (j == cur[:, None] - 1)
    score = jnp.where(j <= cur[:, None], p_slc + jnp.where(forced, FORCE_BONUS, 0.0), NEG)
    _, sel = lax.top_k(score, min(NSA_TOPN, n_slc))
    sel_valid = sel <= cur[:, None]
    ksb = k_slc.reshape(b, n_slc, NSA_SLC_BLOCK, hkv, d).transpose(0, 3, 1, 2, 4)
    vsb = v_slc.reshape(b, n_slc, NSA_SLC_BLOCK, hkv, d).transpose(0, 3, 1, 2, 4)
    nc = s // NSA_Q_CHUNK
    qc = jnp.moveaxis(qg.transpose(0, 2, 3, 1, 4).reshape(b, hkv, g, nc, NSA_Q_CHUNK, d), 3, 0)
    selc = jnp.moveaxis(sel.reshape(b, hkv, nc, NSA_Q_CHUNK, -1), 2, 0)
    valc = jnp.moveaxis(sel_valid.reshape(b, hkv, nc, NSA_Q_CHUNK, -1), 2, 0)
    bi = jnp.arange(b)[:, None, None, None]
    hi = jnp.arange(hkv)[None, :, None, None]

    def chunk(args):
        qi, si, vi, c = args
        ks = ksb[bi, hi, si]
        vs = vsb[bi, hi, si]
        scs = jnp.einsum('bhgqd,bhqnkd->bhgqnk', qi, ks).astype(jnp.float32) / math.sqrt(d)
        qpos = c * NSA_Q_CHUNK + jnp.arange(NSA_Q_CHUNK)
        kpos = si[..., None] * NSA_SLC_BLOCK + jnp.arange(NSA_SLC_BLOCK)
        diff = (qpos[:, None, None] - kpos).astype(jnp.float32)
        mask = vi[..., None] & (diff >= 0)
        scs = jnp.where(mask[:, :, None], scs - m_h[None, :, :, None, None, None] * diff[:, :, None], NEG)
        p = jax.nn.softmax(scs.reshape(b, hkv, g, NSA_Q_CHUNK, -1), axis=-1).reshape(scs.shape)
        return jnp.einsum('bhgqnk,bhqnkd->bhgqd', p, vs.astype(jnp.float32))

    o_slc = lax.map(chunk, (qc, selc, valc, jnp.arange(nc)))
    o_slc = jnp.moveaxis(o_slc, 0, 3).reshape(b, hkv, g, s, d).transpose(0, 3, 1, 2, 4).reshape(b, s, h, d)
    o_win = banded_attention(q, k_win, v_win, NSA_WINDOW, slopes).astype(jnp.float32)
    gf = gates.astype(jnp.float32)
    o = gf[..., 0:1] * o_cmp + gf[..., 1:2] * o_slc + gf[..., 2:3] * o_win
    return o.astype(q.dtype)

def even_mixer(x, norm_g, w_in, q_norm, k_norm, sink, w_out):
    b, s, _ = x.shape
    proj = rms_norm(x, norm_g) @ w_in
    qa, ka, va, qb, kb, vb = _split(proj, EVEN_WIDTHS)
    qa = rms_norm(qa.reshape(b, s, A_HEADS, HEAD_DIM), q_norm)
    ka = rms_norm(ka.reshape(b, s, A_KV_HEADS, HEAD_DIM), k_norm)
    va = va.reshape(b, s, A_KV_HEADS, HEAD_DIM)
    oa = banded_attention(qa, ka, va, A_WINDOW, _alibi_slopes(A_HEADS), sink)
    ob = stick_breaking_attention(qb.reshape(b, s, B_HEADS, HEAD_DIM),
                                  kb.reshape(b, s, B_HEADS, HEAD_DIM),
                                  vb.reshape(b, s, B_HEADS, HEAD_DIM))
    o = jnp.concatenate([oa.reshape(b, s, -1), ob.reshape(b, s, -1)], axis=-1)
    return x + o @ w_out

def odd_mixer(x, norm_g, w_in, c_q_norm, c_k_norm, d_q_norm, d_k_norm, cmp_pos, cmp_w, w_out):
    b, s, _ = x.shape
    proj = rms_norm(x, norm_g) @ w_in
    qc, kc, vc, qd, kcmp, vcmp, kslc, vslc, kwin, vwin, gd = _split(proj, ODD_WIDTHS)

    def heads(t, n):
        return t.reshape(b, s, n, HEAD_DIM)

    oc = moba_attention(rms_norm(heads(qc, C_HEADS), c_q_norm), rms_norm(heads(kc, C_HEADS), c_k_norm),
                        heads(vc, C_HEADS), _alibi_slopes(C_HEADS))
    k_cmp = rms_norm(compress_blocks(heads(kcmp, D_KV_HEADS), cmp_pos[0], cmp_w[0]), d_k_norm[0])
    v_cmp = compress_blocks(heads(vcmp, D_KV_HEADS), cmp_pos[1], cmp_w[1])
    od = nsa_attention(rms_norm(heads(qd, D_HEADS), d_q_norm), k_cmp, v_cmp,
                       rms_norm(heads(kslc, D_KV_HEADS), d_k_norm[1]), heads(vslc, D_KV_HEADS),
                       rms_norm(heads(kwin, D_KV_HEADS), d_k_norm[2]), heads(vwin, D_KV_HEADS),
                       jax.nn.sigmoid(gd.reshape(b, s, D_HEADS, 3)), _alibi_slopes(D_HEADS))
    o = jnp.concatenate([oc.reshape(b, s, -1), od.reshape(b, s, -1)], axis=-1)
    return x + o @ w_out

def hier_moe(x, norm_g, w_grp, b_grp, w_exp, b_exp, w_gate, w_up, w_down):
    shp = x.shape
    h = rms_norm(x, norm_g).reshape(-1, D_MODEL)
    t = h.shape[0]
    grp_logits = (h @ w_grp).astype(jnp.float32) + b_grp.astype(jnp.float32)
    grp_prob = jax.nn.softmax(grp_logits, axis=-1)
    g_sel = jnp.argmax(grp_logits, axis=-1)
    p_g = jnp.take_along_axis(grp_prob, g_sel[:, None], axis=1)
    exp_logits = ((h @ w_exp).astype(jnp.float32) + b_exp.astype(jnp.float32)).reshape(t, N_GROUPS, EXPERTS_PER_GROUP)
    within = jnp.take_along_axis(exp_logits, g_sel[:, None, None], axis=1)[:, 0]
    top_p, top_i = lax.top_k(jax.nn.softmax(within, axis=-1), TOP_K_IN_GROUP)
    wts = p_g * top_p / top_p.sum(axis=-1, keepdims=True)
    expert_id = g_sel[:, None] * EXPERTS_PER_GROUP + top_i
    comb = (jax.nn.one_hot(expert_id, N_EXPERTS, dtype=jnp.float32) * wts[..., None]).sum(axis=1)

    def step(acc, params):
        wg, wu, wd, c = params
        y = (jax.nn.silu(h @ wg) * (h @ wu)) @ wd
        return acc + c[:, None].astype(y.dtype) * y, None

    acc, _ = lax.scan(step, jnp.zeros_like(h), (w_gate, w_up, w_down, comb.T))
    return x + acc.reshape(shp)

def setup_inputs(seed: int = 0) -> dict:
    key = jax.random.key(seed)
    ks = iter(jax.random.split(key, 32))
    ne, no = (DEPTH + 1) // 2, DEPTH // 2

    def nrm(shape, scale):
        return scale * jax.random.normal(next(ks), shape, jnp.float32)

    def gain(shape):
        return 1.0 + nrm(shape, 0.02)

    return {
        'x': nrm((BATCH, SEQ, D_MODEL), 1.0),
        'ev_norm': gain((ne, D_MODEL)),
        'ev_w_in': nrm((ne, D_MODEL, EVEN_IN), D_MODEL ** -0.5),
        'ev_q_norm': gain((ne, HEAD_DIM)),
        'ev_k_norm': gain((ne, HEAD_DIM)),
        'ev_sink': nrm((ne, A_HEADS), 0.5),
        'ev_w_out': nrm((ne, MIX_WIDTH, D_MODEL), MIX_WIDTH ** -0.5),
        'od_norm': gain((no, D_MODEL)),
        'od_w_in': nrm((no, D_MODEL, ODD_IN), D_MODEL ** -0.5),
        'od_c_q_norm': gain((no, HEAD_DIM)),
        'od_c_k_norm': gain((no, HEAD_DIM)),
        'od_d_q_norm': gain((no, HEAD_DIM)),
        'od_d_k_norm': gain((no, 3, HEAD_DIM)),
        'od_cmp_pos': nrm((no, 2, NSA_CMP_LEN, HEAD_DIM), 0.1),
        'od_cmp_w': nrm((no, 2, NSA_CMP_LEN, HEAD_DIM, HEAD_DIM), (NSA_CMP_LEN * HEAD_DIM) ** -0.5),
        'od_w_out': nrm((no, MIX_WIDTH, D_MODEL), MIX_WIDTH ** -0.5),
        'moe_norm': gain((DEPTH, D_MODEL)),
        'moe_w_grp': nrm((DEPTH, D_MODEL, N_GROUPS), D_MODEL ** -0.5),
        'moe_b_grp': nrm((DEPTH, N_GROUPS), 0.01),
        'moe_w_exp': nrm((DEPTH, D_MODEL, N_EXPERTS), D_MODEL ** -0.5),
        'moe_b_exp': nrm((DEPTH, N_EXPERTS), 0.01),
        'moe_w_gate': nrm((DEPTH, N_EXPERTS, D_MODEL, EXPERT_FF), D_MODEL ** -0.5),
        'moe_w_up': nrm((DEPTH, N_EXPERTS, D_MODEL, EXPERT_FF), D_MODEL ** -0.5),
        'moe_w_down': nrm((DEPTH, N_EXPERTS, EXPERT_FF, D_MODEL), EXPERT_FF ** -0.5),
    }

def reference(x, ev_norm, ev_w_in, ev_q_norm, ev_k_norm, ev_sink, ev_w_out,
              od_norm, od_w_in, od_c_q_norm, od_c_k_norm, od_d_q_norm, od_d_k_norm,
              od_cmp_pos, od_cmp_w, od_w_out,
              moe_norm, moe_w_grp, moe_b_grp, moe_w_exp, moe_b_exp, moe_w_gate, moe_w_up, moe_w_down):
    for layer in range(DEPTH):
        i = layer // 2
        if layer % 2 == 0:
            x = even_mixer(x, ev_norm[i], ev_w_in[i], ev_q_norm[i], ev_k_norm[i], ev_sink[i], ev_w_out[i])
        else:
            x = odd_mixer(x, od_norm[i], od_w_in[i], od_c_q_norm[i], od_c_k_norm[i], od_d_q_norm[i],
                          od_d_k_norm[i], od_cmp_pos[i], od_cmp_w[i], od_w_out[i])
        x = hier_moe(x, moe_norm[layer], moe_w_grp[layer], moe_b_grp[layer], moe_w_exp[layer],
                     moe_b_exp[layer], moe_w_gate[layer], moe_w_up[layer], moe_w_down[layer])
    return x


_drawn_inputs = setup_inputs


def setup_inputs(seed=0):
    import zlib

    import numpy as np

    out = dict(_drawn_inputs(seed))
    spreads = {}
    factors = {'ev_q_norm': 2.815,
     'ev_k_norm': 3.755,
     'od_norm': 3.784,
     'od_c_q_norm': 8.0,
     'od_c_k_norm': 8.0,
     'od_d_q_norm': 8.0,
     'od_d_k_norm': 8.0,
     'moe_b_grp': 3.04,
     'od_cmp_pos': 3.953}
    for name, (base, spread) in spreads.items():
        noise = np.random.default_rng([zlib.crc32(name.encode()), seed]).standard_normal(out[name].shape)
        drawn = base * np.exp(spread * noise) if base else spread * noise
        out[name] = __import__('jax').numpy.asarray(drawn.astype(out[name].dtype))
    for name, factor in factors.items():
        out[name] = (out[name] * factor).astype(out[name].dtype)
    return out
```

```python
from contextlib import ExitStack

import concourse.bass as bass
from concourse import mybir

P = 128
S = 256
NT = S // P
D = 1024
KD = D // P
DH = 64
EV_IN = 2304
OD_IN = 2840
NG, EG, NE, FF = 4, 8, 32, 256
KF = FF // P
UNIT = 2048
UC = UNIT // KD
RING = 12
PER_EXPERT = 3
BODY = RING // PER_EXPERT
EV_UNITS = EV_IN // UC
OD_UNITS = OD_IN // UC
OUT_UNITS = D * D // (P * UNIT)
GATES = OD_IN - OD_UNITS * UC
TILE = 64
SLOTS = 2 * S
PADDED = SLOTS + TILE
MAXOVER = 7
EPS = 1e-6
NEG = -1e30
SC = P + S
NCMP = 16
WIN, CSTEP, CLEN = 128, 16, 32

F32 = mybir.dt.float32
I32 = mybir.dt.int32
ALU = mybir.AluOpType
ACT = mybir.ActivationFunctionType
AX = mybir.AxisListType.X

U_EV_IN = 0
U_EV_OUT = U_EV_IN + EV_UNITS
U_MOE0 = U_EV_OUT + OUT_UNITS
U_OD_IN = U_MOE0 + PER_EXPERT * NE
U_CMP = U_OD_IN + OD_UNITS
U_OD_OUT = U_CMP + 1
U_MOE1 = U_OD_OUT + OUT_UNITS
U_END = U_MOE1 + PER_EXPERT * NE
U_MOE = (U_MOE0, U_MOE1)

SLOPES = [2.0 ** -(h + 1) for h in range(8)]


def even_jobs():
    return [("A", h) for h in range(8)] + [("B", h) for h in range(8)]


def odd_jobs():
    return [("C", h) for h in range(8)] + [("L", h) for h in range(8)] + [("W", h) for h in range(8)]


JOBS = (even_jobs(), odd_jobs())
ORDER = (
    [("unit", 0, "dve", 4), ("unit", 1, "dve", 4), ("unit", 2, "dve", 2), ("turn", "qa"),
     ("unit", 3, "act"), ("turn", "ka"), ("steps", 0, 2), ("unit", 4, "act"), ("steps", 2, 4),
     ("unit", 5, "act"), ("turn", "qb"), ("steps", 4, 6), ("unit", 6, "act"), ("steps", 6, 7),
     ("unit", 7, "act"), ("turn", "kb"), ("steps", 7, 9), ("unit", 8, "act"), ("steps", 9, 19)],
    [("unit", 0, "dve", 4), ("unit", 1, "dve", 4), ("unit", 2, "dve", 4), ("turn", "qc"),
     ("unit", 3, "dve", 4), ("unit", 4, "act"), ("turn", "kc"), ("steps", 0, 1), ("unit", 5, "act"),
     ("steps", 1, 3), ("unit", 6, "dve", 4), ("steps", 3, 5), ("unit", 7, "dve", 4), ("steps", 5, 6),
     ("unit", 8, "act"), ("turn", "qd"), ("steps", 6, 8), ("unit", 9, "dve", 2), ("unit", 10, "dve", 2),
     ("cmp", "pos"), ("turn", "ks"), ("turn", "kw"), ("cmp", "in"), ("steps", 8, 9), ("cmp", "compress"),
     ("steps", 9, 10), ("cmp", "keys"), ("steps", 10, 11), ("cmp", "scores"), ("steps", 11, 12),
     ("cmp", "p"), ("steps", 12, 13), ("cmp", "values"), ("steps", 13, 27)])


def turns_before(name):
    a = b = 0
    for layer in range(2):
        a, b = a + 2, b + 2
        for what, *arg in ORDER[layer]:
            if what == "turn" or what == "cmp" and arg[0] in ("pos", "keys", "p"):
                both = arg[0] in ("qa", "qb", "kb", "qc", "kc", "qd")
                a += both or arg[0] in ("ks", "pos", "keys", "p")
                b += both or arg[0] in ("ka", "kw")
                if arg[0] == name:
                    return a, b
        a, b = a + 2 + 2 + 1, b + 2 + 2 + 1


T_QA_A, T_QA_B = turns_before("qa")
T_QC_A, T_QC_B = turns_before("qc")
T_POS = turns_before("pos")[0]
PR, NMN = [], []
for kind, _ in JOBS[0] + JOBS[1]:
    PR.append((PR or [0])[-1] + (1 if kind == "B" else 2))
    NMN.append((NMN or [0])[-1] + (kind != "B"))
V_THERE = {0: ("dve", 3), 8: ("act", 6), 16: ("act", 8), 24: ("dve", 10), 32: ("dve", 11)}
N_LOADS = 28
N_CONST_A, N_CONST = 5, 11
CF_COMPRESSED = 2
CD_T2, CD_KEYS, CD_ARG, CD_P = 1, 2, 4, 5
SKEW = 3


def program(nc, x, ev_norm, ev_w_in, ev_q_norm, ev_k_norm, ev_sink, ev_w_out,
            od_norm, od_w_in, od_c_q_norm, od_c_k_norm, od_d_q_norm, od_d_k_norm,
            od_cmp_pos, od_cmp_w, od_w_out,
            moe_norm, moe_w_grp, moe_b_grp, moe_w_exp, moe_b_exp, moe_w_gate, moe_w_up, moe_w_down,
            out):
    with ExitStack() as ctx:
        def sb(name, shape, dt=F32):
            return ctx.enter_context(nc.sbuf_tensor(name, shape, dt))

        def sem(name):
            return ctx.enter_context(nc.semaphore(name))

        ring = sb("ring", [P, RING, UNIT])
        xs = sb("x_res", [P, NT, D])
        xn = sb("x_normed", [P, NT, D])
        hT = sb("h_transposed", [P, KD, S])
        o_sb = xn
        oT = hT
        ident = sb("ident", [P, P])
        before = sb("before", [P, P])
        ones = sb("ones", [P, P])
        iota_s = sb("iota_slots", [P, SLOTS])
        iota8 = sb("iota_8", [P, NT, EG])
        iota_e = sb("iota_experts", [P, NE])
        g_col = sb("norm_gains", [P, 4, KD])
        w_rt = sb("router_w", [P, 2, KD, NG + NE])
        b_rt = sb("router_b", [P, 2, NG + NE])
        w_gd = sb("gate_w", [P, KD, GATES])
        qk_g = sb("qk_gains", [P, 8])
        sink = sb("sink", [P, 8])
        eps_t = sb("eps", [P, 1])
        one_t = sb("one", [P, 1])
        ssq = sb("ssq", [P, NT])
        lnr = sb("ln_ms", [P, NT])
        rstd = sb("rstd", [P, NT])
        pos_in = sb("pos_rows", [NCMP, 2, P])

        ARENA = 19700
        arena = sb("arena", [P, ARENA])
        at = [0]

        def carve(*dims):
            n = 1
            for v in dims:
                n *= v
            a = arena[:, at[0]:at[0] + n]
            at[0] += n
            assert at[0] <= ARENA, at[0]
            if len(dims) > 1:
                names = "abcd"[:len(dims)]
                a = a.rearrange(f"p ({' '.join(names)}) -> p {' '.join(names)}", **dict(zip(names, dims)))
            return a

        btab = carve(8, SC)
        smask = carve(SC)
        sreset = carve(SC)
        stage = [carve(NT, 512) for _ in range(2)]
        stk = [carve(NT, 128) for _ in range(2)]
        qT = [carve(4, S) for _ in range(2)]
        kT = carve(4, S)
        kTp = [carve(S) for _ in range(2)]
        vbig = carve(NT, 512)
        vsm = [carve(NT, 128) for _ in range(2)]
        sq = carve(NT, 4, DH)
        red = carve(NT, 4)
        lq = carve(NT, 4)
        rq = carve(NT, 4)
        s_sb = [carve(SC) for _ in range(2)]
        mark = at[0]
        ea = [carve(SC) for _ in range(2)]
        la = [carve(SC) for _ in range(2)]
        cu = [carve(SC) for _ in range(2)]
        end, at[0] = at[0], mark
        t2 = [carve(2, S) for _ in range(2)]
        cin = carve(NT, 4, 2, DH)
        v_blk = carve(8, DH)
        at[0] = max(at[0], end)
        p_sb = [carve(SC) for _ in range(3)]
        pT = [carve(SC) for _ in range(2)]
        mx = carve(24, 2)
        nm = carve(24, 2)
        den = carve(24, 2)
        es = carve(8, 2)
        cf = carve(8, 2)
        otmp = carve(NT, 4 * DH)
        posT = carve(2, NCMP)
        kc_n = carve(DH)
        vc = carve(DH)
        spread = carve(4, 32)
        kc_b = carve(2, DH)
        kcT = carve(32)
        ctab = carve(NT, 4, 2, NCMP)
        cmask = carve(NT, 4, 2, NCMP)
        cs = carve(NT, 4, 2, NCMP)
        cmx = carve(NT, 8)
        cden = carve(NT, 8)
        cz = carve(NT, 8)
        ccf = carve(NT, 8)
        pcT = carve(NT, P)
        blk = carve(8)
        csm = carve(4)
        gates = carve(NT, 8, 3)

        at[0] = 0
        hsT = carve(KD, PADDED)
        ysb = hsT.rearrange("p a b -> p (a b)")[:, 0:4 * D].rearrange("p (j d) -> p j d", j=4)
        ysT = carve(KD, PADDED)
        oneh = carve(NT, SLOTS)
        comb = carve(NT, SLOTS)
        combT = carve(4, S)
        ctmp = carve(NT, SLOTS)
        xt = [carve(KD, TILE) for _ in range(2)]
        en = [carve(KF, TILE) for _ in range(2)]
        uc = [carve(KF, TILE) for _ in range(2)]
        aT = [carve(KF, TILE) for _ in range(2)]
        lg = carve(NT, NG + NE)
        r_gm, r_i, r_wm, r_pg, r_ws, r_m1, r_m2, r_s, r_s1, r_s2 = (carve(NT) for _ in range(10))
        ge, g_eq, g_oh = (carve(NT, NG) for _ in range(3))
        we, e_eq, oh1, oh2 = (carve(NT, EG) for _ in range(4))
        mask, f1, f2, wtmp = (carve(NT, NE) for _ in range(4))
        cnt = carve(NE)
        incl = carve(NE)
        offs = carve(NE)
        tov = carve(NE)
        vin = carve(NE)
        vex = carve(NE)
        ov = [carve(8, NE) for _ in range(5)]
        ovr = [carve(8) for _ in range(2)]
        offs_i = sb("offsets", [P, NE], I32)
        ove_i = sb("overflow_expert", [P, 8], I32)
        ovs_i = sb("overflow_start", [P, 8], I32)
        ovn_i = sb("overflow_count", [P, 1], I32)

        bank = [ctx.enter_context(nc.psum_tensor(f"bank{i}", [P, 512], F32)) for i in range(8)]

        landed = [sem(f"unit_landed{i}") for i in range(RING)]
        cmp_landed, x_landed, consts_landed = sem("cmp_landed"), sem("x_landed"), sem("consts_landed")
        consts, tables = sem("consts_built"), sem("tables_built")
        pool_chain, dve_chain, act_chain = sem("pool_chain"), sem("dve_chain"), sem("act_chain")
        rstd_ready, xn_ready, x_ready = sem("rstd_ready"), sem("xn_ready"), sem("x_ready")
        ta_full, ta_free = sem("transposes_a_full"), sem("transposes_a_free")
        tb_full, tb_free = sem("transposes_b_full"), sem("transposes_b_free")
        pr_full, pr_act, pr_dve = sem("proj_full"), sem("proj_drained_act"), sem("proj_drained_dve")
        sq_ready, ms_ready, rq_ready = sem("squares_ready"), sem("head_ms_ready"), sem("head_rstd_ready")
        sc_full, sc_free, nm_ready = sem("scores_full"), sem("scores_masked"), sem("neg_max_ready")
        p_ready, pt_full, pt_ready = sem("p_ready"), sem("pT_full"), sem("pT_ready")
        ln_ready, suffix_ready, arg_ready = sem("ln_ready"), sem("suffix_ready"), sem("stick_arg_ready")
        o_full, o_ready = sem("o_full"), sem("o_ready")
        es_in, es_out = sem("sink_arg_ready"), sem("sink_exp_ready")
        cmp_full, cmp_dve, cmp_act = sem("cmp_psum_full"), sem("cmp_by_dve"), sem("cmp_by_act")
        gate_full, gate_exp, gate_ready = sem("gate_full"), sem("gate_exp_ready"), sem("gate_ready")
        wo_used = sem("out_proj_units_used")
        rt_full, rt_gs, rt_ge = sem("router_psum_full"), sem("group_arg_ready"), sem("group_exp_ready")
        rt_ws, rt_we, rt_mask = sem("expert_arg_ready"), sem("expert_exp_ready"), sem("choice_ready")
        oh_ready, comb_ready, offs_ready = sem("onehot_ready"), sem("comb_ready"), sem("offsets_ready")
        over_ready = sem("overflow_list_ready")
        ga_full, ga_act, ga_dve = sem("gather_full"), sem("gather_drained_act"), sem("gather_drained_dve")
        pad_ready, xt_ready = sem("pad_ready"), sem("expert_input_ready")
        gu_full, gu_act, a_ready = sem("gate_up_full"), sem("gate_up_act"), sem("hidden_ready")
        y_full, y_free = sem("down_full"), sem("down_drained")
        ov_landed = [sem(f"overflow_landed{l}") for l in range(2)]
        ov_x = [sem(f"overflow_input{l}") for l in range(2)]
        ov_gu = [sem(f"overflow_gate_up{l}") for l in range(2)]
        ov_act = [sem(f"overflow_act{l}") for l in range(2)]
        ov_a = [sem(f"overflow_hidden{l}") for l in range(2)]
        ov_y = [sem(f"overflow_down{l}") for l in range(2)]
        ov_done = [sem(f"overflow_stored{l}") for l in range(2)]
        yt_full, yt_act, yt_dve = sem("y_turned_full"), sem("y_drained_act"), sem("y_drained_dve")
        ac_full, stored = sem("combined_full"), sem("stored")

        ov_over = [sem(f"overflow_loads_over{l}") for l in range(2)]
        ov_chain = [sem(f"overflow_chain{l}") for l in range(2)]

        def cols(a, u):
            return a[:, :, u * UC:(u + 1) * UC]

        def by_head(a):
            return a.rearrange("p t (h d) -> p t h d", d=DH)

        def half_pairs(a, u):
            return a.rearrange("p t (a u d) -> p t a u d", a=4, u=2)[:, :, :, u, :]

        DST = ({0: (half_pairs(stage[0], 0), None), 1: (half_pairs(stage[0], 1), None),
                2: (by_head(stk[0]), vsm[0]), 3: cols(stage[1], 0), 4: cols(stage[1], 1),
                5: cols(stage[0], 0), 6: cols(stage[0], 1), 7: cols(vbig, 0), 8: cols(vbig, 1)},
               {0: (by_head(cols(stage[0], 0)), None), 1: (by_head(cols(stage[0], 1)), None),
                2: (by_head(cols(stage[1], 0)), None), 3: (by_head(cols(stage[1], 1)), None),
                4: cols(vbig, 0), 5: cols(vbig, 1),
                6: (half_pairs(stage[0], 0), None), 7: (half_pairs(stage[0], 1), None),
                8: None, 9: (by_head(stk[0]), vsm[0]), 10: (by_head(stk[1]), vsm[1])})
        TURNS = {"qa": (0, None, "dve", 2), "ka": (2, "b", "dve", 3),
                 "qb": (1, None, "act", 2), "kb": (0, None, "act", 4),
                 "qc": (0, None, "dve", 5), "kc": (1, None, "dve", 7),
                 "qd": (0, None, "dve", 9), "ks": (2, "a", "dve", 10), "kw": (3, "b", "dve", 11)}
        TDST = {"qa": (qT[0], qk_g[:, 0:1]), "ka": (kTp[0], qk_g[:, 1:2]), "qb": (qT[1], 0.125), "kb": (kT, None),
                "qc": (qT[0], qk_g[:, 2:3]), "kc": (kT, qk_g[:, 3:4]), "qd": (qT[1], qk_g[:, 4:5]),
                "ks": (kTp[0], qk_g[:, 6:7]), "kw": (kTp[1], qk_g[:, 7:8])}

        def tok(a, k):
            return a.rearrange("q (p k) -> q k p", k=KD)[:, k, :]

        def slot_of(n):
            return n % RING

        def landings(n):
            skipped = n > U_CMP and slot_of(n) == slot_of(U_CMP)
            return 16 * (n // RING + 1 - skipped)

        def released(n):
            if n < U_EV_OUT:
                return pr_full, n + 1
            if n < U_MOE0:
                return wo_used, n - U_EV_OUT + 1
            if n < U_OD_IN or n >= U_MOE1:
                l = int(n >= U_MOE1)
                e, c = divmod(n - U_MOE[l], PER_EXPERT)
                return (y_full if c == 2 else gu_full), l * NE + e + 1
            if n < U_CMP:
                return pr_full, EV_UNITS + n - U_OD_IN + 1
            if n == U_CMP:
                return cmp_full, CF_COMPRESSED
            return wo_used, OUT_UNITS + n - U_OD_OUT + 1

        def seconds(v):
            return v.rearrange("p (h q d) -> p h q d", h=4, q=NT)

        class Chain:
            def __init__(self, eng, s):
                self.eng, self.s, self.n, self.i, self.per = eng, s, 0, None, 0

            def __call__(self, ins):
                self.n += 1
                ins.then_inc(self.s, 1)
                self.eng.wait_ge(self.s, self.n if self.i is None else self.n + self.i * self.per)

            def loop(self, i, first, per):
                self.i, self.per, self.start = i, per, self.n
                self.n -= first * per

            def end(self, trips, first):
                assert self.n == self.start - first * self.per + self.per
                self.n, self.i = self.start + self.per * trips, None

        block = ctx.enter_context(nc.Block())

        @block.sync
        def _(sp):
            for t in range(NT):
                sp.dma_start(xs[:, t, :], x[0, t * P:(t + 1) * P, :]).then_inc(x_landed, 16)

            def load(n, src, shape):
                if n >= RING:
                    sp.wait_ge(*released(n - RING))
                dst = ring[:, slot_of(n), :].rearrange("p (a b) -> p a b", a=shape)
                sp.dma_start(dst, src).then_inc(landed[slot_of(n)], 16)

            def proj_units(u0, w, units):
                wv = w[0].rearrange("(p k) n -> p k n", k=KD)
                for u in range(units):
                    load(u0 + u, wv[:, :, u * UC:(u + 1) * UC], KD)

            def out_units(u0, w):
                for u in range(OUT_UNITS):
                    load(u0 + u, w[0, u * 2 * P:(u + 1) * 2 * P, :].rearrange("(k p) n -> p k n", p=P), 2)

            def expert(l, e, c):
                one = bass.ds(l * NE + e, 1)
                if c < 2:
                    w = (moe_w_gate, moe_w_up)[c].rearrange("l e (p k) n -> (l e) p k n", k=KD)
                else:
                    w = moe_w_down.rearrange("l e (k p) n -> (l e) p k n", p=P)
                return w[one].rearrange("o p k n -> p (o k) n")

            def expert_dst(c, s):
                return ring[:, s, :].rearrange("p (a b) -> p a b", a=KD if c < 2 else KF)

            def moe_units(l):
                u0 = U_MOE[l]
                for e in range(BODY):
                    for c in range(PER_EXPERT):
                        load(u0 + PER_EXPERT * e + c, expert(l, e, c), KD if c < 2 else KF)
                with sp.Fori(1, NE // BODY) as i:
                    for j in range(BODY):
                        for c in range(PER_EXPERT):
                            s = slot_of(u0 + PER_EXPERT * j + c)
                            sp.wait_ge(y_full if c == 2 else gu_full, l * NE + j - BODY + 1 + i * BODY)
                            sp.dma_start(expert_dst(c, s), expert(l, i * BODY + j, c)).then_inc(landed[s], 16)
                last = u0 + PER_EXPERT * (NE - 1)
                sp.wait_ge(over_ready, l + 1)
                n_over = sp.value_load(ovn_i[0:1, 0:1], min_val=0, max_val=MAXOVER)
                with sp.If(n_over):
                    sp.wait_ge(y_full, (l + 1) * NE)
                    with sp.Fori(0, n_over) as j:
                        e = sp.value_load(ove_i[0:1, bass.ds(j, 1)], min_val=0, max_val=NE - 1)
                        for c in range(PER_EXPERT):
                            sp.dma_start(expert_dst(c, slot_of(last + c)),
                                         expert(l, e, c)).then_inc(ov_landed[l], 16)
                        sp.wait_ge(ov_y[l], j + 1)
                        sp.sem_inc(ov_over[l], 1)

            proj_units(U_EV_IN, ev_w_in, EV_UNITS)
            out_units(U_EV_OUT, ev_w_out)
            moe_units(0)
            proj_units(U_OD_IN, od_w_in, OD_UNITS)
            sp.wait_ge(*released(U_CMP - RING))
            cw = od_cmp_w[0].rearrange("w (h l) d e -> h d w l e", h=2)
            for h in range(2):
                for w in range(2):
                    dst = ring[h * DH:(h + 1) * DH, slot_of(U_CMP), w * NCMP * DH:(w + 1) * NCMP * DH]
                    sp.dma_start(dst.rearrange("p (l e) -> p l e", l=NCMP), cw[h, :, w]).then_inc(cmp_landed, 16)
            out_units(U_OD_OUT, od_w_out)
            moe_units(1)
            for t in range(NT):
                sp.wait_ge(x_ready, 3 * NT + t + 1)
                sp.dma_start(out[0, t * P:(t + 1) * P, :], xs[:, t, :]).then_inc(stored, 16)
            sp.wait_ge(stored, 16 * NT)

        @block.gpsimd
        def _(pool):
            g = nc.gpsimd
            chain = Chain(pool, pool_chain)

            g.memset(eps_t[:], EPS).then_inc(consts, 1)
            g.memset(one_t[:], 1.0).then_inc(consts, 1)
            g.memset(ones[:], 1.0).then_inc(consts, 1)
            chain(g.memset(ident[:], 0.0))
            g.affine_select(out=ident[:], in_=ident[:], compare_op=ALU.not_equal, fill=1.0, base=0,
                            pattern=[[-1, P]], channel_multiplier=1).then_inc(consts, 1)
            chain(g.memset(before[:], 1.0))
            g.affine_select(out=before[:], in_=before[:], compare_op=ALU.is_gt, fill=0.0, base=0,
                            pattern=[[1, P]], channel_multiplier=-1).then_inc(consts, 1)

            pool.wait_ge(consts_landed, 16 * N_LOADS)
            for c in (0, 2, 4):
                g.tensor_scalar(qk_g[:, c:c + 1], qk_g[:, c:c + 1], 0.125, None, ALU.mult).then_inc(consts, 1)
            g.iota(iota_s[:], pattern=[[1, SLOTS]], base=0, channel_multiplier=0,
                   allow_small_or_imprecise_dtypes=True).then_inc(consts, 1)
            g.iota(iota8[:], pattern=[[0, NT], [1, EG]], base=0, channel_multiplier=0,
                   allow_small_or_imprecise_dtypes=True).then_inc(consts, 1)
            g.iota(iota_e[:], pattern=[[1, NE]], base=0, channel_multiplier=0,
                   allow_small_or_imprecise_dtypes=True).then_inc(consts, 1)

            def bias_table(windowed):
                chain(g.iota(btab[:, 7, 0:P], pattern=[[-1, P]], base=0, channel_multiplier=1,
                             allow_small_or_imprecise_dtypes=True))
                chain(g.iota(btab[:, 7, P:SC], pattern=[[-1, S]], base=P, channel_multiplier=1,
                             allow_small_or_imprecise_dtypes=True))
                for h in range(8):
                    chain(g.tensor_scalar(btab[:, h, :], btab[:, 7, :], -SLOPES[h], None, ALU.mult))
                for a, n, base in ((0, P, 0), (P, S, P)):
                    v = btab[:, :, a:a + n]
                    chain(g.affine_select(out=v, in_=v, compare_op=ALU.is_ge,
                                          fill=NEG, base=base, pattern=[[0, 8], [-1, n]], channel_multiplier=1))
                if windowed:
                    chain(g.affine_select(out=btab[:, :, P:SC], in_=btab[:, :, P:SC], compare_op=ALU.is_gt,
                                          fill=NEG, base=0, pattern=[[0, 8], [1, S]], channel_multiplier=-1))

            bias_table(True)
            chain(g.memset(smask, 0.0))
            chain(g.affine_select(out=smask[:, 0:P], in_=smask[:, 0:P], compare_op=ALU.is_gt, fill=NEG,
                                  base=0, pattern=[[-1, P]], channel_multiplier=1))
            chain(g.affine_select(out=smask[:, P:SC], in_=smask[:, P:SC], compare_op=ALU.is_gt, fill=NEG,
                                  base=P, pattern=[[-1, S]], channel_multiplier=1))
            chain(g.memset(sreset, 1.0))
            g.memset(sreset[:, P - 1:P], 0.0).then_inc(tables, 1)
            def stick_args():
                for n in range(8):
                    b = n % 2
                    pool.wait_ge(suffix_ready, n + 1)
                    g.tensor_tensor(la[b], s_sb[b], cu[b], ALU.subtract).then_inc(arg_ready, 1)

            def pads(l):
                pool.wait_ge(x_ready, 2 * l * NT + NT)
                g.memset(hsT[:, :, SLOTS:PADDED], 0.0).then_inc(pad_ready, 1)
                g.memset(ysT[:, :, SLOTS:PADDED], 0.0).then_inc(pad_ready, 1)

            def expert_inputs(l):
                def one(s, e, i):
                    k = l * NE + s - 1
                    if i is not None:
                        pool.wait_ge(gu_full, k + i * BODY)
                    elif k > 0:
                        pool.wait_ge(gu_full, k)
                    off = pool.value_load(offs_i[0:1, bass.ds(e, 1)], min_val=0, max_val=SLOTS)
                    g.tensor_copy(xt[s % 2], hsT[:, :, bass.ds(off, TILE)]).then_inc(xt_ready, 1)

                pool.wait_ge(offs_ready, l + 1)
                pool.wait_ge(ga_act, (l + 1) * KD // 2)
                pool.wait_ge(ga_dve, (l + 1) * KD // 2)
                pool.wait_ge(pad_ready, 2 * (l + 1))
                for s in range(BODY):
                    one(s, s, None)
                with pool.Fori(1, NE // BODY) as i:
                    for j in range(BODY):
                        one(j, i * BODY + j, i)
                pool.wait_ge(over_ready, l + 1)
                n_over = pool.value_load(ovn_i[0:1, 0:1], min_val=0, max_val=MAXOVER)
                with pool.If(n_over):
                    pool.wait_ge(gu_full, (l + 1) * NE)
                    with pool.Fori(0, n_over) as j:
                        start = pool.value_load(ovs_i[0:1, bass.ds(j, 1)], min_val=0, max_val=SLOTS)
                        g.tensor_copy(xt[0], hsT[:, :, bass.ds(start, TILE)]).then_inc(ov_x[l], 1)
                        pool.wait_ge(ov_gu[l], j + 1)

            def cmp_tables():
                chain(g.iota(ctab.rearrange("p t a b n -> p t (a b) n"),
                             pattern=[[P, NT], [0, 8], [-CSTEP, NCMP]], base=-(CLEN - 1),
                             channel_multiplier=1, allow_small_or_imprecise_dtypes=True))
                for pr in range(4):
                    for kv in range(2):
                        v = ctab[:, :, pr, kv, :]
                        chain(g.tensor_scalar(v, v, -SLOPES[kv * 4 + pr], None, ALU.mult))
                chain(g.memset(cmask, 1.0))
                for a, fill in ((ctab, NEG), (cmask, 0.0)):
                    for t in range(NT):
                        v = a[:, t].rearrange("p a b n -> p (a b) n")
                        chain(g.affine_select(out=v, in_=v, compare_op=ALU.is_ge, fill=fill,
                                              base=P * t - (CLEN - 1), pattern=[[0, 8], [-CSTEP, NCMP]],
                                              channel_multiplier=1))
                    chain(g.memset(a.rearrange("p t a b n -> p (t a b) n")[:, :, NCMP - 1:NCMP], fill))
                pool.wait_ge(consts, N_CONST)
                for a in range(4):
                    chain(g.tensor_copy(spread[0:32, a, :], ident[0:32, 0:32]))
                chain(g.memset(blk, 1.0))
                chain(g.affine_select(out=blk, in_=blk, compare_op=ALU.is_ge, fill=0.0, base=0,
                                      pattern=[[-NCMP, 8]], channel_multiplier=1))
                g.affine_select(out=blk, in_=blk, compare_op=ALU.is_ge, fill=0.0, base=NCMP - 1,
                                pattern=[[NCMP, 8]], channel_multiplier=-1).then_inc(tables, 1)

            stick_args()
            pads(0)
            expert_inputs(0)
            pool.wait_ge(x_ready, 2 * NT)
            bias_table(False)
            cmp_tables()
            pads(1)
            expert_inputs(1)

        @block.tensor
        def _(pe):
            T = nc.tensor
            turns = {"a": 0, "b": 0}
            units, drains = [0], []
            nd = {"act": 0, "dve": 0}
            job = {"s": 0, "t": 0, "v": 0}

            def turn(which, pieces):
                full, free, bk = (ta_full, ta_free, 2) if which == "a" else (tb_full, tb_free, 3)
                if turns[which]:
                    pe.wait_ge(free, turns[which])
                for c, v in pieces:
                    k, m = v.shape[0], 1
                    for e in v.shape[1:]:
                        m *= e
                    last = T.transpose(bank[bk][0:m, c:c + k], v, ident[0:k, 0:k])
                last.then_inc(full, 1)
                turns[which] += 1

            def turned():
                pe.wait_ge(ta_free, turns["a"])
                pe.wait_ge(tb_free, turns["b"])

            def norm_turn(n):
                if n == 0:
                    pe.wait_ge(consts, N_CONST_A)
                pe.wait_ge(xn_ready, NT * (n + 1))
                for b in range(4):
                    turn("ab"[b % 2], [(kk * S + t * P, tok(xn[:, t, :], 2 * b + kk))
                                       for kk in range(2) for t in range(NT)])
                turned()

            def project(n, who):
                if units[0] >= 2:
                    pe.wait_ge(*drains[units[0] - 2])
                pe.wait_ge(landed[slot_of(n)], landings(n))
                w = ring[:, slot_of(n), :].rearrange("p (k c) -> p k c", k=KD)
                for t in range(NT):
                    for k in range(KD):
                        last = T.matmul(bank[units[0] % 2][:, t * UC:(t + 1) * UC], hT[:, k, t * P:(t + 1) * P],
                                        w[:, k, :], start=(k == 0), stop=(k == KD - 1))
                last.then_inc(pr_full, 1)
                units[0] += 1
                nd[who] += 1
                drains.append((pr_act if who == "act" else pr_dve, nd[who]))

            def qk_of(kind, h):
                if kind in "BC":
                    r = slice(DH * (h % 2), DH * (h % 2) + DH)
                    return (qT[1] if kind == "B" else qT[0])[r, h // 2, :], kT[r, h // 2, :]
                r = slice(DH * (h // 4), DH * (h // 4) + DH)
                k = kTp[1] if kind == "W" else kTp[0]
                return (qT[0] if kind == "A" else qT[1])[r, h % 4, :], k[r, :]

            def v_of(kind, h, t):
                if kind in "BC":
                    return vbig[:, t, h * DH:(h + 1) * DH]
                return vsm[kind == "W"][:, t, (h // 4) * DH:(h // 4 + 1) * DH]

            def scores(kind, h):
                n = job["s"]
                if n >= 2:
                    pe.wait_ge(sc_free, n - 1)
                if n in V_THERE:
                    turned()
                q, k = qk_of(kind, h)
                b = bank[4 + n % 2]
                T.matmul(b[:, 0:P], q[:, 0:P], k[:, 0:P], start=True, stop=True)
                T.matmul(b[:, P:SC], q[:, P:S], k[:, 0:S], start=True, stop=True).then_inc(sc_full, 1)
                job["s"] += 1

            def turn_p():
                n = job["t"]
                pe.wait_ge(p_ready, PR[n])
                if n:
                    pe.wait_ge(pt_ready, n)
                for c in range(3):
                    last = T.transpose(bank[6][:, c * P:(c + 1) * P], p_sb[n % 3][:, c * P:(c + 1) * P], ident[:])
                last.then_inc(pt_full, 1)
                job["t"] += 1

            def values(kind, h):
                n = job["v"]
                pe.wait_ge(pt_ready, n + 1)
                if n % 4 == 0 and n:
                    pe.wait_ge(o_ready, n // 4)
                if n == len(JOBS[0]):
                    pe.wait_ge(gate_ready, 1)
                if n in V_THERE:
                    who, count = V_THERE[n]
                    pe.wait_ge(pr_dve if who == "dve" else pr_act, count)
                o = bank[7][:, (n % 4) * P:(n % 4 + 1) * P]
                pt = pT[n % 2]
                T.matmul(o[:, 0:DH], pt[:, 0:P], v_of(kind, h, 0), start=True, stop=True)
                T.matmul(o[:, DH:P], pt[:, P:2 * P], v_of(kind, h, 0), start=True, stop=False)
                T.matmul(o[:, DH:P], pt[:, 2 * P:3 * P], v_of(kind, h, 1), start=False, stop=True).then_inc(o_full, 1)
                job["v"] += 1

            def step(jobs, i):
                if i < len(jobs):
                    scores(*jobs[i])
                if 0 <= i - 2 < len(jobs):
                    turn_p()
                if 0 <= i - SKEW < len(jobs):
                    values(*jobs[i - SKEW])

            def pairs(src, ps):
                return [(i * S + t * P, src[:, t, pr * P:(pr + 1) * P]) for i, pr in enumerate(ps) for t in range(NT)]

            def turn_qk(what):
                src, which, who, count = TURNS[what]
                pe.wait_ge(pr_act if who == "act" else pr_dve, count)
                if src in (2, 3):
                    turn(which, pairs(stk[src - 2], [0]))
                else:
                    turn("a", pairs(stage[src], [0, 1]))
                    turn("b", pairs(stage[src], [2, 3]))

            def cmp_stage(k):
                w = ring[:, slot_of(U_CMP), :].rearrange("p (w l e) -> p w l e", w=2, l=NCMP)
                if k == "pos":
                    pe.wait_ge(consts_landed, 16 * N_LOADS)
                    turn("a", [(c * NCMP, pos_in[:, c, :]) for c in range(2)])
                elif k == "in":
                    pe.wait_ge(pr_act, nd["act"])
                    pe.wait_ge(pr_dve, nd["dve"])
                    for c in range(2):
                        for h in range(2):
                            for t in range(NT):
                                v = cin[:, t, 2 * c + h].rearrange("p a d -> p (a d)")
                                last = T.transpose(bank[c][:, h * S + t * P:h * S + (t + 1) * P],
                                                   v, ident[:])
                    last.then_inc(cmp_full, 1)
                elif k == "compress":
                    pe.wait_ge(cmp_landed, 4 * 16)
                    pe.wait_ge(cmp_dve, CD_T2)
                    tk, tv = (a.rearrange("p h (n l) -> p l (h n)", l=CSTEP) for a in t2)
                    for l in range(NCMP):
                        T.matmul(bank[0][0:32, 0:DH], tk[:, l], w[:, 0, l, :], start=(l == 0), stop=(l == NCMP - 1))
                    for l in range(NCMP):
                        last = T.matmul(bank[1][0:32, 0:DH], tv[:, l],
                                        w[:, 1, l, :], start=(l == 0), stop=(l == NCMP - 1))
                    last.then_inc(cmp_full, 1)
                elif k == "keys":
                    pe.wait_ge(cmp_dve, CD_KEYS)
                    turn("a", [(0, kc_b[0:32].rearrange("p a d -> p (a d)"))])
                    pe.wait_ge(cmp_act, 1)
                    T.matmul(bank[1][:, 0:DH], spread[0:32].rearrange("p a b -> p (a b)"), vc[0:32, :],
                             start=True, stop=True).then_inc(cmp_full, 1)
                elif k == "scores":
                    turned()
                    for t in range(NT):
                        for pr in range(4):
                            last = T.matmul(bank[0][:, t * P + pr * 32:t * P + (pr + 1) * 32],
                                            qT[1][:, pr, t * P:(t + 1) * P], kcT[:], start=True, stop=True)
                    last.then_inc(cmp_full, 1)
                elif k == "p":
                    pe.wait_ge(cmp_dve, CD_P)
                    turn("a", [(t * P, cs[:, t].rearrange("p a b n -> p (a b n)")) for t in range(NT)])
                elif k == "values":
                    turned()
                    for t in range(NT):
                        last = T.matmul(bank[t][:], pcT[:, t, :], v_blk.rearrange("p h e -> p (h e)"), start=True, stop=True)
                    last.then_inc(cmp_full, 1)

            def mixer(layer):
                norm_turn(2 * layer)
                if layer:
                    for t in range(NT):
                        for k in range(KD):
                            last = T.matmul(bank[7][:, t * 32:t * 32 + GATES], hT[:, k, t * P:(t + 1) * P], w_gd[:, k, :],
                                            start=(k == 0), stop=(k == KD - 1))
                    last.then_inc(gate_full, 1)
                for what, *arg in ORDER[layer]:
                    if what == "unit":
                        project((U_EV_IN, U_OD_IN)[layer] + arg[0], arg[1])
                    elif what == "turn":
                        turn_qk(arg[0])
                    elif what == "cmp":
                        cmp_stage(arg[0])
                    elif what == "steps":
                        for i in range(arg[0], arg[1]):
                            step(JOBS[layer], i)
                pe.wait_ge(o_ready, (4, 10)[layer])
                for b in range(4):
                    turn("ab"[b % 2], [(kk * S + t * P, o_sb[:, t, (2 * b + kk) * P:(2 * b + kk + 1) * P])
                                       for kk in range(2) for t in range(NT)])
                turned()
                for u in range(OUT_UNITS):
                    n = (U_EV_OUT, U_OD_OUT)[layer] + u
                    pe.wait_ge(landed[slot_of(n)], landings(n))
                    w = ring[:, slot_of(n), :].rearrange("p (k c) -> p k c", k=2)
                    for kk in range(2):
                        for t in range(NT):
                            for hf in range(2):
                                last = T.matmul(bank[4 + 2 * t + hf][:], oT[:, 2 * u + kk, t * P:(t + 1) * P],
                                                w[:, kk, hf * 512:(hf + 1) * 512],
                                                start=(u == 0 and kk == 0), stop=(u == OUT_UNITS - 1 and kk == 1))
                    last.then_inc(wo_used, 1)

            def moe(l):
                norm_turn(2 * l + 1)
                for t in range(NT):
                    for k in range(KD):
                        last = T.matmul(bank[0][:, t * 64:t * 64 + NG + NE], hT[:, k, t * P:(t + 1) * P], w_rt[:, l, k, :],
                                        start=(k == 0), stop=(k == KD - 1))
                last.then_inc(rt_full, 1)
                pe.wait_ge(rt_mask, l + 1)
                m0, m1, c = mask[:, 0, :], mask[:, 1, :], bank[1]
                T.matmul(c[:, 0:NE], before[:], m0, start=True, stop=True)
                T.matmul(c[:, NE:2 * NE], ones[:], m0, start=True, stop=False)
                T.matmul(c[:, NE:2 * NE], before[:], m1, start=False, stop=True)
                T.matmul(c[:, 2 * NE:3 * NE], ones[:], m0, start=True, stop=False)
                T.matmul(c[:, 2 * NE:3 * NE], ones[:], m1, start=False, stop=True).then_inc(rt_full, 1)
                pe.wait_ge(oh_ready, NT * (l + 1))
                for k in range(KD):
                    if k >= 4:
                        pe.wait_ge(ga_dve if k % 2 else ga_act, l * KD // 2 + (k - 4) // 2 + 1)
                    for t in range(NT):
                        last = T.matmul(bank[4 + k % 4][:], tok(xn[:, t, :], k), oneh[:, t, :],
                                        start=(t == 0), stop=(t == NT - 1))
                    last.then_inc(ga_full, 1)
                pe.wait_ge(comb_ready, l + 1)
                for b in range(2):
                    turn("ab"[b], [(jj * S + t * P, comb[:, t, (2 * b + jj) * P:(2 * b + jj + 1) * P])
                                   for jj in range(2) for t in range(NT)])
                pe.wait_ge(ga_act, (l + 1) * KD // 2)
                pe.wait_ge(ga_dve, (l + 1) * KD // 2)
                u0 = U_MOE[l]

                def at_step(s, i, k):
                    return l * NE + s + k + (0 if i is None else i * BODY)

                def products_gu(s, v, u):
                    for c in range(2):
                        if u is not None:
                            u(c)
                        w = ring[:, slot_of(u0 + PER_EXPERT * s + c), :].rearrange("p (k c) -> p k c", k=KD)
                        for m in range(KF):
                            for k in range(KD):
                                last = T.matmul(bank[s % 2][:, (c * KF + m) * TILE:(c * KF + m + 1) * TILE],
                                                w[:, k, m * P:(m + 1) * P], v[:, k, :],
                                                start=(k == 0), stop=(k == KD - 1))
                    return last

                def products_down(s, v):
                    w = ring[:, slot_of(u0 + PER_EXPERT * s + 2), :].rearrange("p (k c) -> p k c", k=KF)
                    for m in range(KD):
                        for k in range(KF):
                            last = T.matmul(bank[4 + s % 2][:, m * TILE:(m + 1) * TILE], w[:, k, m * P:(m + 1) * P],
                                            v[:, k, :], start=(k == 0), stop=(k == KF - 1))
                    return last

                def wait_unit(s, i, c):
                    n = u0 + PER_EXPERT * s + c
                    pe.wait_ge(landed[slot_of(n)], landings(n) + (0 if i is None else 16 * i))

                def gate_up(s, i):
                    pe.wait_ge(xt_ready, at_step(s, i, 1))
                    if i is not None or l * NE + s >= 2:
                        pe.wait_ge(a_ready, at_step(s, i, -1))
                    products_gu(s, xt[s % 2], lambda c: wait_unit(s, i, c)).then_inc(gu_full, 1)

                def down(s, i):
                    pe.wait_ge(a_ready, at_step(s, i, 1))
                    if i is not None or l * NE + s >= 2:
                        pe.wait_ge(y_free, at_step(s, i, -1))
                    wait_unit(s, i, 2)
                    products_down(s, aT[s % 2]).then_inc(y_full, 1)

                for s in range(BODY):
                    gate_up(s, None)
                    if s:
                        down(s - 1, None)
                with pe.Fori(1, NE // BODY) as i:
                    for j in range(BODY):
                        gate_up(j, i)
                        down(j - 1, i)
                down(BODY - 1, NE // BODY - 1)
                pe.wait_ge(a_ready, (l + 1) * NE)
                pe.wait_ge(y_free, (l + 1) * NE)
                pe.wait_ge(over_ready, l + 1)
                n_over = pe.value_load(ovn_i[0:1, 0:1], min_val=0, max_val=MAXOVER)
                with pe.If(n_over):
                    with pe.Fori(0, n_over) as j:
                        pe.wait_ge(ov_landed[l], 16 * PER_EXPERT * (j + 1))
                        pe.wait_ge(ov_x[l], j + 1)
                        products_gu(BODY - 1, xt[0], None).then_inc(ov_gu[l], 1)
                        pe.wait_ge(ov_a[l], j + 1)
                        products_down(BODY - 1, aT[0]).then_inc(ov_y[l], 1)
                        pe.wait_ge(ov_done[l], j + 1)

                def turn_y(j):
                    for hf in range(2):
                        if j >= 2:
                            pe.wait_ge(yt_dve if hf else yt_act, l * 4 + j - 1)
                        for m in range(4):
                            last = T.transpose(bank[2 * (j % 2) + hf][:, m * P:(m + 1) * P],
                                               ysT[:, 4 * hf + m, j * P:(j + 1) * P], ident[:])
                        last.then_inc(yt_full, 1)

                def combine(j):
                    pe.wait_ge(yt_act, l * 4 + j + 1)
                    pe.wait_ge(yt_dve, l * 4 + j + 1)
                    for t in range(NT):
                        for hf in range(2):
                            last = T.matmul(bank[4 + 2 * t + hf][:], combT[:, j, t * P:(t + 1) * P],
                                            ysb[:, j, hf * 512:(hf + 1) * 512], start=(j == 0), stop=(j == 3))
                    return last
                turned()
                turn_y(0)
                for j in range(4):
                    if j < 3:
                        turn_y(j + 1)
                    last = combine(j)
                last.then_inc(ac_full, 1)

            mixer(0)
            moe(0)
            mixer(1)
            moe(1)

        @block.scalar
        def _(act):
            A = nc.scalar
            chain = Chain(act, act_chain)
            n_a, unit, n_act, n_sq, job = [0], [0], [0], [0], [0]
            A.preload_act_table_set("natural_log_exp_and_others")

            def col(v):
                return v.rearrange("(p k) -> p k", k=KD)

            def up(v):
                return v.rearrange("a d -> d a")
            loads = [
                (g_col[:, 0, :], col(ev_norm[0])),
                (sink[:], ev_sink.broadcast_to([P, 8])),
                (g_col[:, 1, :], col(moe_norm[0])), (g_col[:, 2, :], col(od_norm[0])), (g_col[:, 3, :], col(moe_norm[1])),
                (w_gd[:], od_w_in[0, :, OD_UNITS * UC:].rearrange("(p k) n -> p k n", k=KD)),
            ]
            for l in range(2):
                loads += [(w_rt[:, l, :, 0:NG], moe_w_grp[l].rearrange("(p k) n -> p k n", k=KD)),
                          (w_rt[:, l, :, NG:], moe_w_exp[l].rearrange("(p k) n -> p k n", k=KD)),
                          (b_rt[:, l, 0:NG], moe_b_grp[l:l + 1].broadcast_to([P, NG])),
                          (b_rt[:, l, NG:], moe_b_exp[l:l + 1].broadcast_to([P, NE])),
                          (pos_in[:, l, :].rearrange("l (h d) -> l h d", h=2),
                           od_cmp_pos[0, l].rearrange("(h l) d -> l h d", h=2))]
            for half in range(2):
                r = slice(half * DH, half * DH + DH)
                loads += [(qk_g[r, 0:1], up(ev_q_norm)), (qk_g[r, 1:2], up(ev_k_norm)),
                          (qk_g[r, 2:3], up(od_c_q_norm)), (qk_g[r, 3:4], up(od_c_k_norm)),
                          (qk_g[r, 4:5], up(od_d_q_norm)), (qk_g[r, 5:8], up(od_d_k_norm[0]))]
            assert len(loads) == N_LOADS
            for dst, src in loads:
                act.dma_start(dst, src, allow_slow_non_contiguous=True).then_inc(consts_landed, 16)


            def rms(n):
                junk = ctmp if n % 2 else stage[0]
                for t in range(NT):
                    act.wait_ge(*((x_landed, 16 * NT) if n == 0 else (x_ready, NT * (n - 1) + t + 1)))
                    chain(A.activation(junk.rearrange("p a b -> p (a b)"), xs[:, t, :], ACT.Square, accum_out=ssq[:, t:t + 1]))
                if n == 0:
                    act.wait_ge(consts, N_CONST_A)
                chain(A.activation(lnr[:], ssq[:], ACT.Ln, bias=eps_t[:], scale=1.0 / D))
                A.activation(rstd[:], lnr[:], ACT.Exp, scale=-0.5).then_inc(rstd_ready, 1)

            def drain_a(dst, scale=None, cols=512, rows=P, split=1):
                n_a[0] += 1
                act.wait_ge(ta_full, n_a[0])
                w = cols // split
                for i in range(split):
                    src = bank[2][0:rows, i * w:(i + 1) * w]
                    s = scale[i] if isinstance(scale, list) else scale
                    d = dst[i] if split > 1 else dst
                    if s is None:
                        last = A.copy(d, src)
                    else:
                        last = A.mul(d, src, s)
                last.then_inc(ta_free, 1)

            def norm_drain(n):
                if n == 0:
                    act.wait_ge(consts, N_CONST)
                for b in (0, 2):
                    drain_a([hT[:, 2 * b + kk, :] for kk in range(2)],
                            [g_col[:, n, 2 * b + kk:2 * b + kk + 1] for kk in range(2)], split=2)

            def squares(normed):
                n_sq[0] += 1
                n = n_sq[0]
                if n > 1:
                    act.wait_ge(ms_ready, n - 1)
                w = normed * DH
                b = bank[unit[0] % 2][:].rearrange("p (t c) -> p t c", t=NT)
                A.activation(sq[:, :, 0:normed, :].rearrange("p t h d -> p t (h d)"), b[:, :, 0:w],
                             ACT.Square).then_inc(sq_ready, 1)
                act.wait_ge(ms_ready, n)
                chain(A.activation(lq[:, :, 0:normed], red[:, :, 0:normed], ACT.Ln, bias=eps_t[:], scale=1.0 / DH))
                A.activation(rq[:, :, 0:normed], lq[:, :, 0:normed], ACT.Exp, scale=-0.5).then_inc(rq_ready, 1)

            def step(jobs, i, first):
                if i < len(jobs) and jobs[i][0] == "B":
                    n, b = i - 8, i % 2
                    act.wait_ge(sc_free, first + i + 1)
                    if n >= 2:
                        act.wait_ge(suffix_ready, n - 1)
                    chain(A.activation(ea[b], s_sb[b], ACT.Abs))
                    chain(A.activation(ea[b], ea[b], ACT.Exp, scale=-1.0))
                    A.activation(ea[b], ea[b], ACT.Ln, bias=one_t[:]).then_inc(ln_ready, 1)
                elif i < len(jobs):
                    n = first + i
                    act.wait_ge(nm_ready, NMN[n])
                    if n >= 3:
                        act.wait_ge(pt_full, n - 2)
                    for q, (a, b) in enumerate(((0, P), (P, SC))):
                        A.activation(p_sb[n % 3][:, a:b], s_sb[n % 2][:, a:b], ACT.Exp, bias=nm[:, i, q:q + 1],
                                     accum_out=den[:, i, q:q + 1]).then_inc(p_ready, 1)
                if 0 <= i - 1 < len(jobs) and jobs[i - 1][0] == "B":
                    n = first + i - 1
                    act.wait_ge(arg_ready, i - 1 - 8 + 1)
                    act.wait_ge(pt_full, n - 2)
                    A.activation(p_sb[n % 3], la[n % 2], ACT.Exp).then_inc(p_ready, 1)
                if first == 0 and i in (4, 8):
                    act.wait_ge(es_in, i)
                    A.activation(es[:, i - 4:i, :], es[:, i - 4:i, :], ACT.Exp).then_inc(es_out, 1)

            def drain_cmp(k):
                if k == "pos":
                    drain_a(posT.rearrange("p w l -> p (w l)"), cols=2 * NCMP)
                elif k == "compress":
                    act.wait_ge(cmp_full, CF_COMPRESSED)
                    A.copy(vc[0:32, :], bank[1][0:32, 0:DH]).then_inc(cmp_act, 1)
                    chain(A.activation(kc_n[0:32, :], bank[0][0:32, 0:DH], ACT.Square, accum_out=csm[0:32, 0:1]))
                    chain(A.activation(csm[0:32, 1:2], csm[0:32, 0:1], ACT.Ln, bias=eps_t[0:32, :], scale=1.0 / DH))
                    A.activation(csm[0:32, 2:3], csm[0:32, 1:2], ACT.Exp, scale=-0.5).then_inc(cmp_act, 1)
                elif k == "keys":
                    drain_a(kcT[:], qk_g[:, 5:6], cols=32)
                elif k == "scores":
                    act.wait_ge(cmp_dve, CD_ARG)
                    A.activation(cs, cs, ACT.Exp).then_inc(cmp_act, 1)
                elif k == "p":
                    drain_a(pcT.rearrange("p t q -> p (t q)"), cols=NT * P)

            def mixer(layer):
                rms(2 * layer)
                norm_drain(2 * layer)
                if layer:
                    act.wait_ge(gate_full, 1)
                    v = bank[7][:, 0:64].rearrange("p (t c) -> p t c", t=NT)[:, :, 0:GATES]
                    A.activation(gates.rearrange("p t h c -> p t (h c)"), v, ACT.Exp, scale=-1.0).then_inc(gate_exp, 1)
                first = layer * len(JOBS[0])
                for what, *arg in ORDER[layer]:
                    if what == "unit":
                        act.wait_ge(pr_full, unit[0] + 1)
                        if arg[1] == "dve":
                            squares(arg[2])
                        else:
                            dst = DST[layer][arg[0]]
                            if arg[0] in (5, 6) and layer == 0:
                                act.wait_ge(ta_full, T_QA_A)
                                act.wait_ge(tb_full, T_QA_B)
                            v = bank[unit[0] % 2][:]
                            if dst is None:
                                v = v.rearrange("p (t h d) -> p t h d", t=NT, h=4)
                                A.copy(cin[:, :, :, 0, :], v)
                                A.copy(cin[:, :, :, 1, :], v).then_inc(pr_act, 1)
                            else:
                                A.copy(dst, v.rearrange("p (t c) -> p t c", t=NT)).then_inc(pr_act, 1)
                        unit[0] += 1
                    elif what == "turn":
                        src, which, who, count = TURNS[arg[0]]
                        dst, scale = TDST[arg[0]]
                        if src < 2:
                            drain_a(dst[:, 0:2, :].rearrange("p a b -> p (a b)"), scale)
                        elif which == "a":
                            drain_a(dst, scale, cols=S)
                    elif what == "cmp":
                        drain_cmp(arg[0])
                    elif what == "steps":
                        for i in range(arg[0], arg[1]):
                            step(JOBS[layer], i, first)
                for b in (0, 2):
                    drain_a(oT[:, 2 * b:2 * b + 2, :].rearrange("p a b -> p (a b)"))

            def moe(l):
                rms(2 * l + 1)
                norm_drain(2 * l + 1)
                act.wait_ge(rt_gs, l + 1)
                A.activation(ge, ge, ACT.Exp).then_inc(rt_ge, 1)
                act.wait_ge(rt_ws, l + 1)
                A.activation(we, we, ACT.Exp).then_inc(rt_we, 1)
                for k in range(0, KD, 2):
                    act.wait_ge(ga_full, l * KD + k + 1)
                    A.mul(hsT[:, k, 0:SLOTS], bank[4 + k % 4][:], g_col[:, 2 * l + 1, k:k + 1]).then_inc(ga_act, 1)
                drain_a(combT[:, 0:2, :].rearrange("p a b -> p (a b)"))
                act.wait_ge(offs_ready, l + 1)

                def hidden(s, bk, b, sm, waits):
                    for w in waits:
                        act.wait_ge(*w)
                    v = bank[bk][:, 0:4 * TILE].rearrange("p (c m x) -> p c m x", c=2, m=KF)
                    A.activation(en[b], v[:, 0], ACT.Exp, scale=-1.0).then_inc(sm, 1)
                    A.copy(uc[b], v[:, 1]).then_inc(sm, 1)

                def one_hidden(s, i):
                    k = l * NE + s + (0 if i is None else i * BODY)
                    waits = [(gu_full, k + 1)]
                    if i is not None or k >= 2:
                        waits.append((a_ready, k - 1))
                    hidden(s, s % 2, s % 2, gu_act, waits)

                def one_out(s, i, e):
                    off = act.value_load(offs_i[0:1, bass.ds(e, 1)], min_val=0, max_val=SLOTS)
                    act.wait_ge(y_full, l * NE + s + 1 + (0 if i is None else i * BODY))
                    if i is not None:
                        act.wait_ge(y_free, l * NE + s + i * BODY)
                    elif l * NE + s > 0:
                        act.wait_ge(y_free, l * NE + s)
                    A.copy(ysT[:, :, bass.ds(off, TILE)],
                           bank[4 + s % 2][:].rearrange("p (m x) -> p m x", m=KD)).then_inc(y_free, 1)

                for s in range(BODY):
                    one_hidden(s, None)
                    if s:
                        one_out(s - 1, None, s - 1)
                with act.Fori(1, NE // BODY) as i:
                    for j in range(BODY):
                        one_hidden(j, i)
                        one_out(j - 1, i, i * BODY + j - 1)
                one_out(BODY - 1, NE // BODY - 1, NE - 1)
                act.wait_ge(over_ready, l + 1)
                n_over = act.value_load(ovn_i[0:1, 0:1], min_val=0, max_val=MAXOVER)
                act.wait_ge(y_free, (l + 1) * NE)
                with act.If(n_over):
                    with act.Fori(0, n_over) as j:
                        hidden(0, (BODY - 1) % 2, 0, ov_act[l], [(ov_gu[l], j + 1), (a_ready, (l + 1) * NE)])
                        start = act.value_load(ovs_i[0:1, bass.ds(j, 1)], min_val=0, max_val=SLOTS)
                        act.wait_ge(ov_y[l], j + 1)
                        A.copy(ysT[:, :, bass.ds(start, TILE)],
                               bank[4 + (BODY - 1) % 2][:].rearrange("p (m x) -> p m x", m=KD)).then_inc(ov_done[l], 1)
                        act.wait_ge(ov_done[l], j + 1)
                for j in range(4):
                    act.wait_ge(yt_full, l * 8 + 2 * j + 1)
                    A.copy(ysb[:, j, 0:512], bank[2 * (j % 2)][:]).then_inc(yt_act, 1)

            mixer(0)
            moe(0)
            mixer(1)
            moe(1)

        @block.vector
        def _(dve):
            V = nc.vector
            chain = Chain(dve, dve_chain)
            n_b, unit, n_sq = [0], [0], [0]

            def normed(n):
                dve.wait_ge(rstd_ready, n + 1)
                for t in range(NT):
                    V.tensor_scalar(xn[:, t, :], xs[:, t, :], rstd[:, t:t + 1], None, ALU.mult).then_inc(xn_ready, 1)

            def drain_b(dst, scale=None, cols=512, split=1):
                n_b[0] += 1
                dve.wait_ge(tb_full, n_b[0])
                w = cols // split
                for i in range(split):
                    src = bank[3][:, i * w:(i + 1) * w]
                    s = scale[i] if isinstance(scale, list) else scale
                    d = dst[i] if split > 1 else dst
                    if s is None:
                        last = V.tensor_copy(d, src)
                    else:
                        last = V.tensor_scalar(d, src, s, None, ALU.mult)
                last.then_inc(tb_free, 1)

            def norm_drain(n):
                for b in (1, 3):
                    drain_b([hT[:, 2 * b + kk, :] for kk in range(2)],
                            [g_col[:, n, 2 * b + kk:2 * b + kk + 1] for kk in range(2)], split=2)

            def normed_unit(layer, u, heads):
                n_sq[0] += 1
                n = n_sq[0]
                dve.wait_ge(sq_ready, n)
                V.tensor_reduce(red[:, :, 0:heads], sq[:, :, 0:heads, :], AX, ALU.add).then_inc(ms_ready, 1)
                b = bank[unit[0] % 2][:].rearrange("p (t h d) -> p t h d", t=NT, h=4)
                dst, rest = DST[layer][u]
                if layer == 1 and u in (6, 7):
                    dve.wait_ge(ta_full, T_QC_A)
                    dve.wait_ge(tb_full, T_QC_B)
                if heads < 4:
                    V.tensor_copy(rest, bank[unit[0] % 2][:].rearrange("p (t c) -> p t c", t=NT)[:, :, heads * DH:])
                dve.wait_ge(rq_ready, n)
                V.tensor_tensor(dst, b[:, :, 0:heads, :], rq[:, :, 0:heads].unsqueeze(3).broadcast_to([P, NT, heads, DH]),
                                ALU.mult).then_inc(pr_dve, 1)

            def step(jobs, i, layer):
                first = layer * len(JOBS[0])
                if i < len(jobs):
                    kind, h = jobs[i]
                    n = first + i
                    dve.wait_ge(sc_full, n + 1)
                    if n >= 2:
                        dve.wait_ge(p_ready, PR[n - 2])
                    b = bank[4 + n % 2]
                    if kind == "B":
                        V.tensor_tensor(s_sb[n % 2], b[:, 0:SC], smask, ALU.add).then_inc(sc_free, 1)
                    else:
                        V.tensor_tensor_reduce(s_sb[n % 2][:, 0:P], b[:, 0:P], btab[:, h, 0:P], 1.0, 3 * NEG,
                                               ALU.add, ALU.max, mx[:, i, 0:1])
                        V.tensor_tensor_reduce(s_sb[n % 2][:, P:SC], b[:, P:SC], btab[:, h, P:SC], 1.0, 3 * NEG,
                                               ALU.add, ALU.max, mx[:, i, 1:2]).then_inc(sc_free, 1)
                        dve.wait_ge(sc_free, n + 1)
                        if kind == "A":
                            V.tensor_scalar(nm[:, i, :], mx[:, i, :], sink[:, h:h + 1], -1.0,
                                            ALU.max, ALU.mult).then_inc(nm_ready, 1)
                            dve.wait_ge(nm_ready, NMN[n])
                            V.tensor_scalar(es[:, h, :], nm[:, i, :], sink[:, h:h + 1], None, ALU.add).then_inc(es_in, 1)
                        else:
                            V.tensor_scalar(nm[:, i, :], mx[:, i, :], -1.0, None, ALU.mult).then_inc(nm_ready, 1)
                if 0 <= i - 1 < len(jobs) and jobs[i - 1][0] == "B":
                    m, b = i - 1 - 8, (i - 1) % 2
                    dve.wait_ge(ln_ready, m + 1)
                    chain(V.scalar_tensor_tensor(out=la[b], in0=s_sb[b], scalar=0.0, in1=ea[b], op0=ALU.max, op1=ALU.add))
                    V.tensor_tensor_scan(cu[b][:, ::-1], sreset[:, ::-1], la[b][:, ::-1], 0.0,
                                         ALU.mult, ALU.add).then_inc(suffix_ready, 1)
                if 0 <= i - 2 < len(jobs):
                    n = first + i - 2
                    dve.wait_ge(pt_full, n + 1)
                    if n >= 2:
                        dve.wait_ge(o_full, n - 1)
                    V.tensor_copy(pT[n % 2], bank[6][:, 0:SC]).then_inc(pt_ready, 1)
                if 0 <= i - SKEW < len(jobs) and (i - SKEW) % 4 == 3:
                    heads_out(jobs, i - SKEW - 3, layer)

            def heads_out(jobs, i, layer):
                n = layer * len(JOBS[0]) + i
                kind, h = jobs[i]
                c0 = (512 if kind in "BLW" else 0) + h * DH
                dst = o_sb[:, :, c0:c0 + 4 * DH].rearrange("p t (h d) -> p h t d", h=4)
                v = bank[7][:].rearrange("p (h t d) -> p h t d", h=4, t=NT)
                if kind == "B":
                    dve.wait_ge(o_full, n + 4)
                    V.tensor_copy(dst, v).then_inc(o_ready, 1)
                    return
                dve.wait_ge(p_ready, PR[n + 3])
                d, c = den[:, i:i + 4, :], cf[:, 0:4, :]
                if kind == "A":
                    dve.wait_ge(es_out, h // 4 + 1)
                    chain(V.tensor_tensor(d, d, es[:, h:h + 4, :], ALU.add))
                chain(V.reciprocal(c, d))
                if kind in "LW":
                    gt = gates.rearrange("p t h c -> p h t c")[:, h:h + 4, :, 1 if kind == "L" else 2]
                    chain(V.tensor_tensor(c, c, gt, ALU.mult))
                dve.wait_ge(o_full, n + 4)
                c = c.unsqueeze(3).broadcast_to([P, 4, NT, DH])
                if kind in "LW":
                    o4 = otmp.rearrange("p t (h d) -> p h t d", h=4)
                    chain(V.tensor_tensor(o4, v, c, ALU.mult))
                    full = o_sb[:, :, c0:c0 + 4 * DH]
                    V.tensor_tensor(full, full, otmp, ALU.add).then_inc(o_ready, 1)
                else:
                    V.tensor_tensor(dst, v, c, ALU.mult).then_inc(o_ready, 1)

            def cmp_stage(k):
                if k == "in":
                    dve.wait_ge(cmp_full, 1)
                    dve.wait_ge(ta_free, T_POS)
                    for c in range(2):
                        lo = bank[c][0:DH, :].rearrange("p (m l) -> p m l", l=CSTEP)
                        V.tensor_tensor(t2[c][0:DH].rearrange("p h (n l) -> p (h n) l", l=CSTEP), lo,
                                        posT[0:DH, c, :].unsqueeze(1).broadcast_to([DH, 32, CSTEP]), ALU.add)
                        hi = bank[c][DH:P, :].rearrange("p (h n l) -> p h n l", h=2, l=CSTEP)[:, :, 1:, :]
                        dst = t2[c][DH:P].rearrange("p h (n l) -> p h n l", l=CSTEP)
                        V.tensor_tensor(dst[:, :, 0:NCMP - 1, :], hi,
                                        posT[DH:P, c, :].unsqueeze(1).unsqueeze(1).broadcast_to([DH, 2, NCMP - 1, CSTEP]),
                                        ALU.add)
                        last = V.memset(dst[:, :, NCMP - 1, :], 0.0)
                    last.then_inc(cmp_dve, 1)
                elif k == "compress":
                    dve.wait_ge(cmp_act, 2)
                    dve.wait_ge(tables, 2)
                    chain(V.tensor_scalar(kc_n[0:32, :], bank[0][0:32, 0:DH], csm[0:32, 2:3], None, ALU.mult))
                    V.tensor_tensor(kc_b[0:32], kc_n[0:32].unsqueeze(1).broadcast_to([32, 2, DH]),
                                    blk[0:32, 0:2].unsqueeze(2).broadcast_to([32, 2, DH]), ALU.mult).then_inc(cmp_dve, 1)
                elif k == "keys":
                    dve.wait_ge(cmp_full, 3)
                    V.tensor_tensor(v_blk, bank[1][:, 0:DH].unsqueeze(1).broadcast_to([P, 8, DH]),
                                    blk.unsqueeze(2).broadcast_to([P, 8, DH]), ALU.mult).then_inc(cmp_dve, 1)
                elif k == "scores":
                    dve.wait_ge(cmp_full, 4)
                    c3 = cs.rearrange("p t a b n -> p (t a b) n")
                    bc = [P, NT * 8, NCMP]
                    flat = [v.rearrange("p t h -> p (t h)") for v in (cmx, cden, cz, ccf)]
                    chain(V.tensor_tensor(cs.rearrange("p t a b n -> p (t a b n)"), bank[0][:, 0:NT * P],
                                          ctab.rearrange("p t a b n -> p (t a b n)"), ALU.add))
                    chain(V.tensor_reduce(flat[0], c3, AX, ALU.max))
                    V.tensor_tensor(c3, c3, flat[0].unsqueeze(2).broadcast_to(bc), ALU.subtract).then_inc(cmp_dve, 1)
                    dve.wait_ge(cmp_act, 3)
                    V.tensor_tensor(c3, c3, cmask.rearrange("p t a b n -> p (t a b) n"), ALU.mult).then_inc(cmp_dve, 1)
                    dve.wait_ge(cmp_dve, CD_P)
                    chain(V.tensor_reduce(flat[1], c3, AX, ALU.add))
                    chain(V.tensor_scalar(flat[2], flat[1], 0.0, None, ALU.is_equal))
                    chain(V.tensor_tensor(flat[1], flat[1], flat[2], ALU.add))
                    chain(V.reciprocal(flat[3], flat[1]))
                    gt = gates[:, :, :, 0].rearrange("p t (b a) -> p t a b", b=2)
                    v = ccf.rearrange("p t (a b) -> p t a b", a=4)
                    chain(V.tensor_tensor(v, v, gt, ALU.mult))
                elif k == "values":
                    dve.wait_ge(cmp_full, 5)
                    for t in range(NT):
                        dst = o_sb[:, t, 512:].rearrange("p (b a e) -> p a b e", b=2, a=4)
                        last = V.tensor_tensor(dst, bank[t][:].rearrange("p (a b e) -> p a b e", a=4, b=2),
                                               ccf[:, t, :].rearrange("p (a b) -> p a b", a=4).unsqueeze(3)
                                               .broadcast_to([P, 4, 2, DH]), ALU.mult)
                    chain(last)

            def add_out(event):
                for t in range(NT):
                    for hf in range(2):
                        v = xs[:, t, hf * 512:(hf + 1) * 512]
                        last = V.tensor_tensor(v, v, bank[4 + 2 * t + hf][:], ALU.add)
                    last.then_inc(x_ready, 1)

            def mixer(layer):
                normed(2 * layer)
                if layer == 0:
                    dve.wait_ge(consts_landed, 16 * N_LOADS)
                    dve.wait_ge(consts, N_CONST)
                norm_drain(2 * layer)
                if layer:
                    dve.wait_ge(gate_exp, 1)
                    v = gates.rearrange("p t h c -> p (t h c)")
                    chain(V.tensor_scalar(v, v, 1.0, None, ALU.add))
                    V.reciprocal(v, v).then_inc(gate_ready, 1)
                waited = False
                for what, *arg in ORDER[layer]:
                    if what == "unit":
                        if arg[1] == "dve":
                            normed_unit(layer, arg[0], arg[2])
                        unit[0] += 1
                    elif what == "turn":
                        src, which, who, count = TURNS[arg[0]]
                        dst, scale = TDST[arg[0]]
                        if src < 2:
                            drain_b(dst[:, 2:4, :].rearrange("p a b -> p (a b)"), scale)
                        elif which == "b":
                            drain_b(dst, scale, cols=S)
                    elif what == "cmp":
                        cmp_stage(arg[0])
                    elif what == "steps":
                        if not waited:
                            dve.wait_ge(tables, layer + 1)
                            waited = True
                        for i in range(arg[0], arg[1]):
                            step(JOBS[layer], i, layer)
                for b in (1, 3):
                    drain_b(oT[:, 2 * b:2 * b + 2, :].rearrange("p a b -> p (a b)"))
                dve.wait_ge(wo_used, OUT_UNITS * (layer + 1))
                add_out(2 * layer)

            def first_max(p, width, mxv, eq, idx, oh):
                bc = [P, NT, width]
                iota = iota8[:, :, 0:width]
                chain(V.tensor_reduce(mxv, p, AX, ALU.max))
                chain(V.tensor_tensor(eq, p, mxv.unsqueeze(2).broadcast_to(bc), ALU.is_equal))
                chain(V.scalar_tensor_tensor(out=eq, in0=eq, scalar=-100.0, in1=iota, op0=ALU.mult, op1=ALU.add))
                chain(V.tensor_reduce(idx, eq, AX, ALU.min))
                chain(V.tensor_scalar(idx, idx, 100.0, None, ALU.add))
                chain(V.tensor_tensor(oh, iota, idx.unsqueeze(2).broadcast_to(bc), ALU.is_equal))

            def route(l):
                n36 = NG + NE
                dve.wait_ge(rt_full, 2 * l + 1)
                v = bank[0][:, 0:NT * 64].rearrange("p (t c) -> p t c", t=NT)[:, :, 0:n36]
                chain(V.tensor_tensor(lg, v, b_rt[:, l, :].unsqueeze(1).broadcast_to([P, NT, n36]), ALU.add))
                gl = lg[:, :, 0:NG]
                chain(V.tensor_reduce(r_gm, gl, AX, ALU.max))
                V.tensor_tensor(ge, gl, r_gm.unsqueeze(2).broadcast_to([P, NT, NG]), ALU.subtract).then_inc(rt_gs, 1)
                dve.wait_ge(rt_gs, l + 1)
                first_max(gl, NG, r_gm, g_eq, r_i, g_oh)
                el = lg[:, :, NG:].rearrange("p t (g e) -> p t g e", g=NG)
                w4 = wtmp.rearrange("p t (g e) -> p t g e", g=NG)
                goh = g_oh.unsqueeze(3).broadcast_to([P, NT, NG, EG])
                chain(V.tensor_tensor(w4, el, goh, ALU.mult))
                chain(V.tensor_reduce(we, w4.rearrange("p t g e -> p t e g"), AX, ALU.add))
                chain(V.tensor_reduce(r_wm, we, AX, ALU.max))
                V.tensor_tensor(we, we, r_wm.unsqueeze(2).broadcast_to([P, NT, EG]), ALU.subtract).then_inc(rt_ws, 1)
                dve.wait_ge(rt_ge, l + 1)
                chain(V.tensor_reduce(r_pg, ge, AX, ALU.add))
                chain(V.reciprocal(r_pg, r_pg))
                dve.wait_ge(rt_we, l + 1)
                chain(V.tensor_reduce(r_ws, we, AX, ALU.add))
                chain(V.reciprocal(r_ws, r_ws))
                bc8 = [P, NT, EG]
                chain(V.tensor_tensor(we, we, r_ws.unsqueeze(2).broadcast_to(bc8), ALU.mult))
                first_max(we, EG, r_m1, e_eq, r_i, oh1)
                chain(V.scalar_tensor_tensor(out=we, in0=oh1, scalar=-2.0, in1=we, op0=ALU.mult, op1=ALU.add))
                first_max(we, EG, r_m2, e_eq, r_i, oh2)
                for oh, f in ((oh1, f1), (oh2, f2)):
                    chain(V.tensor_tensor(f.rearrange("p t (g e) -> p t g e", g=NG), goh,
                                          oh.unsqueeze(2).broadcast_to([P, NT, NG, EG]), ALU.mult))
                V.tensor_tensor(mask, f1, f2, ALU.add).then_inc(rt_mask, 1)
                chain(V.tensor_tensor(r_s, r_m1, r_m2, ALU.add))
                chain(V.reciprocal(r_s, r_s))
                chain(V.tensor_tensor(r_s, r_s, r_pg, ALU.mult))
                chain(V.tensor_tensor(r_m1, r_m1, r_s, ALU.mult))
                chain(V.tensor_tensor(r_m2, r_m2, r_s, ALU.mult))
                dve.wait_ge(rt_full, 2 * l + 2)
                chain(V.tensor_copy(cnt, bank[1][:, 2 * NE:3 * NE]))
                chain(V.tensor_tensor_scan(incl, ones[:, 0:NE], cnt, 0.0, ALU.mult, ALU.add))
                chain(V.tensor_tensor(offs, incl, cnt, ALU.subtract))
                V.tensor_copy(offs_i[:], offs).then_inc(offs_ready, 1)
                rk = wtmp
                chain(V.tensor_tensor(rk, bank[1][:, 0:2 * NE].rearrange("p (t e) -> p t e", t=NT),
                                      offs.unsqueeze(1).broadcast_to([P, NT, NE]), ALU.add))
                for f, s in ((f1, r_s1), (f2, r_s2)):
                    chain(V.tensor_tensor(f, f, rk, ALU.mult))
                    chain(V.tensor_reduce(s, f, AX, ALU.add))
                for t in range(NT):
                    chain(V.tensor_scalar(ctmp[:, t, :], iota_s[:], r_s2[:, t:t + 1], None, ALU.is_equal))
                    V.scalar_tensor_tensor(out=oneh[:, t, :], in0=iota_s[:], scalar=r_s1[:, t:t + 1], in1=ctmp[:, t, :],
                                           op0=ALU.is_equal, op1=ALU.add).then_inc(oh_ready, 1)
                for t in range(NT):
                    chain(V.tensor_scalar(ctmp[:, t, :], iota_s[:], r_s2[:, t:t + 1], r_m2[:, t:t + 1],
                                          ALU.is_equal, ALU.mult))
                    chain(V.tensor_scalar(comb[:, t, :], iota_s[:], r_s1[:, t:t + 1], r_m1[:, t:t + 1],
                                          ALU.is_equal, ALU.mult))
                for t in range(NT):
                    last = V.tensor_tensor(comb[:, t, :], comb[:, t, :], ctmp[:, t, :], ALU.add)
                last.then_inc(comb_ready, 1)

            def overflow_list():
                chain(V.tensor_scalar(tov, cnt, float(TILE), None, ALU.is_gt))
                for k in range(2, S // TILE):
                    chain(V.scalar_tensor_tensor(out=tov, in0=cnt, scalar=float(k * TILE), in1=tov,
                                                 op0=ALU.is_gt, op1=ALU.add))
                chain(V.tensor_tensor_scan(vin, ones[:, 0:NE], tov, 0.0, ALU.mult, ALU.add))
                chain(V.tensor_tensor(vex, vin, tov, ALU.subtract))
                bc = [P, 8, NE]
                j8 = iota8[:, 0, :].unsqueeze(2).broadcast_to(bc)

                def row(v):
                    return v.unsqueeze(1).broadcast_to(bc)
                chain(V.tensor_tensor(ov[0], j8, row(vex), ALU.subtract))
                chain(V.tensor_scalar(ov[1], ov[0], 0.0, None, ALU.is_ge))
                chain(V.tensor_tensor(ov[2], j8, row(vin), ALU.is_lt))
                chain(V.tensor_tensor(ov[1], ov[1], ov[2], ALU.mult))
                chain(V.tensor_tensor(ov[2], ov[1], row(iota_e[:]), ALU.mult))
                chain(V.tensor_reduce(ovr[0], ov[2], AX, ALU.add))
                chain(V.tensor_scalar(ov[0], ov[0], float(TILE), float(TILE), ALU.mult, ALU.add))
                chain(V.tensor_tensor(ov[0], ov[0], row(offs), ALU.add))
                chain(V.tensor_scalar(vex, incl, -float(TILE), None, ALU.add))
                chain(V.tensor_tensor(ov[0], ov[0], row(vex), ALU.min))
                chain(V.tensor_tensor(ov[0], ov[0], ov[1], ALU.mult))
                chain(V.tensor_reduce(ovr[1], ov[0], AX, ALU.add))
                chain(V.tensor_copy(ove_i[:], ovr[0]))
                chain(V.tensor_copy(ovs_i[:], ovr[1]))
                V.tensor_copy(ovn_i[:], vin[:, NE - 1:NE]).then_inc(over_ready, 1)

            def moe(l):
                normed(2 * l + 1)
                norm_drain(2 * l + 1)
                route(l)
                for k in range(1, KD, 2):
                    dve.wait_ge(ga_full, l * KD + k + 1)
                    V.tensor_scalar(hsT[:, k, 0:SLOTS], bank[4 + k % 4][:], g_col[:, 2 * l + 1, k:k + 1], None,
                                    ALU.mult).then_inc(ga_dve, 1)
                drain_b(combT[:, 2:4, :].rearrange("p a b -> p (a b)"))
                overflow_list()

                def hidden(bk, b, out_sem, *waits):
                    for w in waits:
                        dve.wait_ge(*w)
                    gate = bank[bk][:, 0:2 * TILE].rearrange("p (m x) -> p m x", m=KF)
                    chain(V.tensor_scalar(en[b], en[b], 1.0, None, ALU.add))
                    chain(V.reciprocal(en[b], en[b]))
                    chain(V.tensor_tensor(en[b], en[b], gate, ALU.mult))
                    V.tensor_tensor(aT[b], en[b], uc[b], ALU.mult).then_inc(out_sem, 1)

                def one(s, i):
                    k = l * NE + s
                    m = 0 if i is None else i * BODY
                    waits = [(gu_act, 2 * (k + 1) + 2 * m)]
                    if i is not None or k >= 2:
                        waits.append((y_full, k - 1 + m))
                    hidden(s % 2, s % 2, a_ready, *waits)

                for s in range(BODY):
                    one(s, None)
                with dve.Fori(1, NE // BODY) as i:
                    chain.loop(i, 1, 3 * BODY)
                    for j in range(BODY):
                        one(j, i)
                chain.end(NE // BODY - 1, 1)
                n_over = dve.value_load(ovn_i[0:1, 0:1], min_val=0, max_val=MAXOVER)
                with dve.If(n_over):
                    dve.wait_ge(y_full, (l + 1) * NE)
                    with dve.Fori(0, n_over) as j:
                        dve.wait_ge(ov_act[l], 2 * (j + 1))
                        gate = bank[(BODY - 1) % 2][:, 0:2 * TILE].rearrange("p (m x) -> p m x", m=KF)
                        c0 = 3 * j
                        V.tensor_scalar(en[0], en[0], 1.0, None, ALU.add).then_inc(ov_chain[l], 1)
                        dve.wait_ge(ov_chain[l], c0 + 1)
                        V.reciprocal(en[0], en[0]).then_inc(ov_chain[l], 1)
                        dve.wait_ge(ov_chain[l], c0 + 2)
                        V.tensor_tensor(en[0], en[0], gate, ALU.mult).then_inc(ov_chain[l], 1)
                        dve.wait_ge(ov_chain[l], c0 + 3)
                        V.tensor_tensor(aT[0], en[0], uc[0], ALU.mult).then_inc(ov_a[l], 1)
                for j in range(4):
                    dve.wait_ge(yt_full, l * 8 + 2 * j + 2)
                    V.tensor_copy(ysb[:, j, 512:], bank[2 * (j % 2) + 1][:]).then_inc(yt_dve, 1)
                dve.wait_ge(ac_full, l + 1)
                add_out(2 * l + 1)

            mixer(0)
            moe(0)
            mixer(1)
            moe(1)


_INS = ['x', 'ev_norm', 'ev_w_in', 'ev_q_norm', 'ev_k_norm', 'ev_sink', 'ev_w_out',
        'od_norm', 'od_w_in', 'od_c_q_norm', 'od_c_k_norm', 'od_d_q_norm', 'od_d_k_norm',
        'od_cmp_pos', 'od_cmp_w', 'od_w_out',
        'moe_norm', 'moe_w_grp', 'moe_b_grp', 'moe_w_exp', 'moe_b_exp', 'moe_w_gate', 'moe_w_up', 'moe_w_down']
_OUTS = [((1, S, D), 'float32')]


def kernel(**inputs):
    import numpy as _np
    import concourse.bacc as _bacc
    from concourse import mybir as _mybir
    from concourse.bass_utils import run_bass_kernel_spmd as _run

    nc = _bacc.Bacc("TRN2", target_bir_lowering=False, num_devices=1)
    arrays, args = {}, []
    for name in _INS:
        a = _np.ascontiguousarray(inputs[name])
        arrays[f"in_{name}_dram"] = a
        args.append(nc.dram_tensor(f"in_{name}_dram", a.shape, _mybir.dt.from_np(a.dtype), kind="ExternalInput").ap())
    for i, (shape, dtype) in enumerate(_OUTS):
        dt = _mybir.dt.from_np(_np.dtype(dtype))
        args.append(nc.dram_tensor(f"out_{i}_dram", shape, dt, kind="ExternalOutput").ap())
    program(nc, *args)
    r = _run(nc, [arrays], core_ids=[0])
    got = tuple(r.results[0][f"out_{i}_dram"] for i in range(len(_OUTS)))
    return got[0]
```

```python
from contextlib import ExitStack

import concourse.bass as bass
from concourse import mybir

P = 128
S = 256
NT = S // P
D = 1024
KD = D // P
DH = 64
EV_IN = 2304
OD_IN = 2840
NG, EG, NE, FF = 4, 8, 32, 256
KF = FF // P
UNIT = 2048
UC = UNIT // KD
RING = 12
PER_EXPERT = 3
GROUPS = 4
BATCH = GROUPS * PER_EXPERT
EV_UNITS = EV_IN // UC
OD_UNITS = OD_IN // UC
OUT_UNITS = D * D // (P * UNIT)
GATES = OD_IN - OD_UNITS * UC
TILE = P // GROUPS
OWN = NE // GROUPS
MAXOVER = 16
MAXB = OWN + MAXOVER // GROUPS
EPS = 1e-6
NEG = -1e30
SC = P + S
NCMP = 16
WIN, CSTEP, CLEN = 128, 16, 32

F32 = mybir.dt.float32
I32 = mybir.dt.int32
ALU = mybir.AluOpType
ACT = mybir.ActivationFunctionType
AX = mybir.AxisListType.X

U_EV_IN = 0
U_EV_OUT = U_EV_IN + EV_UNITS
U_MOE0 = U_EV_OUT + OUT_UNITS + 1
U_OD_IN = U_MOE0 + PER_EXPERT * NE
U_CMP = U_OD_IN + OD_UNITS
U_OD_OUT = U_CMP + 1
U_MOE1 = U_OD_OUT + OUT_UNITS
U_END = U_MOE1 + PER_EXPERT * NE
U_MOE = (U_MOE0, U_MOE1)

SLOPES = [2.0 ** -(h + 1) for h in range(8)]


def even_jobs():
    return [("A", h) for h in range(8)] + [("B", h) for h in range(8)]


def odd_jobs():
    return [("C", h) for h in range(8)] + [("L", h) for h in range(8)] + [("W", h) for h in range(8)]


JOBS = (even_jobs(), odd_jobs())
ORDER = (
    [("unit", 0, "dve", 4), ("unit", 1, "dve", 4), ("unit", 2, "dve", 2), ("turn", "qa"),
     ("unit", 3, "act"), ("turn", "ka"), ("steps", 0, 2), ("unit", 4, "act"), ("steps", 2, 4),
     ("unit", 5, "act"), ("turn", "qb"), ("steps", 4, 6), ("unit", 6, "act"), ("steps", 6, 7),
     ("unit", 7, "act"), ("turn", "kb"), ("steps", 7, 9), ("unit", 8, "act"), ("steps", 9, 19)],
    [("unit", 0, "dve", 4), ("unit", 1, "dve", 4), ("unit", 2, "dve", 4), ("turn", "qc"),
     ("unit", 3, "dve", 4), ("unit", 4, "act"), ("turn", "kc"), ("steps", 0, 1), ("unit", 5, "act"),
     ("steps", 1, 3), ("unit", 6, "dve", 4), ("steps", 3, 5), ("unit", 7, "dve", 4), ("steps", 5, 6),
     ("unit", 8, "act"), ("turn", "qd"), ("steps", 6, 8), ("unit", 9, "dve", 2), ("unit", 10, "dve", 2),
     ("cmp", "pos"), ("turn", "ks"), ("turn", "kw"), ("cmp", "in"), ("steps", 8, 9), ("cmp", "compress"),
     ("steps", 9, 10), ("cmp", "keys"), ("steps", 10, 11), ("cmp", "scores"), ("steps", 11, 12),
     ("cmp", "p"), ("steps", 12, 13), ("cmp", "values"), ("steps", 13, 27)])


def turns_before(name):
    a = b = 0
    for layer in range(2):
        a, b = a + 2, b + 2
        for what, *arg in ORDER[layer]:
            if what == "turn" or what == "cmp" and arg[0] in ("pos", "keys", "p"):
                both = arg[0] in ("qa", "qb", "kb", "qc", "kc", "qd")
                a += both or arg[0] in ("ks", "pos", "keys", "p")
                b += both or arg[0] in ("ka", "kw")
                if arg[0] == name:
                    return a, b
        a, b = a + 2 + 2 + 1, b + 2 + 2 + 1


T_QA_A, T_QA_B = turns_before("qa")
T_QC_A, T_QC_B = turns_before("qc")
T_POS = turns_before("pos")[0]
PR, NMN = [], []
for kind, _ in JOBS[0] + JOBS[1]:
    PR.append((PR or [0])[-1] + (1 if kind == "B" else 2))
    NMN.append((NMN or [0])[-1] + (kind != "B"))
V_THERE = {0: ("dve", 3), 8: ("act", 6), 16: ("act", 8), 24: ("dve", 10), 32: ("dve", 11)}
N_LOADS = 28
N_CONST_A, N_CONST = 5, 14
CF_COMPRESSED = 2
CD_T2, CD_KEYS, CD_ARG, CD_P = 1, 2, 4, 5
SKEW = 3


def program(nc, x, ev_norm, ev_w_in, ev_q_norm, ev_k_norm, ev_sink, ev_w_out,
            od_norm, od_w_in, od_c_q_norm, od_c_k_norm, od_d_q_norm, od_d_k_norm,
            od_cmp_pos, od_cmp_w, od_w_out,
            moe_norm, moe_w_grp, moe_b_grp, moe_w_exp, moe_b_exp, moe_w_gate, moe_w_up, moe_w_down,
            out):
    with ExitStack() as ctx:
        def sb(name, shape, dt=F32):
            return ctx.enter_context(nc.sbuf_tensor(name, shape, dt))

        def sem(name):
            return ctx.enter_context(nc.semaphore(name))

        ring = sb("ring", [P, RING, UNIT])
        xs = sb("x_res", [P, NT, D])
        xn = sb("x_normed", [P, NT, D])
        hT = sb("h_transposed", [P, KD, S])
        o_sb = xn
        oT = hT
        ident = sb("ident", [P, P])
        before = sb("before", [P, P])
        ones = sb("ones", [P, P])
        iota_s = sb("iota_slots", [P, P])
        iota8 = sb("iota_8", [P, NT, EG])
        iota_e = sb("iota_experts", [P, NE])
        first_q = sb("first_positions", [P, NE])
        iota_j = sb("iota_tiles", [P, MAXOVER])
        steps7 = sb("tile_ends", [P, S // TILE - 1])
        g_col = sb("norm_gains", [P, 4, KD])
        w_rt = sb("router_w", [P, 2, KD, NG + NE])
        b_rt = sb("router_b", [P, 2, NG + NE])
        w_gd = sb("gate_w", [P, KD, GATES])
        qk_g = sb("qk_gains", [P, 8])
        sink = sb("sink", [P, 8])
        eps_t = sb("eps", [P, 1])
        one_t = sb("one", [P, 1])
        ssq = sb("ssq", [P, NT])
        lnr = sb("ln_ms", [P, NT])
        rstd = sb("rstd", [P, NT])
        pos_in = sb("pos_rows", [NCMP, 2, P])

        ARENA = 19700
        arena = sb("arena", [P, ARENA])
        at = [0]

        def carve(*dims):
            n = 1
            for v in dims:
                n *= v
            a = arena[:, at[0]:at[0] + n]
            at[0] += n
            assert at[0] <= ARENA, at[0]
            if len(dims) > 1:
                names = "abcd"[:len(dims)]
                a = a.rearrange(f"p ({' '.join(names)}) -> p {' '.join(names)}", **dict(zip(names, dims)))
            return a

        btab = carve(8, SC)
        smask = carve(SC)
        sreset = carve(SC)
        stage = [carve(NT, 512) for _ in range(2)]
        stk = [carve(NT, 128) for _ in range(2)]
        qT = [carve(4, S) for _ in range(2)]
        kT = carve(4, S)
        kTp = [carve(S) for _ in range(2)]
        vbig = carve(NT, 512)
        vsm = [carve(NT, 128) for _ in range(2)]
        sq = carve(NT, 4, DH)
        red = carve(NT, 4)
        lq = carve(NT, 4)
        rq = carve(NT, 4)
        s_sb = [carve(SC) for _ in range(2)]
        mark = at[0]
        ea = [carve(SC) for _ in range(2)]
        la = [carve(SC) for _ in range(2)]
        cu = [carve(SC) for _ in range(2)]
        end, at[0] = at[0], mark
        t2 = [carve(2, S) for _ in range(2)]
        cin = carve(NT, 4, 2, DH)
        v_blk = carve(8, DH)
        at[0] = max(at[0], end)
        p_sb = [carve(SC) for _ in range(3)]
        pT = [carve(SC) for _ in range(2)]
        mx = carve(24, 2)
        nm = carve(24, 2)
        den = carve(24, 2)
        es = carve(8, 2)
        cf = carve(8, 2)
        otmp = carve(NT, 4 * DH)
        posT = carve(2, NCMP)
        kc_n = carve(DH)
        vc = carve(DH)
        spread = carve(4, 32)
        kc_b = carve(2, DH)
        kcT = carve(32)
        ctab = carve(NT, 4, 2, NCMP)
        cmask = carve(NT, 4, 2, NCMP)
        cs = carve(NT, 4, 2, NCMP)
        cmx = carve(NT, 8)
        cden = carve(NT, 8)
        cz = carve(NT, 8)
        ccf = carve(NT, 8)
        pcT = carve(NT, P)
        blk = carve(8)
        csm = carve(4)
        gates = carve(NT, 8, 3)

        at[0] = 0
        junk_m = carve(D)
        xt = carve(KD, P)
        oneh = carve(NT, P)
        comb = carve(NT, P)
        ctmp = carve(NT, P)
        otmp_m = carve(NT, P)
        combT = carve(NT, P)
        en = carve(FF)
        hid = carve(FF)
        hidT = carve(KF, P)
        yb = carve(D)
        lg = carve(NT, NG + NE)
        r_gm, r_i, r_wm, r_pg, r_ws, r_m1, r_m2, r_s, r_q1, r_q2 = (carve(NT) for _ in range(10))
        p_q, places = (carve(2, NT) for _ in range(2))
        ge, g_eq, g_oh = (carve(NT, NG) for _ in range(3))
        we, e_eq, oh1, oh2 = (carve(NT, EG) for _ in range(4))
        mask, f1, f2, wtmp, qe, over = (carve(NT, NE) for _ in range(6))
        cnt, tov, vin, vex, dq = (carve(NE) for _ in range(5))
        cmp7 = carve(NE, S // TILE - 1)
        ov = [carve(MAXOVER, NE) for _ in range(3)]
        ovr = carve(MAXOVER)
        nb_f = carve(GROUPS)
        nb_s = carve(1)
        ove_i = sb("overflow_expert", [P, MAXOVER], I32)
        nb_i = sb("batches", [P, 1], I32)

        bank = [ctx.enter_context(nc.psum_tensor(f"bank{i}", [P, 512], F32)) for i in range(8)]

        landed = [sem(f"unit_landed{i}") for i in range(RING)]
        cmp_landed, x_landed, consts_landed = sem("cmp_landed"), sem("x_landed"), sem("consts_landed")
        consts, tables = sem("consts_built"), sem("tables_built")
        pool_chain, dve_chain, act_chain = sem("pool_chain"), sem("dve_chain"), sem("act_chain")
        rstd_ready, xn_ready, x_ready = sem("rstd_ready"), sem("xn_ready"), sem("x_ready")
        ta_full, ta_free = sem("transposes_a_full"), sem("transposes_a_free")
        tb_full, tb_free = sem("transposes_b_full"), sem("transposes_b_free")
        pr_full, pr_act, pr_dve = sem("proj_full"), sem("proj_drained_act"), sem("proj_drained_dve")
        sq_ready, ms_ready, rq_ready = sem("squares_ready"), sem("head_ms_ready"), sem("head_rstd_ready")
        sc_full, sc_free, nm_ready = sem("scores_full"), sem("scores_masked"), sem("neg_max_ready")
        p_ready, pt_full, pt_ready = sem("p_ready"), sem("pT_full"), sem("pT_ready")
        ln_ready, suffix_ready, arg_ready = sem("ln_ready"), sem("suffix_ready"), sem("stick_arg_ready")
        o_full, o_ready = sem("o_full"), sem("o_ready")
        es_in, es_out = sem("sink_arg_ready"), sem("sink_exp_ready")
        cmp_full, cmp_dve, cmp_act = sem("cmp_psum_full"), sem("cmp_by_dve"), sem("cmp_by_act")
        gate_full, gate_exp, gate_ready = sem("gate_full"), sem("gate_exp_ready"), sem("gate_ready")
        wo_used = sem("out_proj_units_used")
        rt_full, rt_gs, rt_ge = sem("router_psum_full"), sem("group_arg_ready"), sem("group_exp_ready")
        rt_ws, rt_we, rt_mask = sem("expert_arg_ready"), sem("expert_exp_ready"), sem("choice_ready")
        list_ready = sem("batch_count_ready")
        moe_landed = [[sem(f"expert_unit_landed{l}_{i}") for i in range(BATCH)] for l in range(2)]

        def two(name):
            return [sem(f"{name}{l}") for l in range(2)]
        added = two("batch_added")
        c_copied, places_moved = sem("places_copied"), sem("places_moved")
        q_ready, b_ready, c_ready = two("places_ready"), two("onehot_ready"), two("weights_ready")
        ga_full, xt_ready = two("gathered"), two("inputs_ready")
        gu_full, en_ready, hid_ready = two("gate_up_full"), two("exp_ready"), two("hidden_ready")
        ct_full, ct_ready = two("weights_turned"), two("weightsT_ready")
        ht_full, ht_ready = two("hidden_turned"), two("hiddenT_ready")
        y_full, y_act, y_dve = two("down_full"), two("y_ready_act"), two("y_ready_dve")
        loop_dve, loop_pool = two("batch_chain_dve"), two("batch_chain_pool")
        ac_full, stored = sem("combined_full"), sem("stored")

        def cols(a, u):
            return a[:, :, u * UC:(u + 1) * UC]

        def by_head(a):
            return a.rearrange("p t (h d) -> p t h d", d=DH)

        def half_pairs(a, u):
            return a.rearrange("p t (a u d) -> p t a u d", a=4, u=2)[:, :, :, u, :]

        DST = ({0: (half_pairs(stage[0], 0), None), 1: (half_pairs(stage[0], 1), None),
                2: (by_head(stk[0]), vsm[0]), 3: cols(stage[1], 0), 4: cols(stage[1], 1),
                5: cols(stage[0], 0), 6: cols(stage[0], 1), 7: cols(vbig, 0), 8: cols(vbig, 1)},
               {0: (by_head(cols(stage[0], 0)), None), 1: (by_head(cols(stage[0], 1)), None),
                2: (by_head(cols(stage[1], 0)), None), 3: (by_head(cols(stage[1], 1)), None),
                4: cols(vbig, 0), 5: cols(vbig, 1),
                6: (half_pairs(stage[0], 0), None), 7: (half_pairs(stage[0], 1), None),
                8: None, 9: (by_head(stk[0]), vsm[0]), 10: (by_head(stk[1]), vsm[1])})
        TURNS = {"qa": (0, None, "dve", 2), "ka": (2, "b", "dve", 3),
                 "qb": (1, None, "act", 2), "kb": (0, None, "act", 4),
                 "qc": (0, None, "dve", 5), "kc": (1, None, "dve", 7),
                 "qd": (0, None, "dve", 9), "ks": (2, "a", "dve", 10), "kw": (3, "b", "dve", 11)}
        TDST = {"qa": (qT[0], qk_g[:, 0:1]), "ka": (kTp[0], qk_g[:, 1:2]), "qb": (qT[1], 0.125), "kb": (kT, None),
                "qc": (qT[0], qk_g[:, 2:3]), "kc": (kT, qk_g[:, 3:4]), "qd": (qT[1], qk_g[:, 4:5]),
                "ks": (kTp[0], qk_g[:, 6:7]), "kw": (kTp[1], qk_g[:, 7:8])}

        def tok(a, k):
            return a.rearrange("q (p k) -> q k p", k=KD)[:, k, :]

        def slot_of(n):
            return n % RING

        def landings(n):
            here = [m for m in range(slot_of(n), n + 1, RING)
                    if m < U_MOE0 - 1 or U_OD_IN <= m < U_MOE1 and m != U_CMP]
            return 16 * len(here)

        def released(n):
            if n < U_EV_OUT:
                return pr_full, n + 1
            if n == U_MOE0 - 1:
                return released(n - RING)
            if n < U_MOE0:
                return wo_used, n - U_EV_OUT + 1
            if n < U_CMP:
                return pr_full, EV_UNITS + n - U_OD_IN + 1
            if n == U_CMP:
                return cmp_full, CF_COMPRESSED
            return wo_used, OUT_UNITS + n - U_OD_OUT + 1

        def seconds(v):
            return v.rearrange("p (h q d) -> p h q d", h=4, q=NT)

        class Chain:
            def __init__(self, eng, s, before=0):
                self.eng, self.s, self.n, self.before = eng, s, 0, before

            def count(self, ins):
                self.n += 1
                ins.then_inc(self.s, 1)

            def __call__(self, ins):
                self.count(ins)
                self.eng.wait_ge(self.s, self.before + self.n)

        block = ctx.enter_context(nc.Block())

        @block.sync
        def _(sp):
            for t in range(NT):
                sp.dma_start(xs[:, t, :], x[0, t * P:(t + 1) * P, :]).then_inc(x_landed, 16)

            def load(n, src, shape, after_moe=None):
                if after_moe is not None and n - RING < U_MOE0 + NE * PER_EXPERT:
                    nb = after_moe
                    sp.wait_ge(gu_full[0] if (n - U_MOE0) % RING < 2 * GROUPS else y_full[0], nb)
                elif n >= RING:
                    sp.wait_ge(*released(n - RING))
                dst = ring[:, slot_of(n), :].rearrange("p (a b) -> p a b", a=shape)
                sp.dma_start(dst, src).then_inc(landed[slot_of(n)], 16)

            def proj_units(u0, w, units, after_moe=None):
                wv = w[0].rearrange("(p k) n -> p k n", k=KD)
                for u in range(units):
                    load(u0 + u, wv[:, :, u * UC:(u + 1) * UC], KD, after_moe)

            def out_units(u0, w):
                for u in range(OUT_UNITS):
                    load(u0 + u, w[0, u * 2 * P:(u + 1) * 2 * P, :].rearrange("(k p) n -> p k n", p=P), 2)

            def expert(l, e, c):
                one = bass.ds(l * NE + e, 1)
                if c < 2:
                    w = (moe_w_gate, moe_w_up)[c].rearrange("l e (p k) n -> (l e) p k n", k=KD)
                else:
                    w = moe_w_down.rearrange("l e (k p) n -> (l e) p k n", p=P)
                return w[one].rearrange("o p k n -> p (o k) n")

            def expert_dst(l, i):
                return ring[:, slot_of(U_MOE[l] + i), :].rearrange("p (a b) -> p a b", a=KD if i < 2 * GROUPS else KF)

            def part(i):
                return (i // 2, i % 2) if i < 2 * GROUPS else (i - 2 * GROUPS, 2)

            def moe_units(l):
                for i in range(BATCH):
                    sp.wait_ge(*released(U_MOE[l] + i - RING))
                    g, c = part(i)
                    sp.dma_start(expert_dst(l, i), expert(l, g, c)).then_inc(moe_landed[l][i], 16)
                with sp.Fori(1, OWN) as b:
                    for i in range(BATCH):
                        g, c = part(i)
                        sp.wait_ge(y_full[l] if c == 2 else gu_full[l], b)
                        sp.dma_start(expert_dst(l, i), expert(l, b * GROUPS + g, c)).then_inc(moe_landed[l][i], 16)
                sp.wait_ge(list_ready, l + 1)
                nb = sp.value_load(nb_i[0:1, 0:1], min_val=OWN, max_val=MAXB)
                with sp.If(nb - OWN):
                    with sp.Fori(OWN, nb) as b:
                        ids = [sp.value_load(ove_i[0:1, bass.ds((b - OWN) * GROUPS + g, 1)], min_val=0, max_val=NE - 1)
                               for g in range(GROUPS)]
                        for i in range(BATCH):
                            g, c = part(i)
                            sp.wait_ge(y_full[l] if c == 2 else gu_full[l], b)
                            sp.dma_start(expert_dst(l, i), expert(l, ids[g], c)).then_inc(moe_landed[l][i], 16)
                return nb

            proj_units(U_EV_IN, ev_w_in, EV_UNITS)
            out_units(U_EV_OUT, ev_w_out)
            nb = moe_units(0)
            proj_units(U_OD_IN, od_w_in, OD_UNITS, nb)
            sp.wait_ge(y_full[0], nb)
            cw = od_cmp_w[0].rearrange("w (h l) d e -> h d w l e", h=2)
            for h in range(2):
                for w in range(2):
                    dst = ring[h * DH:(h + 1) * DH, slot_of(U_CMP), w * NCMP * DH:(w + 1) * NCMP * DH]
                    sp.dma_start(dst.rearrange("p (l e) -> p l e", l=NCMP), cw[h, :, w]).then_inc(cmp_landed, 16)
            out_units(U_OD_OUT, od_w_out)
            moe_units(1)
            for t in range(NT):
                sp.wait_ge(x_ready, 3 * NT + t + 1)
                sp.dma_start(out[0, t * P:(t + 1) * P, :], xs[:, t, :]).then_inc(stored, 16)
            sp.wait_ge(stored, 16 * NT)

        @block.gpsimd
        def _(pool):
            g = nc.gpsimd
            chain = Chain(pool, pool_chain)

            g.memset(eps_t[:], EPS).then_inc(consts, 1)
            g.memset(one_t[:], 1.0).then_inc(consts, 1)
            g.memset(ones[:], 1.0).then_inc(consts, 1)
            chain(g.memset(ident[:], 0.0))
            g.affine_select(out=ident[:], in_=ident[:], compare_op=ALU.not_equal, fill=1.0, base=0,
                            pattern=[[-1, P]], channel_multiplier=1).then_inc(consts, 1)
            chain(g.memset(before[:], 1.0))
            g.affine_select(out=before[:], in_=before[:], compare_op=ALU.is_gt, fill=0.0, base=0,
                            pattern=[[1, P]], channel_multiplier=-1).then_inc(consts, 1)

            pool.wait_ge(consts_landed, 16 * N_LOADS)
            for c in (0, 2, 4):
                g.tensor_scalar(qk_g[:, c:c + 1], qk_g[:, c:c + 1], 0.125, None, ALU.mult).then_inc(consts, 1)
            g.iota(first_q[:], pattern=[[TILE, NE]], base=0, channel_multiplier=0,
                   allow_small_or_imprecise_dtypes=True).then_inc(consts, 1)
            g.iota(iota_j[:], pattern=[[1, MAXOVER]], base=0, channel_multiplier=0,
                   allow_small_or_imprecise_dtypes=True).then_inc(consts, 1)
            g.iota(steps7[:], pattern=[[TILE, S // TILE - 1]], base=TILE, channel_multiplier=0,
                   allow_small_or_imprecise_dtypes=True).then_inc(consts, 1)
            g.iota(iota_s[:], pattern=[[1, P]], base=0, channel_multiplier=0,
                   allow_small_or_imprecise_dtypes=True).then_inc(consts, 1)
            g.iota(iota8[:], pattern=[[0, NT], [1, EG]], base=0, channel_multiplier=0,
                   allow_small_or_imprecise_dtypes=True).then_inc(consts, 1)
            g.iota(iota_e[:], pattern=[[1, NE]], base=0, channel_multiplier=0,
                   allow_small_or_imprecise_dtypes=True).then_inc(consts, 1)

            def bias_table(windowed):
                chain(g.iota(btab[:, 7, 0:P], pattern=[[-1, P]], base=0, channel_multiplier=1,
                             allow_small_or_imprecise_dtypes=True))
                chain(g.iota(btab[:, 7, P:SC], pattern=[[-1, S]], base=P, channel_multiplier=1,
                             allow_small_or_imprecise_dtypes=True))
                for h in range(8):
                    chain(g.tensor_scalar(btab[:, h, :], btab[:, 7, :], -SLOPES[h], None, ALU.mult))
                for a, n, base in ((0, P, 0), (P, S, P)):
                    v = btab[:, :, a:a + n]
                    chain(g.affine_select(out=v, in_=v, compare_op=ALU.is_ge,
                                          fill=NEG, base=base, pattern=[[0, 8], [-1, n]], channel_multiplier=1))
                if windowed:
                    chain(g.affine_select(out=btab[:, :, P:SC], in_=btab[:, :, P:SC], compare_op=ALU.is_gt,
                                          fill=NEG, base=0, pattern=[[0, 8], [1, S]], channel_multiplier=-1))

            bias_table(True)
            chain(g.memset(smask, 0.0))
            chain(g.affine_select(out=smask[:, 0:P], in_=smask[:, 0:P], compare_op=ALU.is_gt, fill=NEG,
                                  base=0, pattern=[[-1, P]], channel_multiplier=1))
            chain(g.affine_select(out=smask[:, P:SC], in_=smask[:, P:SC], compare_op=ALU.is_gt, fill=NEG,
                                  base=P, pattern=[[-1, S]], channel_multiplier=1))
            chain(g.memset(sreset, 1.0))
            g.memset(sreset[:, P - 1:P], 0.0).then_inc(tables, 1)
            def stick_args():
                for n in range(8):
                    b = n % 2
                    pool.wait_ge(suffix_ready, n + 1)
                    g.tensor_tensor(la[b], s_sb[b], cu[b], ALU.subtract).then_inc(arg_ready, 1)

            def batch_weights(l):
                def one(b, before, first):
                    ch = Chain(pool, loop_pool[l], before)
                    if not first:
                        pool.wait_ge(ct_full[l], b)
                        ch(g.tensor_tensor(p_q, p_q, places, ALU.subtract))
                        g.sem_inc(places_moved, 1)
                    for t in range(NT):
                        for dst, q, w in ((comb, 0, r_m1), (otmp_m, 1, r_m2)):
                            last = g.tensor_scalar(dst[:, t, :], iota_s[:], p_q[:, q, t:t + 1], w[:, t:t + 1],
                                                   ALU.is_equal, ALU.mult)
                            if not (t == NT - 1 and q == 1):
                                ch.count(last)
                    ch(last)
                    g.tensor_tensor(comb, comb, otmp_m, ALU.add).then_inc(c_ready[l], 1)
                    return ch.n

                pool.wait_ge(q_ready[l], 1)
                chain(g.tensor_copy(p_q[:, 0], r_q1))
                chain(g.tensor_copy(p_q[:, 1], r_q2))
                chain(g.memset(places, float(P)))
                g.sem_inc(c_copied, 1)
                done = one(0, 0, True)
                pool.wait_ge(list_ready, l + 1)
                nb = pool.value_load(nb_i[0:1, 0:1], min_val=OWN, max_val=MAXB)
                with pool.Fori(1, nb) as b:
                    per = done + 1
                    assert one(b, b * per - 1, False) == per

            def cmp_tables():
                chain(g.iota(ctab.rearrange("p t a b n -> p t (a b) n"),
                             pattern=[[P, NT], [0, 8], [-CSTEP, NCMP]], base=-(CLEN - 1),
                             channel_multiplier=1, allow_small_or_imprecise_dtypes=True))
                for pr in range(4):
                    for kv in range(2):
                        v = ctab[:, :, pr, kv, :]
                        chain(g.tensor_scalar(v, v, -SLOPES[kv * 4 + pr], None, ALU.mult))
                chain(g.memset(cmask, 1.0))
                for a, fill in ((ctab, NEG), (cmask, 0.0)):
                    for t in range(NT):
                        v = a[:, t].rearrange("p a b n -> p (a b) n")
                        chain(g.affine_select(out=v, in_=v, compare_op=ALU.is_ge, fill=fill,
                                              base=P * t - (CLEN - 1), pattern=[[0, 8], [-CSTEP, NCMP]],
                                              channel_multiplier=1))
                    chain(g.memset(a.rearrange("p t a b n -> p (t a b) n")[:, :, NCMP - 1:NCMP], fill))
                pool.wait_ge(consts, N_CONST)
                for a in range(4):
                    chain(g.tensor_copy(spread[0:32, a, :], ident[0:32, 0:32]))
                chain(g.memset(blk, 1.0))
                chain(g.affine_select(out=blk, in_=blk, compare_op=ALU.is_ge, fill=0.0, base=0,
                                      pattern=[[-NCMP, 8]], channel_multiplier=1))
                g.affine_select(out=blk, in_=blk, compare_op=ALU.is_ge, fill=0.0, base=NCMP - 1,
                                pattern=[[NCMP, 8]], channel_multiplier=-1).then_inc(tables, 1)

            stick_args()
            batch_weights(0)
            pool.wait_ge(x_ready, 2 * NT)
            bias_table(False)
            cmp_tables()
            batch_weights(1)

        @block.tensor
        def _(pe):
            T = nc.tensor
            turns = {"a": 0, "b": 0}
            units, drains = [0], []
            nd = {"act": 0, "dve": 0}
            job = {"s": 0, "t": 0, "v": 0}

            def turn(which, pieces):
                full, free, bk = (ta_full, ta_free, 2) if which == "a" else (tb_full, tb_free, 3)
                if turns[which]:
                    pe.wait_ge(free, turns[which])
                for c, v in pieces:
                    k, m = v.shape[0], 1
                    for e in v.shape[1:]:
                        m *= e
                    last = T.transpose(bank[bk][0:m, c:c + k], v, ident[0:k, 0:k])
                last.then_inc(full, 1)
                turns[which] += 1

            def turned():
                pe.wait_ge(ta_free, turns["a"])
                pe.wait_ge(tb_free, turns["b"])

            def norm_turn(n):
                if n == 0:
                    pe.wait_ge(consts, N_CONST_A)
                pe.wait_ge(xn_ready, NT * (n + 1))
                for b in range(4):
                    turn("ab"[b % 2], [(kk * S + t * P, tok(xn[:, t, :], 2 * b + kk))
                                       for kk in range(2) for t in range(NT)])
                turned()

            def project(n, who):
                if units[0] >= 2:
                    pe.wait_ge(*drains[units[0] - 2])
                pe.wait_ge(landed[slot_of(n)], landings(n))
                w = ring[:, slot_of(n), :].rearrange("p (k c) -> p k c", k=KD)
                for t in range(NT):
                    for k in range(KD):
                        last = T.matmul(bank[units[0] % 2][:, t * UC:(t + 1) * UC], hT[:, k, t * P:(t + 1) * P],
                                        w[:, k, :], start=(k == 0), stop=(k == KD - 1))
                last.then_inc(pr_full, 1)
                units[0] += 1
                nd[who] += 1
                drains.append((pr_act if who == "act" else pr_dve, nd[who]))

            def qk_of(kind, h):
                if kind in "BC":
                    r = slice(DH * (h % 2), DH * (h % 2) + DH)
                    return (qT[1] if kind == "B" else qT[0])[r, h // 2, :], kT[r, h // 2, :]
                r = slice(DH * (h // 4), DH * (h // 4) + DH)
                k = kTp[1] if kind == "W" else kTp[0]
                return (qT[0] if kind == "A" else qT[1])[r, h % 4, :], k[r, :]

            def v_of(kind, h, t):
                if kind in "BC":
                    return vbig[:, t, h * DH:(h + 1) * DH]
                return vsm[kind == "W"][:, t, (h // 4) * DH:(h // 4 + 1) * DH]

            def scores(kind, h):
                n = job["s"]
                if n >= 2:
                    pe.wait_ge(sc_free, n - 1)
                if n in V_THERE:
                    turned()
                q, k = qk_of(kind, h)
                b = bank[4 + n % 2]
                T.matmul(b[:, 0:P], q[:, 0:P], k[:, 0:P], start=True, stop=True)
                T.matmul(b[:, P:SC], q[:, P:S], k[:, 0:S], start=True, stop=True).then_inc(sc_full, 1)
                job["s"] += 1

            def turn_p():
                n = job["t"]
                pe.wait_ge(p_ready, PR[n])
                if n:
                    pe.wait_ge(pt_ready, n)
                for c in range(3):
                    last = T.transpose(bank[6][:, c * P:(c + 1) * P], p_sb[n % 3][:, c * P:(c + 1) * P], ident[:])
                last.then_inc(pt_full, 1)
                job["t"] += 1

            def values(kind, h):
                n = job["v"]
                pe.wait_ge(pt_ready, n + 1)
                if n % 4 == 0 and n:
                    pe.wait_ge(o_ready, n // 4)
                if n == len(JOBS[0]):
                    pe.wait_ge(gate_ready, 1)
                if n in V_THERE:
                    who, count = V_THERE[n]
                    pe.wait_ge(pr_dve if who == "dve" else pr_act, count)
                o = bank[7][:, (n % 4) * P:(n % 4 + 1) * P]
                pt = pT[n % 2]
                T.matmul(o[:, 0:DH], pt[:, 0:P], v_of(kind, h, 0), start=True, stop=True)
                T.matmul(o[:, DH:P], pt[:, P:2 * P], v_of(kind, h, 0), start=True, stop=False)
                T.matmul(o[:, DH:P], pt[:, 2 * P:3 * P], v_of(kind, h, 1), start=False, stop=True).then_inc(o_full, 1)
                job["v"] += 1

            def step(jobs, i):
                if i < len(jobs):
                    scores(*jobs[i])
                if 0 <= i - 2 < len(jobs):
                    turn_p()
                if 0 <= i - SKEW < len(jobs):
                    values(*jobs[i - SKEW])

            def pairs(src, ps):
                return [(i * S + t * P, src[:, t, pr * P:(pr + 1) * P]) for i, pr in enumerate(ps) for t in range(NT)]

            def turn_qk(what):
                src, which, who, count = TURNS[what]
                pe.wait_ge(pr_act if who == "act" else pr_dve, count)
                if src in (2, 3):
                    turn(which, pairs(stk[src - 2], [0]))
                else:
                    turn("a", pairs(stage[src], [0, 1]))
                    turn("b", pairs(stage[src], [2, 3]))

            def cmp_stage(k):
                w = ring[:, slot_of(U_CMP), :].rearrange("p (w l e) -> p w l e", w=2, l=NCMP)
                if k == "pos":
                    pe.wait_ge(consts_landed, 16 * N_LOADS)
                    turn("a", [(c * NCMP, pos_in[:, c, :]) for c in range(2)])
                elif k == "in":
                    pe.wait_ge(pr_act, nd["act"])
                    pe.wait_ge(pr_dve, nd["dve"])
                    for c in range(2):
                        for h in range(2):
                            for t in range(NT):
                                v = cin[:, t, 2 * c + h].rearrange("p a d -> p (a d)")
                                last = T.transpose(bank[c][:, h * S + t * P:h * S + (t + 1) * P],
                                                   v, ident[:])
                    last.then_inc(cmp_full, 1)
                elif k == "compress":
                    pe.wait_ge(cmp_landed, 4 * 16)
                    pe.wait_ge(cmp_dve, CD_T2)
                    tk, tv = (a.rearrange("p h (n l) -> p l (h n)", l=CSTEP) for a in t2)
                    for l in range(NCMP):
                        T.matmul(bank[0][0:32, 0:DH], tk[:, l], w[:, 0, l, :], start=(l == 0), stop=(l == NCMP - 1))
                    for l in range(NCMP):
                        last = T.matmul(bank[1][0:32, 0:DH], tv[:, l],
                                        w[:, 1, l, :], start=(l == 0), stop=(l == NCMP - 1))
                    last.then_inc(cmp_full, 1)
                elif k == "keys":
                    pe.wait_ge(cmp_dve, CD_KEYS)
                    turn("a", [(0, kc_b[0:32].rearrange("p a d -> p (a d)"))])
                    pe.wait_ge(cmp_act, 1)
                    T.matmul(bank[1][:, 0:DH], spread[0:32].rearrange("p a b -> p (a b)"), vc[0:32, :],
                             start=True, stop=True).then_inc(cmp_full, 1)
                elif k == "scores":
                    turned()
                    for t in range(NT):
                        for pr in range(4):
                            last = T.matmul(bank[0][:, t * P + pr * 32:t * P + (pr + 1) * 32],
                                            qT[1][:, pr, t * P:(t + 1) * P], kcT[:], start=True, stop=True)
                    last.then_inc(cmp_full, 1)
                elif k == "p":
                    pe.wait_ge(cmp_dve, CD_P)
                    turn("a", [(t * P, cs[:, t].rearrange("p a b n -> p (a b n)")) for t in range(NT)])
                elif k == "values":
                    turned()
                    for t in range(NT):
                        last = T.matmul(bank[t][:], pcT[:, t, :], v_blk.rearrange("p h e -> p (h e)"), start=True, stop=True)
                    last.then_inc(cmp_full, 1)

            def mixer(layer):
                norm_turn(2 * layer)
                if layer:
                    for t in range(NT):
                        for k in range(KD):
                            last = T.matmul(bank[7][:, t * 32:t * 32 + GATES], hT[:, k, t * P:(t + 1) * P], w_gd[:, k, :],
                                            start=(k == 0), stop=(k == KD - 1))
                    last.then_inc(gate_full, 1)
                for what, *arg in ORDER[layer]:
                    if what == "unit":
                        project((U_EV_IN, U_OD_IN)[layer] + arg[0], arg[1])
                    elif what == "turn":
                        turn_qk(arg[0])
                    elif what == "cmp":
                        cmp_stage(arg[0])
                    elif what == "steps":
                        for i in range(arg[0], arg[1]):
                            step(JOBS[layer], i)
                pe.wait_ge(o_ready, (4, 10)[layer])
                for b in range(4):
                    turn("ab"[b % 2], [(kk * S + t * P, o_sb[:, t, (2 * b + kk) * P:(2 * b + kk + 1) * P])
                                       for kk in range(2) for t in range(NT)])
                turned()
                for u in range(OUT_UNITS):
                    n = (U_EV_OUT, U_OD_OUT)[layer] + u
                    pe.wait_ge(landed[slot_of(n)], landings(n))
                    w = ring[:, slot_of(n), :].rearrange("p (k c) -> p k c", k=2)
                    for kk in range(2):
                        for t in range(NT):
                            for hf in range(2):
                                last = T.matmul(bank[4 + 2 * t + hf][:], oT[:, 2 * u + kk, t * P:(t + 1) * P],
                                                w[:, kk, hf * 512:(hf + 1) * 512],
                                                start=(u == 0 and kk == 0), stop=(u == OUT_UNITS - 1 and kk == 1))
                    last.then_inc(wo_used, 1)

            def moe(l):
                norm_turn(2 * l + 1)
                for t in range(NT):
                    for k in range(KD):
                        last = T.matmul(bank[0][:, t * 64:t * 64 + NG + NE], hT[:, k, t * P:(t + 1) * P], w_rt[:, l, k, :],
                                        start=(k == 0), stop=(k == KD - 1))
                last.then_inc(rt_full, 1)
                pe.wait_ge(rt_mask, l + 1)
                m0, m1, c = mask[:, 0, :], mask[:, 1, :], bank[1]
                T.matmul(c[:, 0:NE], before[:], m0, start=True, stop=True)
                T.matmul(c[:, NE:2 * NE], ones[:], m0, start=True, stop=False)
                T.matmul(c[:, NE:2 * NE], before[:], m1, start=False, stop=True)
                T.matmul(c[:, 2 * NE:3 * NE], ones[:], m0, start=True, stop=False)
                T.matmul(c[:, 2 * NE:3 * NE], ones[:], m1, start=False, stop=True).then_inc(rt_full, 1)

                def gather(b):
                    pe.wait_ge(b_ready[l], b + 1)
                    for k in range(KD):
                        for t in range(NT):
                            last = T.matmul(bank[2 + k // 4][:, (k % 4) * P:(k % 4 + 1) * P], tok(xn[:, t, :], k),
                                            oneh[:, t, :], start=(t == 0), stop=(t == NT - 1))
                    last.then_inc(ga_full[l], 1)

                def there(i, b):
                    pe.wait_ge(moe_landed[l][i], 16 * (b + 1))

                def batch(b, first):
                    pe.wait_ge(xt_ready[l], b + 1)
                    if not first:
                        pe.wait_ge(hid_ready[l], b)
                    for k in range(KD):
                        for g in range(GROUPS):
                            if k == 0:
                                there(2 * g, b)
                                there(2 * g + 1, b)
                            s = slot_of(U_MOE[l] + 2 * g)
                            w = ring[:, s:s + 2, :].rearrange("p u (k c) -> p u k c", k=KD)[:, :, k, :]
                            last = T.matmul(bank[0][g * TILE:(g + 1) * TILE, :], xt[:, k, g * TILE:(g + 1) * TILE], w,
                                            start=(k == 0), stop=(k == KD - 1))
                    last.then_inc(gu_full[l], 1)
                    pe.wait_ge(c_ready[l], b + 1)
                    if not first:
                        pe.wait_ge(ht_ready[l], b)
                    for t in range(NT):
                        last = T.transpose(bank[1][:, (2 + t) * P:(3 + t) * P], comb[:, t, :], ident[:])
                    last.then_inc(ct_full[l], 1)
                    if not first:
                        pe.wait_ge(y_act[l], b)
                        pe.wait_ge(y_dve[l], b)
                    gather(b + 1)
                    pe.wait_ge(hid_ready[l], b + 1)
                    pe.wait_ge(ct_ready[l], b + 1)
                    for k in range(KF):
                        last = T.transpose(bank[1][:, k * P:(k + 1) * P], hid[:, k * P:(k + 1) * P], ident[:])
                    last.then_inc(ht_full[l], 1)
                    pe.wait_ge(ht_ready[l], b + 1)
                    pe.wait_ge(xt_ready[l], b + 2)
                    for k in range(KF):
                        for hf in range(2):
                            for g in range(GROUPS):
                                if k == 0 and hf == 0:
                                    there(2 * GROUPS + g, b)
                                w = ring[:, slot_of(U_MOE[l] + 2 * GROUPS + g), :].rearrange("p (k c) -> p k c", k=KF)
                                last = T.matmul(bank[2 + hf][g * TILE:(g + 1) * TILE, :], hidT[:, k, g * TILE:(g + 1) * TILE],
                                                w[:, k, hf * 512:(hf + 1) * 512], start=(k == 0), stop=(k == KF - 1))
                    last.then_inc(y_full[l], 1)
                    pe.wait_ge(y_act[l], b + 1)
                    pe.wait_ge(y_dve[l], b + 1)
                    for t in range(NT):
                        for hf in range(2):
                            last = T.matmul(bank[4 + 2 * t + hf][:], combT[:, t, :], yb[:, hf * 512:(hf + 1) * 512],
                                            start=first, stop=True, skip_group_check=True)
                    last.then_inc(added[l], 1)

                gather(0)
                batch(0, True)
                pe.wait_ge(list_ready, l + 1)
                nb = pe.value_load(nb_i[0:1, 0:1], min_val=OWN, max_val=MAXB)
                with pe.Fori(1, nb) as b:
                    batch(b, False)

            mixer(0)
            moe(0)
            mixer(1)
            moe(1)

        @block.scalar
        def _(act):
            A = nc.scalar
            chain = Chain(act, act_chain)
            n_a, unit, n_act, n_sq, job = [0], [0], [0], [0], [0]
            A.preload_act_table_set("natural_log_exp_and_others")

            def col(v):
                return v.rearrange("(p k) -> p k", k=KD)

            def up(v):
                return v.rearrange("a d -> d a")
            loads = [
                (g_col[:, 0, :], col(ev_norm[0])),
                (sink[:], ev_sink.broadcast_to([P, 8])),
                (g_col[:, 1, :], col(moe_norm[0])), (g_col[:, 2, :], col(od_norm[0])), (g_col[:, 3, :], col(moe_norm[1])),
                (w_gd[:], od_w_in[0, :, OD_UNITS * UC:].rearrange("(p k) n -> p k n", k=KD)),
            ]
            for l in range(2):
                loads += [(w_rt[:, l, :, 0:NG], moe_w_grp[l].rearrange("(p k) n -> p k n", k=KD)),
                          (w_rt[:, l, :, NG:], moe_w_exp[l].rearrange("(p k) n -> p k n", k=KD)),
                          (b_rt[:, l, 0:NG], moe_b_grp[l:l + 1].broadcast_to([P, NG])),
                          (b_rt[:, l, NG:], moe_b_exp[l:l + 1].broadcast_to([P, NE])),
                          (pos_in[:, l, :].rearrange("l (h d) -> l h d", h=2),
                           od_cmp_pos[0, l].rearrange("(h l) d -> l h d", h=2))]
            for half in range(2):
                r = slice(half * DH, half * DH + DH)
                loads += [(qk_g[r, 0:1], up(ev_q_norm)), (qk_g[r, 1:2], up(ev_k_norm)),
                          (qk_g[r, 2:3], up(od_c_q_norm)), (qk_g[r, 3:4], up(od_c_k_norm)),
                          (qk_g[r, 4:5], up(od_d_q_norm)), (qk_g[r, 5:8], up(od_d_k_norm[0]))]
            assert len(loads) == N_LOADS
            for dst, src in loads:
                act.dma_start(dst, src, allow_slow_non_contiguous=True).then_inc(consts_landed, 16)


            def rms(n):
                junk = junk_m if n % 2 else stage[0].rearrange("p a b -> p (a b)")
                for t in range(NT):
                    act.wait_ge(*((x_landed, 16 * NT) if n == 0 else (x_ready, NT * (n - 1) + t + 1)))
                    chain(A.activation(junk, xs[:, t, :], ACT.Square, accum_out=ssq[:, t:t + 1]))
                if n == 0:
                    act.wait_ge(consts, N_CONST_A)
                chain(A.activation(lnr[:], ssq[:], ACT.Ln, bias=eps_t[:], scale=1.0 / D))
                A.activation(rstd[:], lnr[:], ACT.Exp, scale=-0.5).then_inc(rstd_ready, 1)

            def drain_a(dst, scale=None, cols=512, rows=P, split=1):
                n_a[0] += 1
                act.wait_ge(ta_full, n_a[0])
                w = cols // split
                for i in range(split):
                    src = bank[2][0:rows, i * w:(i + 1) * w]
                    s = scale[i] if isinstance(scale, list) else scale
                    d = dst[i] if split > 1 else dst
                    if s is None:
                        last = A.copy(d, src)
                    else:
                        last = A.mul(d, src, s)
                last.then_inc(ta_free, 1)

            def norm_drain(n):
                if n == 0:
                    act.wait_ge(consts, N_CONST)
                for b in (0, 2):
                    drain_a([hT[:, 2 * b + kk, :] for kk in range(2)],
                            [g_col[:, n, 2 * b + kk:2 * b + kk + 1] for kk in range(2)], split=2)

            def squares(normed):
                n_sq[0] += 1
                n = n_sq[0]
                if n > 1:
                    act.wait_ge(ms_ready, n - 1)
                w = normed * DH
                b = bank[unit[0] % 2][:].rearrange("p (t c) -> p t c", t=NT)
                A.activation(sq[:, :, 0:normed, :].rearrange("p t h d -> p t (h d)"), b[:, :, 0:w],
                             ACT.Square).then_inc(sq_ready, 1)
                act.wait_ge(ms_ready, n)
                chain(A.activation(lq[:, :, 0:normed], red[:, :, 0:normed], ACT.Ln, bias=eps_t[:], scale=1.0 / DH))
                A.activation(rq[:, :, 0:normed], lq[:, :, 0:normed], ACT.Exp, scale=-0.5).then_inc(rq_ready, 1)

            def step(jobs, i, first):
                if i < len(jobs) and jobs[i][0] == "B":
                    n, b = i - 8, i % 2
                    act.wait_ge(sc_free, first + i + 1)
                    if n >= 2:
                        act.wait_ge(suffix_ready, n - 1)
                    chain(A.activation(ea[b], s_sb[b], ACT.Abs))
                    chain(A.activation(ea[b], ea[b], ACT.Exp, scale=-1.0))
                    A.activation(ea[b], ea[b], ACT.Ln, bias=one_t[:]).then_inc(ln_ready, 1)
                elif i < len(jobs):
                    n = first + i
                    act.wait_ge(nm_ready, NMN[n])
                    if n >= 3:
                        act.wait_ge(pt_full, n - 2)
                    for q, (a, b) in enumerate(((0, P), (P, SC))):
                        A.activation(p_sb[n % 3][:, a:b], s_sb[n % 2][:, a:b], ACT.Exp, bias=nm[:, i, q:q + 1],
                                     accum_out=den[:, i, q:q + 1]).then_inc(p_ready, 1)
                if 0 <= i - 1 < len(jobs) and jobs[i - 1][0] == "B":
                    n = first + i - 1
                    act.wait_ge(arg_ready, i - 1 - 8 + 1)
                    act.wait_ge(pt_full, n - 2)
                    A.activation(p_sb[n % 3], la[n % 2], ACT.Exp).then_inc(p_ready, 1)
                if first == 0 and i in (4, 8):
                    act.wait_ge(es_in, i)
                    A.activation(es[:, i - 4:i, :], es[:, i - 4:i, :], ACT.Exp).then_inc(es_out, 1)

            def drain_cmp(k):
                if k == "pos":
                    drain_a(posT.rearrange("p w l -> p (w l)"), cols=2 * NCMP)
                elif k == "compress":
                    act.wait_ge(cmp_full, CF_COMPRESSED)
                    A.copy(vc[0:32, :], bank[1][0:32, 0:DH]).then_inc(cmp_act, 1)
                    chain(A.activation(kc_n[0:32, :], bank[0][0:32, 0:DH], ACT.Square, accum_out=csm[0:32, 0:1]))
                    chain(A.activation(csm[0:32, 1:2], csm[0:32, 0:1], ACT.Ln, bias=eps_t[0:32, :], scale=1.0 / DH))
                    A.activation(csm[0:32, 2:3], csm[0:32, 1:2], ACT.Exp, scale=-0.5).then_inc(cmp_act, 1)
                elif k == "keys":
                    drain_a(kcT[:], qk_g[:, 5:6], cols=32)
                elif k == "scores":
                    act.wait_ge(cmp_dve, CD_ARG)
                    A.activation(cs, cs, ACT.Exp).then_inc(cmp_act, 1)
                elif k == "p":
                    drain_a(pcT.rearrange("p t q -> p (t q)"), cols=NT * P)

            def mixer(layer):
                rms(2 * layer)
                norm_drain(2 * layer)
                if layer:
                    act.wait_ge(gate_full, 1)
                    v = bank[7][:, 0:64].rearrange("p (t c) -> p t c", t=NT)[:, :, 0:GATES]
                    A.activation(gates.rearrange("p t h c -> p t (h c)"), v, ACT.Exp, scale=-1.0).then_inc(gate_exp, 1)
                first = layer * len(JOBS[0])
                for what, *arg in ORDER[layer]:
                    if what == "unit":
                        act.wait_ge(pr_full, unit[0] + 1)
                        if arg[1] == "dve":
                            squares(arg[2])
                        else:
                            dst = DST[layer][arg[0]]
                            if arg[0] in (5, 6) and layer == 0:
                                act.wait_ge(ta_full, T_QA_A)
                                act.wait_ge(tb_full, T_QA_B)
                            v = bank[unit[0] % 2][:]
                            if dst is None:
                                v = v.rearrange("p (t h d) -> p t h d", t=NT, h=4)
                                A.copy(cin[:, :, :, 0, :], v)
                                A.copy(cin[:, :, :, 1, :], v).then_inc(pr_act, 1)
                            else:
                                A.copy(dst, v.rearrange("p (t c) -> p t c", t=NT)).then_inc(pr_act, 1)
                        unit[0] += 1
                    elif what == "turn":
                        src, which, who, count = TURNS[arg[0]]
                        dst, scale = TDST[arg[0]]
                        if src < 2:
                            drain_a(dst[:, 0:2, :].rearrange("p a b -> p (a b)"), scale)
                        elif which == "a":
                            drain_a(dst, scale, cols=S)
                    elif what == "cmp":
                        drain_cmp(arg[0])
                    elif what == "steps":
                        for i in range(arg[0], arg[1]):
                            step(JOBS[layer], i, first)
                for b in (0, 2):
                    drain_a(oT[:, 2 * b:2 * b + 2, :].rearrange("p a b -> p (a b)"))

            def moe(l):
                rms(2 * l + 1)
                norm_drain(2 * l + 1)
                act.wait_ge(rt_gs, l + 1)
                A.activation(ge, ge, ACT.Exp).then_inc(rt_ge, 1)
                act.wait_ge(rt_ws, l + 1)
                A.activation(we, we, ACT.Exp).then_inc(rt_we, 1)

                def batch(b):
                    act.wait_ge(gu_full[l], b + 1)
                    A.activation(en, bank[0][:, 0:FF], ACT.Exp, scale=-1.0).then_inc(en_ready[l], 1)
                    act.wait_ge(ct_full[l], b + 1)
                    A.copy(combT.rearrange("p t q -> p (t q)"), bank[1][:, 2 * P:4 * P]).then_inc(ct_ready[l], 1)
                    act.wait_ge(ht_full[l], b + 1)
                    A.copy(hidT.rearrange("p k q -> p (k q)"), bank[1][:, 0:2 * P]).then_inc(ht_ready[l], 1)
                    act.wait_ge(y_full[l], b + 1)
                    A.copy(yb[:, 0:512], bank[2][:]).then_inc(y_act[l], 1)

                batch(0)
                act.wait_ge(list_ready, l + 1)
                nb = act.value_load(nb_i[0:1, 0:1], min_val=OWN, max_val=MAXB)
                with act.Fori(1, nb) as b:
                    batch(b)

            mixer(0)
            moe(0)
            mixer(1)
            moe(1)

        @block.vector
        def _(dve):
            V = nc.vector
            chain = Chain(dve, dve_chain)
            n_b, unit, n_sq = [0], [0], [0]

            def normed(n):
                dve.wait_ge(rstd_ready, n + 1)
                for t in range(NT):
                    V.tensor_scalar(xn[:, t, :], xs[:, t, :], rstd[:, t:t + 1], None, ALU.mult).then_inc(xn_ready, 1)

            def drain_b(dst, scale=None, cols=512, split=1):
                n_b[0] += 1
                dve.wait_ge(tb_full, n_b[0])
                w = cols // split
                for i in range(split):
                    src = bank[3][:, i * w:(i + 1) * w]
                    s = scale[i] if isinstance(scale, list) else scale
                    d = dst[i] if split > 1 else dst
                    if s is None:
                        last = V.tensor_copy(d, src)
                    else:
                        last = V.tensor_scalar(d, src, s, None, ALU.mult)
                last.then_inc(tb_free, 1)

            def norm_drain(n):
                for b in (1, 3):
                    drain_b([hT[:, 2 * b + kk, :] for kk in range(2)],
                            [g_col[:, n, 2 * b + kk:2 * b + kk + 1] for kk in range(2)], split=2)

            def normed_unit(layer, u, heads):
                n_sq[0] += 1
                n = n_sq[0]
                dve.wait_ge(sq_ready, n)
                V.tensor_reduce(red[:, :, 0:heads], sq[:, :, 0:heads, :], AX, ALU.add).then_inc(ms_ready, 1)
                b = bank[unit[0] % 2][:].rearrange("p (t h d) -> p t h d", t=NT, h=4)
                dst, rest = DST[layer][u]
                if layer == 1 and u in (6, 7):
                    dve.wait_ge(ta_full, T_QC_A)
                    dve.wait_ge(tb_full, T_QC_B)
                if heads < 4:
                    V.tensor_copy(rest, bank[unit[0] % 2][:].rearrange("p (t c) -> p t c", t=NT)[:, :, heads * DH:])
                dve.wait_ge(rq_ready, n)
                V.tensor_tensor(dst, b[:, :, 0:heads, :], rq[:, :, 0:heads].unsqueeze(3).broadcast_to([P, NT, heads, DH]),
                                ALU.mult).then_inc(pr_dve, 1)

            def step(jobs, i, layer):
                first = layer * len(JOBS[0])
                if i < len(jobs):
                    kind, h = jobs[i]
                    n = first + i
                    dve.wait_ge(sc_full, n + 1)
                    if n >= 2:
                        dve.wait_ge(p_ready, PR[n - 2])
                    b = bank[4 + n % 2]
                    if kind == "B":
                        V.tensor_tensor(s_sb[n % 2], b[:, 0:SC], smask, ALU.add).then_inc(sc_free, 1)
                    else:
                        V.tensor_tensor_reduce(s_sb[n % 2][:, 0:P], b[:, 0:P], btab[:, h, 0:P], 1.0, 3 * NEG,
                                               ALU.add, ALU.max, mx[:, i, 0:1])
                        V.tensor_tensor_reduce(s_sb[n % 2][:, P:SC], b[:, P:SC], btab[:, h, P:SC], 1.0, 3 * NEG,
                                               ALU.add, ALU.max, mx[:, i, 1:2]).then_inc(sc_free, 1)
                        dve.wait_ge(sc_free, n + 1)
                        if kind == "A":
                            V.tensor_scalar(nm[:, i, :], mx[:, i, :], sink[:, h:h + 1], -1.0,
                                            ALU.max, ALU.mult).then_inc(nm_ready, 1)
                            dve.wait_ge(nm_ready, NMN[n])
                            V.tensor_scalar(es[:, h, :], nm[:, i, :], sink[:, h:h + 1], None, ALU.add).then_inc(es_in, 1)
                        else:
                            V.tensor_scalar(nm[:, i, :], mx[:, i, :], -1.0, None, ALU.mult).then_inc(nm_ready, 1)
                if 0 <= i - 1 < len(jobs) and jobs[i - 1][0] == "B":
                    m, b = i - 1 - 8, (i - 1) % 2
                    dve.wait_ge(ln_ready, m + 1)
                    chain(V.scalar_tensor_tensor(out=la[b], in0=s_sb[b], scalar=0.0, in1=ea[b], op0=ALU.max, op1=ALU.add))
                    V.tensor_tensor_scan(cu[b][:, ::-1], sreset[:, ::-1], la[b][:, ::-1], 0.0,
                                         ALU.mult, ALU.add).then_inc(suffix_ready, 1)
                if 0 <= i - 2 < len(jobs):
                    n = first + i - 2
                    dve.wait_ge(pt_full, n + 1)
                    if n >= 2:
                        dve.wait_ge(o_full, n - 1)
                    V.tensor_copy(pT[n % 2], bank[6][:, 0:SC]).then_inc(pt_ready, 1)
                if 0 <= i - SKEW < len(jobs) and (i - SKEW) % 4 == 3:
                    heads_out(jobs, i - SKEW - 3, layer)

            def heads_out(jobs, i, layer):
                n = layer * len(JOBS[0]) + i
                kind, h = jobs[i]
                c0 = (512 if kind in "BLW" else 0) + h * DH
                dst = o_sb[:, :, c0:c0 + 4 * DH].rearrange("p t (h d) -> p h t d", h=4)
                v = bank[7][:].rearrange("p (h t d) -> p h t d", h=4, t=NT)
                if kind == "B":
                    dve.wait_ge(o_full, n + 4)
                    V.tensor_copy(dst, v).then_inc(o_ready, 1)
                    return
                dve.wait_ge(p_ready, PR[n + 3])
                d, c = den[:, i:i + 4, :], cf[:, 0:4, :]
                if kind == "A":
                    dve.wait_ge(es_out, h // 4 + 1)
                    chain(V.tensor_tensor(d, d, es[:, h:h + 4, :], ALU.add))
                chain(V.reciprocal(c, d))
                if kind in "LW":
                    gt = gates.rearrange("p t h c -> p h t c")[:, h:h + 4, :, 1 if kind == "L" else 2]
                    chain(V.tensor_tensor(c, c, gt, ALU.mult))
                dve.wait_ge(o_full, n + 4)
                c = c.unsqueeze(3).broadcast_to([P, 4, NT, DH])
                if kind in "LW":
                    o4 = otmp.rearrange("p t (h d) -> p h t d", h=4)
                    chain(V.tensor_tensor(o4, v, c, ALU.mult))
                    full = o_sb[:, :, c0:c0 + 4 * DH]
                    V.tensor_tensor(full, full, otmp, ALU.add).then_inc(o_ready, 1)
                else:
                    V.tensor_tensor(dst, v, c, ALU.mult).then_inc(o_ready, 1)

            def cmp_stage(k):
                if k == "in":
                    dve.wait_ge(cmp_full, 1)
                    dve.wait_ge(ta_free, T_POS)
                    for c in range(2):
                        lo = bank[c][0:DH, :].rearrange("p (m l) -> p m l", l=CSTEP)
                        V.tensor_tensor(t2[c][0:DH].rearrange("p h (n l) -> p (h n) l", l=CSTEP), lo,
                                        posT[0:DH, c, :].unsqueeze(1).broadcast_to([DH, 32, CSTEP]), ALU.add)
                        hi = bank[c][DH:P, :].rearrange("p (h n l) -> p h n l", h=2, l=CSTEP)[:, :, 1:, :]
                        dst = t2[c][DH:P].rearrange("p h (n l) -> p h n l", l=CSTEP)
                        V.tensor_tensor(dst[:, :, 0:NCMP - 1, :], hi,
                                        posT[DH:P, c, :].unsqueeze(1).unsqueeze(1).broadcast_to([DH, 2, NCMP - 1, CSTEP]),
                                        ALU.add)
                        last = V.memset(dst[:, :, NCMP - 1, :], 0.0)
                    last.then_inc(cmp_dve, 1)
                elif k == "compress":
                    dve.wait_ge(cmp_act, 2)
                    dve.wait_ge(tables, 2)
                    chain(V.tensor_scalar(kc_n[0:32, :], bank[0][0:32, 0:DH], csm[0:32, 2:3], None, ALU.mult))
                    V.tensor_tensor(kc_b[0:32], kc_n[0:32].unsqueeze(1).broadcast_to([32, 2, DH]),
                                    blk[0:32, 0:2].unsqueeze(2).broadcast_to([32, 2, DH]), ALU.mult).then_inc(cmp_dve, 1)
                elif k == "keys":
                    dve.wait_ge(cmp_full, 3)
                    V.tensor_tensor(v_blk, bank[1][:, 0:DH].unsqueeze(1).broadcast_to([P, 8, DH]),
                                    blk.unsqueeze(2).broadcast_to([P, 8, DH]), ALU.mult).then_inc(cmp_dve, 1)
                elif k == "scores":
                    dve.wait_ge(cmp_full, 4)
                    c3 = cs.rearrange("p t a b n -> p (t a b) n")
                    bc = [P, NT * 8, NCMP]
                    flat = [v.rearrange("p t h -> p (t h)") for v in (cmx, cden, cz, ccf)]
                    chain(V.tensor_tensor(cs.rearrange("p t a b n -> p (t a b n)"), bank[0][:, 0:NT * P],
                                          ctab.rearrange("p t a b n -> p (t a b n)"), ALU.add))
                    chain(V.tensor_reduce(flat[0], c3, AX, ALU.max))
                    V.tensor_tensor(c3, c3, flat[0].unsqueeze(2).broadcast_to(bc), ALU.subtract).then_inc(cmp_dve, 1)
                    dve.wait_ge(cmp_act, 3)
                    V.tensor_tensor(c3, c3, cmask.rearrange("p t a b n -> p (t a b) n"), ALU.mult).then_inc(cmp_dve, 1)
                    dve.wait_ge(cmp_dve, CD_P)
                    chain(V.tensor_reduce(flat[1], c3, AX, ALU.add))
                    chain(V.tensor_scalar(flat[2], flat[1], 0.0, None, ALU.is_equal))
                    chain(V.tensor_tensor(flat[1], flat[1], flat[2], ALU.add))
                    chain(V.reciprocal(flat[3], flat[1]))
                    gt = gates[:, :, :, 0].rearrange("p t (b a) -> p t a b", b=2)
                    v = ccf.rearrange("p t (a b) -> p t a b", a=4)
                    chain(V.tensor_tensor(v, v, gt, ALU.mult))
                elif k == "values":
                    dve.wait_ge(cmp_full, 5)
                    for t in range(NT):
                        dst = o_sb[:, t, 512:].rearrange("p (b a e) -> p a b e", b=2, a=4)
                        last = V.tensor_tensor(dst, bank[t][:].rearrange("p (a b e) -> p a b e", a=4, b=2),
                                               ccf[:, t, :].rearrange("p (a b) -> p a b", a=4).unsqueeze(3)
                                               .broadcast_to([P, 4, 2, DH]), ALU.mult)
                    chain(last)

            def add_out(event):
                for t in range(NT):
                    for hf in range(2):
                        v = xs[:, t, hf * 512:(hf + 1) * 512]
                        last = V.tensor_tensor(v, v, bank[4 + 2 * t + hf][:], ALU.add)
                    last.then_inc(x_ready, 1)

            def mixer(layer):
                normed(2 * layer)
                if layer == 0:
                    dve.wait_ge(consts_landed, 16 * N_LOADS)
                    dve.wait_ge(consts, N_CONST)
                norm_drain(2 * layer)
                if layer:
                    dve.wait_ge(gate_exp, 1)
                    v = gates.rearrange("p t h c -> p (t h c)")
                    chain(V.tensor_scalar(v, v, 1.0, None, ALU.add))
                    V.reciprocal(v, v).then_inc(gate_ready, 1)
                waited = False
                for what, *arg in ORDER[layer]:
                    if what == "unit":
                        if arg[1] == "dve":
                            normed_unit(layer, arg[0], arg[2])
                        unit[0] += 1
                    elif what == "turn":
                        src, which, who, count = TURNS[arg[0]]
                        dst, scale = TDST[arg[0]]
                        if src < 2:
                            drain_b(dst[:, 2:4, :].rearrange("p a b -> p (a b)"), scale)
                        elif which == "b":
                            drain_b(dst, scale, cols=S)
                    elif what == "cmp":
                        cmp_stage(arg[0])
                    elif what == "steps":
                        if not waited:
                            dve.wait_ge(tables, layer + 1)
                            waited = True
                        for i in range(arg[0], arg[1]):
                            step(JOBS[layer], i, layer)
                for b in (1, 3):
                    drain_b(oT[:, 2 * b:2 * b + 2, :].rearrange("p a b -> p (a b)"))
                dve.wait_ge(wo_used, OUT_UNITS * (layer + 1))
                add_out(2 * layer)

            def first_max(p, width, mxv, eq, idx, oh):
                bc = [P, NT, width]
                iota = iota8[:, :, 0:width]
                chain(V.tensor_reduce(mxv, p, AX, ALU.max))
                chain(V.tensor_tensor(eq, p, mxv.unsqueeze(2).broadcast_to(bc), ALU.is_equal))
                chain(V.scalar_tensor_tensor(out=eq, in0=eq, scalar=-100.0, in1=iota, op0=ALU.mult, op1=ALU.add))
                chain(V.tensor_reduce(idx, eq, AX, ALU.min))
                chain(V.tensor_scalar(idx, idx, 100.0, None, ALU.add))
                chain(V.tensor_tensor(oh, iota, idx.unsqueeze(2).broadcast_to(bc), ALU.is_equal))

            def route(l):
                n36 = NG + NE
                dve.wait_ge(rt_full, 2 * l + 1)
                v = bank[0][:, 0:NT * 64].rearrange("p (t c) -> p t c", t=NT)[:, :, 0:n36]
                chain(V.tensor_tensor(lg, v, b_rt[:, l, :].unsqueeze(1).broadcast_to([P, NT, n36]), ALU.add))
                gl = lg[:, :, 0:NG]
                chain(V.tensor_reduce(r_gm, gl, AX, ALU.max))
                V.tensor_tensor(ge, gl, r_gm.unsqueeze(2).broadcast_to([P, NT, NG]), ALU.subtract).then_inc(rt_gs, 1)
                dve.wait_ge(rt_gs, l + 1)
                first_max(gl, NG, r_gm, g_eq, r_i, g_oh)
                el = lg[:, :, NG:].rearrange("p t (g e) -> p t g e", g=NG)
                w4 = wtmp.rearrange("p t (g e) -> p t g e", g=NG)
                goh = g_oh.unsqueeze(3).broadcast_to([P, NT, NG, EG])
                chain(V.tensor_tensor(w4, el, goh, ALU.mult))
                chain(V.tensor_reduce(we, w4.rearrange("p t g e -> p t e g"), AX, ALU.add))
                chain(V.tensor_reduce(r_wm, we, AX, ALU.max))
                V.tensor_tensor(we, we, r_wm.unsqueeze(2).broadcast_to([P, NT, EG]), ALU.subtract).then_inc(rt_ws, 1)
                dve.wait_ge(rt_ge, l + 1)
                chain(V.tensor_reduce(r_pg, ge, AX, ALU.add))
                chain(V.reciprocal(r_pg, r_pg))
                dve.wait_ge(rt_we, l + 1)
                chain(V.tensor_reduce(r_ws, we, AX, ALU.add))
                chain(V.reciprocal(r_ws, r_ws))
                bc8 = [P, NT, EG]
                chain(V.tensor_tensor(we, we, r_ws.unsqueeze(2).broadcast_to(bc8), ALU.mult))
                first_max(we, EG, r_m1, e_eq, r_i, oh1)
                chain(V.scalar_tensor_tensor(out=we, in0=oh1, scalar=-2.0, in1=we, op0=ALU.mult, op1=ALU.add))
                first_max(we, EG, r_m2, e_eq, r_i, oh2)
                for oh, f in ((oh1, f1), (oh2, f2)):
                    chain(V.tensor_tensor(f.rearrange("p t (g e) -> p t g e", g=NG), goh,
                                          oh.unsqueeze(2).broadcast_to([P, NT, NG, EG]), ALU.mult))
                V.tensor_tensor(mask, f1, f2, ALU.add).then_inc(rt_mask, 1)
                chain(V.tensor_tensor(r_s, r_m1, r_m2, ALU.add))
                chain(V.reciprocal(r_s, r_s))
                chain(V.tensor_tensor(r_s, r_s, r_pg, ALU.mult))
                chain(V.tensor_tensor(r_m1, r_m1, r_s, ALU.mult))
                chain(V.tensor_tensor(r_m2, r_m2, r_s, ALU.mult))
                dve.wait_ge(rt_full, 2 * l + 2)
                n7 = S // TILE - 1
                chain(V.tensor_copy(cnt, bank[1][:, 2 * NE:3 * NE]))
                chain(V.tensor_tensor(cmp7, cnt.unsqueeze(2).broadcast_to([P, NE, n7]),
                                      steps7[:].unsqueeze(1).broadcast_to([P, NE, n7]), ALU.is_gt))
                chain(V.tensor_reduce(tov, cmp7, AX, ALU.add))
                chain(V.tensor_tensor_scan(vin, ones[:, 0:NE], tov, 0.0, ALU.mult, ALU.add))
                chain(V.tensor_tensor(vex, vin, tov, ALU.subtract))
                chain(V.scalar_tensor_tensor(out=dq, in0=vex, scalar=float(TILE), in1=first_q[:],
                                             op0=ALU.mult, op1=ALU.subtract))
                chain(V.tensor_scalar(dq, dq, float(NE * TILE - TILE), None, ALU.add))
                bc = [P, NT, NE]
                rank = bank[1][:, 0:2 * NE].rearrange("p (t e) -> p t e", t=NT)
                chain(V.tensor_scalar(over, rank, float(TILE), None, ALU.is_ge))
                chain(V.tensor_tensor(over, over, dq.unsqueeze(1).broadcast_to(bc), ALU.mult))
                chain(V.tensor_tensor(qe, rank, first_q[:].unsqueeze(1).broadcast_to(bc), ALU.add))
                chain(V.tensor_tensor(qe, qe, over, ALU.add))
                chain(V.tensor_tensor(f1, f1, qe, ALU.mult))
                chain(V.tensor_tensor(f2, f2, qe, ALU.mult))
                chain(V.tensor_reduce(r_q1, f1, AX, ALU.add))
                chain(V.tensor_reduce(r_q2, f2, AX, ALU.add))
                dve.sem_inc(q_ready[l], 1)

            def batch_list():
                bc = [P, MAXOVER, NE]

                def row(v):
                    return v.unsqueeze(1).broadcast_to(bc)
                j = iota_j[:].unsqueeze(2).broadcast_to(bc)
                chain(V.tensor_tensor(ov[0], j, row(vex), ALU.is_ge))
                chain(V.tensor_tensor(ov[1], j, row(vin), ALU.is_lt))
                chain(V.tensor_tensor(ov[2], ov[0], ov[1], ALU.mult))
                chain(V.tensor_tensor(ov[0], ov[2], row(iota_e[:]), ALU.mult))
                chain(V.tensor_reduce(ovr, ov[0], AX, ALU.add))
                chain(V.tensor_copy(ove_i[:], ovr))
                chain(V.tensor_tensor(nb_f, vin[:, NE - 1:NE].broadcast_to([P, GROUPS]),
                                      iota_j[:, 0:MAXOVER:GROUPS], ALU.is_gt))
                chain(V.tensor_reduce(nb_s, nb_f, AX, ALU.add))
                V.tensor_scalar(nb_i[:], nb_s, float(OWN), None, ALU.add).then_inc(list_ready, 1)

            def moe(l):
                normed(2 * l + 1)
                norm_drain(2 * l + 1)
                route(l)

                def onehots(b, ch):
                    for t in range(NT):
                        ch(V.tensor_scalar(ctmp[:, t, :], iota_s[:], r_q2[:, t:t + 1], None, ALU.is_equal))
                        last = V.scalar_tensor_tensor(out=oneh[:, t, :], in0=iota_s[:], scalar=r_q1[:, t:t + 1],
                                                      in1=ctmp[:, t, :], op0=ALU.is_equal, op1=ALU.add)
                    last.then_inc(b_ready[l], 1)
                    dve.wait_ge(b_ready[l], b + 1)
                    ch(V.tensor_scalar(r_q1, r_q1, float(-P), None, ALU.add))
                    ch(V.tensor_scalar(r_q2, r_q2, float(-P), None, ALU.add))

                def inputs(b):
                    dve.wait_ge(ga_full[l], b + 1)
                    for hf in range(2):
                        last = V.tensor_tensor(xt[:, 4 * hf:4 * hf + 4, :], bank[2 + hf][:].rearrange("p (k q) -> p k q", k=4),
                                               g_col[:, 2 * l + 1, 4 * hf:4 * hf + 4].unsqueeze(2).broadcast_to([P, 4, P]),
                                               ALU.mult)
                    last.then_inc(xt_ready[l], 1)

                def batch(b, before):
                    ch = Chain(dve, loop_dve[l], before)
                    dve.wait_ge(ga_full[l], b + 1)
                    onehots(b + 1, ch)
                    dve.wait_ge(en_ready[l], b + 1)
                    ch(V.tensor_scalar(en, en, 1.0, None, ALU.add))
                    ch(V.reciprocal(en, en))
                    ch(V.tensor_tensor(en, en, bank[0][:, 0:FF], ALU.mult))
                    V.tensor_tensor(hid, en, bank[0][:, FF:], ALU.mult).then_inc(hid_ready[l], 1)
                    inputs(b + 1)
                    dve.wait_ge(y_full[l], b + 1)
                    V.tensor_copy(yb[:, 512:], bank[3][:]).then_inc(y_dve[l], 1)
                    return ch.n

                dve.wait_ge(c_copied, l + 1)
                onehots(0, chain)
                inputs(0)
                batch_list()
                per = batch(0, 0)
                nb = dve.value_load(nb_i[0:1, 0:1], min_val=OWN, max_val=MAXB)
                with dve.Fori(1, nb) as b:
                    batch(b, b * per)
                dve.wait_ge(added[l], nb)
                add_out(2 * l + 1)

            mixer(0)
            moe(0)
            mixer(1)
            moe(1)


_INS = ['x', 'ev_norm', 'ev_w_in', 'ev_q_norm', 'ev_k_norm', 'ev_sink', 'ev_w_out',
        'od_norm', 'od_w_in', 'od_c_q_norm', 'od_c_k_norm', 'od_d_q_norm', 'od_d_k_norm',
        'od_cmp_pos', 'od_cmp_w', 'od_w_out',
        'moe_norm', 'moe_w_grp', 'moe_b_grp', 'moe_w_exp', 'moe_b_exp', 'moe_w_gate', 'moe_w_up', 'moe_w_down']
_OUTS = [((1, S, D), 'float32')]


def kernel(**inputs):
    import numpy as _np
    import concourse.bacc as _bacc
    from concourse import mybir as _mybir
    from concourse.bass_utils import run_bass_kernel_spmd as _run

    nc = _bacc.Bacc("TRN2", target_bir_lowering=False, num_devices=1)
    arrays, args = {}, []
    for name in _INS:
        a = _np.ascontiguousarray(inputs[name])
        arrays[f"in_{name}_dram"] = a
        args.append(nc.dram_tensor(f"in_{name}_dram", a.shape, _mybir.dt.from_np(a.dtype), kind="ExternalInput").ap())
    for i, (shape, dtype) in enumerate(_OUTS):
        dt = _mybir.dt.from_np(_np.dtype(dtype))
        args.append(nc.dram_tensor(f"out_{i}_dram", shape, dt, kind="ExternalOutput").ap())
    program(nc, *args)
    r = _run(nc, [arrays], core_ids=[0])
    got = tuple(r.results[0][f"out_{i}_dram"] for i in range(len(_OUTS)))
    return got[0]
```

```python
from contextlib import ExitStack

import concourse.bass as bass
from concourse import mybir

P = 128
S = 256
NT = S // P
D = 1024
KD = D // P
DH = 64
EV_IN = 2304
OD_IN = 2840
NG, EG, NE, FF = 4, 8, 32, 256
KF = FF // P
UNIT = 2048
UC = UNIT // KD
RING = 12
PER_EXPERT = 3
GROUPS = 4
BATCH = GROUPS * PER_EXPERT
EV_UNITS = EV_IN // UC
OD_UNITS = OD_IN // UC
OUT_UNITS = D * D // (P * UNIT)
GATES = OD_IN - OD_UNITS * UC
TILE = P // GROUPS
OWN = NE // GROUPS
MAXOVER = 16
MAXB = OWN + MAXOVER // GROUPS
EPS = 1e-6
NEG = -1e30
SC = P + S
NCMP = 16
WIN, CSTEP, CLEN = 128, 16, 32

F32 = mybir.dt.float32
I32 = mybir.dt.int32
BF16 = mybir.dt.bfloat16
ALU = mybir.AluOpType
ACT = mybir.ActivationFunctionType
AX = mybir.AxisListType.X

U_EV_IN = 0
U_EV_OUT = U_EV_IN + EV_UNITS
U_MOE0 = U_EV_OUT + OUT_UNITS + 1
U_OD_IN = U_MOE0 + PER_EXPERT * NE
U_CMP = U_OD_IN + OD_UNITS
U_OD_OUT = U_CMP + 1
U_MOE1 = U_OD_OUT + OUT_UNITS
U_END = U_MOE1 + PER_EXPERT * NE
U_MOE = (U_MOE0, U_MOE1)
SIDE = (0, 1, 2 * GROUPS)

SLOPES = [2.0 ** -(h + 1) for h in range(8)]


def even_jobs():
    return [("A", h) for h in range(8)] + [("B", h) for h in range(8)]


def odd_jobs():
    jobs = [("C", h) for h in range(8)]
    for h in (0, 4):
        jobs += [("L", h + i) for i in range(4)] + [("W", h + i) for i in range(4)]
    return jobs


JOBS = (even_jobs(), odd_jobs())


def out_steps(i0, i1, tiles):
    return [("steps", i, i + 1, tiles.get(i)) for i in range(i0, i1)]


ORDER = (
    [("unit", 0, "dve", 4), ("unit", 1, "dve", 4), ("unit", 2, "dve", 2), ("turn", "qa"),
     ("unit", 3, "act"), ("turn", "ka"), ("steps", 0, 2), ("unit", 4, "act"), ("steps", 2, 4),
     ("unit", 5, "act"), ("turn", "qb"), ("steps", 4, 6), ("unit", 6, "act"), ("steps", 6, 7),
     ("unit", 7, "act"), ("turn", "kb"), ("steps", 7, 9), ("unit", 8, "act"), ("steps", 9, 11)] +
    out_steps(11, 19, {11: 0, 12: 1, 13: 2, 14: 3, 16: 4, 17: 5}),
    [("unit", 0, "dve", 4), ("unit", 1, "dve", 4), ("unit", 2, "dve", 4), ("turn", "qc"),
     ("unit", 3, "dve", 4), ("unit", 4, "act"), ("turn", "kc"), ("steps", 0, 1), ("unit", 5, "act"),
     ("steps", 1, 3), ("unit", 6, "dve", 4), ("steps", 3, 5), ("unit", 7, "dve", 4), ("steps", 5, 6),
     ("unit", 8, "act"), ("turn", "qd"), ("steps", 6, 8), ("unit", 9, "dve", 2), ("unit", 10, "dve", 2),
     ("cmp", "pos"), ("turn", "ks"), ("turn", "kw"), ("cmp", "in"), ("steps", 8, 9), ("cmp", "compress"),
     ("steps", 9, 10), ("cmp", "keys"), ("steps", 10, 11), ("cmp", "scores"), ("steps", 11, 12),
     ("cmp", "norm"), ("steps", 12, 13), ("cmp", "p"), ("steps", 13, 14)] + out_steps(14, 27, {14: 0, 16: 1, 18: 2, 20: 3, 21: 4, 23: 5}))


def drained_late(order):
    late = []
    for i, what in enumerate(order):
        if what[0] == "steps" and order[i - 1][0] == "unit":
            late.insert(-1, what)
        else:
            late.append(what)
    return late


DRAIN_ORDER = tuple(drained_late(order) for order in ORDER)


def turns_before(name):
    a = b = 0
    for layer in range(2):
        a, b = a + 2, b + 2
        for what, *arg in ORDER[layer]:
            if what == "turn" or what == "cmp" and arg[0] in ("pos", "keys", "p"):
                both = arg[0] in ("qa", "qb", "kb", "qc", "kc", "qd")
                a += both or arg[0] in ("ks", "pos", "keys", "p")
                b += both or arg[0] in ("ka", "kw")
                if arg[0] == name:
                    return a, b
        a, b = a + 2, b + 2


T_QA_A, T_QA_B = turns_before("qa")
T_QC_A, T_QC_B = turns_before("qc")
T_POS = turns_before("pos")[0]
PR, NMN = [], []
for kind, _ in JOBS[0] + JOBS[1]:
    PR.append((PR or [0])[-1] + (1 if kind == "B" else 2))
    NMN.append((NMN or [0])[-1] + (kind != "B"))
V_THERE = {0: ("dve", 3), 8: ("act", 6), 16: ("act", 8), 24: ("dve", 10), 28: ("dve", 11)}


def groups():
    before, first, last = [], [], []
    for kind, h in JOBS[0] + JOBS[1]:
        first.append(h % 4 == 0 and kind != "W")
        before.append(sum(last))
        last.append(h % 4 == 3 and kind != "L")
    return before, first, last


GROUPS_BEFORE, GROUP_FIRST, GROUP_LAST = groups()
N_HEAD_GAINS, N_LATE = 13, 14
N_CONST_A, N_CONST = 5, 15
CF_COMPRESSED = 2
CD_T2, CD_KEYS, CD_ARG, CD_P = 1, 2, 4, 5
WARM_NORM, WARM_CHOICE, WARM_PLACES = (4, 0, 8, 0), 3, 2
SKEW = 3


def program(nc, x, ev_norm, ev_w_in, ev_q_norm, ev_k_norm, ev_sink, ev_w_out,
            od_norm, od_w_in, od_c_q_norm, od_c_k_norm, od_d_q_norm, od_d_k_norm,
            od_cmp_pos, od_cmp_w, od_w_out,
            moe_norm, moe_w_grp, moe_b_grp, moe_w_exp, moe_b_exp, moe_w_gate, moe_w_up, moe_w_down,
            out):
    with ExitStack() as ctx:
        def sb(name, shape, dt=F32):
            return ctx.enter_context(nc.sbuf_tensor(name, shape, dt))

        def sem(name):
            return ctx.enter_context(nc.semaphore(name))

        ring = sb("ring", [P, RING, UNIT])
        xs = sb("x_res", [P, NT, D])
        xn = sb("x_normed", [P, NT, D])
        hT = sb("h_transposed", [P, KD, S])
        oT = xn[:].rearrange("p t d -> p (t d)").rearrange("p (k s) -> p k s", k=KD)
        ident = sb("ident", [P, P])
        before = sb("before", [P, P])
        ones = sb("ones", [P, P])
        iota_s = sb("iota_slots", [P, P])
        iota8 = sb("iota_8", [P, NT, EG])
        iota_e = sb("iota_experts", [P, NE])
        first_q = sb("first_places", [P, NE])
        first_far = sb("first_far_places", [P, NE])
        iota_j = sb("iota_tiles", [P, MAXOVER])
        steps7 = sb("tile_ends", [P, S // TILE - 1])
        g_col = sb("norm_gains", [P, 4, KD])
        w_rt = sb("router_w", [P, 2, KD, NG + NE])
        b_rt = sb("router_b", [P, 2, NG + NE])
        w_gd = sb("gate_w", [P, KD, GATES])
        qk_g = sb("qk_gains", [P, 8])
        sink = sb("sink", [P, 8])
        eps_t = sb("eps", [P, 1])
        one_t = sb("one", [P, 1])
        ssq = sb("ssq", [P, NT])
        lnr = sb("ln_ms", [P, NT])
        rstd = sb("rstd", [P, NT])
        pos_in = sb("pos_rows", [NCMP, 2, P])

        btab = sb("bias", [P, 8, SC], BF16)
        smask = sb("strict_mask", [P, SC], BF16)
        sreset = sb("scan_reset", [P, SC], BF16)
        side_down = sb("side_down", [P, UNIT])

        ARENA = 16450
        arena = sb("arena", [P, ARENA])
        at = [0]

        def carve(*dims):
            n = 1
            for v in dims:
                n *= v
            a = arena[:, at[0]:at[0] + n]
            at[0] += n
            assert at[0] <= ARENA, at[0]
            if len(dims) > 1:
                names = "abcd"[:len(dims)]
                a = a.rearrange(f"p ({' '.join(names)}) -> p {' '.join(names)}", **dict(zip(names, dims)))
            return a

        kept_qT = carve(4, S)
        kT = carve(4, S)
        kTp = [carve(S) for _ in range(2)]
        vbig = carve(NT, 512)
        vsm = [carve(NT, 128) for _ in range(2)]
        red = carve(NT, 4)
        lq = carve(NT, 4)
        rq = carve(NT, 4)
        s_sb = [carve(SC) for _ in range(3)]
        mark = at[0]
        ea = [carve(SC) for _ in range(2)]
        la = [carve(SC) for _ in range(2)]
        cu = [carve(SC) for _ in range(2)]
        end, at[0] = at[0], mark
        t2 = [carve(2, S) for _ in range(2)]
        cin = carve(NT, 4, 2, DH)
        v_blk = carve(8, DH)
        at[0] = max(at[0], end)
        p_sb = [carve(SC) for _ in range(3)]
        pT = [carve(SC) for _ in range(3)]
        mx = carve(24, 2)
        nm = carve(24, 2)
        den = carve(24, 2)
        es = carve(8, 2)
        cf = carve(24, 2)
        posT = carve(2, NCMP)
        kc_n = carve(DH)
        vc = carve(DH)
        spread = carve(4, 32)
        kc_b = carve(2, DH)
        kcT = carve(32)
        ctab = carve(NT, 4, 2, NCMP)
        cmask = carve(NT, 4, 2, NCMP)
        cs = carve(NT, 4, 2, NCMP)
        cmx = carve(NT, 8)
        cden = carve(NT, 8)
        cz = carve(NT, 8)
        ccf = carve(NT, 8)
        pcT = carve(NT, P)
        blk = carve(8)
        csm = carve(4)
        gates = carve(NT, 8, 3)
        side_pair = arena[:, at[0]:at[0] + 2 * UNIT].rearrange("p (u w) -> p u w", u=2)
        side_at = at[0]
        stage = [carve(NT, 512) for _ in range(2)]
        stk = [carve(NT, 128) for _ in range(2)]
        sq = carve(NT, 4, DH)
        qT = [carve(4, S), kept_qT]
        assert at[0] - side_at == 2 * UNIT

        at[0] = 0
        junk_m = carve(D)
        xt = carve(KD, P)
        oneh = carve(NT, P)
        comb = carve(NT, P)
        ctmp = carve(NT, P)
        otmp_m = carve(NT, P)
        combT = carve(NT, P)
        en = carve(FF)
        hid = carve(FF)
        hidT = carve(KF, P)
        yb = carve(D)
        lg = carve(NT, NG + NE)
        r_gm, r_i, r_pg, r_ws, r_m1, r_m2, r_s = (carve(NT) for _ in range(7))
        r_q, p_q, places = (carve(2, NT) for _ in range(3))
        ge, g_eq, g_oh = (carve(NT, NG) for _ in range(3))
        we, e_eq, oh1, oh2 = (carve(NT, EG) for _ in range(4))
        mask, wtmp, qe, over = (carve(NT, NE) for _ in range(4))
        f12 = carve(2, NT, NE)
        cnt, tov, vin, vex, dq = (carve(NE) for _ in range(5))
        cmp7 = carve(NE, S // TILE - 1)
        ov = [carve(MAXOVER, NE) for _ in range(3)]
        ovr = carve(MAXOVER)
        nb_f = carve(GROUPS)
        nb_s = carve(1)
        assert at[0] <= side_at
        ove_i = sb("overflow_expert", [P, MAXOVER], I32)
        nb_i = sb("batches", [P, 1], I32)

        bank = [ctx.enter_context(nc.psum_tensor(f"bank{i}", [P, 512], F32)) for i in range(8)]

        landed = [sem(f"unit_landed{i}") for i in range(RING)]
        cmp_landed, x_landed, gains_landed = sem("cmp_landed"), sem("x_landed"), sem("first_gains_landed")
        gains2_landed, late_landed = sem("head_gains_landed"), sem("late_constants_landed")
        consts, tables = sem("consts_built"), sem("tables_built")
        pool_chain, dve_chain, act_chain = sem("pool_chain"), sem("dve_chain"), sem("act_chain")
        rstd_ready, xn_ready, x_ready = sem("rstd_ready"), sem("xn_ready"), sem("x_ready")
        ta_full, ta_free = sem("transposes_a_full"), sem("transposes_a_free")
        tb_full, tb_free = sem("transposes_b_full"), sem("transposes_b_free")
        pr_full, pr_act, pr_dve = sem("proj_full"), sem("proj_drained_act"), sem("proj_drained_dve")
        sq_ready, ms_ready, rq_ready = sem("squares_ready"), sem("head_ms_ready"), sem("head_rstd_ready")
        sc_full, sc_free, nm_ready = sem("scores_full"), sem("scores_masked"), sem("neg_max_ready")
        p_ready, pt_full, pt_ready = sem("p_ready"), sem("pT_full"), sem("pT_ready")
        ps_ready = sem("p_normed")
        ln_ready, suffix_ready, arg_ready = sem("ln_ready"), sem("suffix_ready"), sem("stick_arg_ready")
        o_full, o_ready = sem("o_full"), sem("o_ready")
        es_in, es_out = sem("sink_arg_ready"), sem("sink_exp_ready")
        cmp_full, cmp_dve, cmp_act = sem("cmp_psum_full"), sem("cmp_by_dve"), sem("cmp_by_act")
        gate_full, gate_exp, gate_ready = sem("gate_full"), sem("gate_exp_ready"), sem("gate_ready")
        wo_used, mix_tile = sem("out_proj_units_used"), sem("first_token_tile_projected")
        rt_full, rt_gs, rt_ge = sem("router_psum_full"), sem("group_arg_ready"), sem("group_exp_ready")
        rt_ws, rt_we, rt_mask = sem("expert_arg_ready"), sem("expert_exp_ready"), sem("choice_ready")
        side_landed = sem("side_units_landed")
        list_ready = sem("batch_count_ready")
        moe_landed = [[sem(f"expert_unit_landed{l}_{i}") for i in range(BATCH)] for l in range(2)]

        def two(name):
            return [sem(f"{name}{l}") for l in range(2)]
        added = two("batch_added")
        c_copied, places_moved = sem("places_copied"), sem("places_moved")
        q_ready, b_ready, c_ready = two("places_ready"), two("onehot_ready"), two("weights_ready")
        ga_full, xt_ready = two("gathered"), two("inputs_ready")
        gu_full, en_ready, hid_ready = two("gate_up_full"), two("exp_ready"), two("hidden_ready")
        ct_full, ct_ready = two("weights_turned"), two("weightsT_ready")
        ht_full, ht_ready = two("hidden_turned"), two("hiddenT_ready")
        y_full, y_act, y_dve = two("down_full"), two("y_ready_act"), two("y_ready_dve")
        loop_dve, loop_pool = two("batch_chain_dve"), two("batch_chain_pool")
        ac_full, stored = sem("combined_full"), sem("stored")

        def cols(a, u):
            return a[:, :, u * UC:(u + 1) * UC]

        def by_head(a):
            return a.rearrange("p t (h d) -> p t h d", d=DH)

        def half_pairs(a, u):
            return a.rearrange("p t (a u d) -> p t a u d", a=4, u=2)[:, :, :, u, :]

        DST = ({0: (half_pairs(stage[0], 0), None), 1: (half_pairs(stage[0], 1), None),
                2: (by_head(stk[0]), vsm[0]), 3: cols(stage[1], 0), 4: cols(stage[1], 1),
                5: cols(stage[0], 0), 6: cols(stage[0], 1), 7: cols(vbig, 0), 8: cols(vbig, 1)},
               {0: (by_head(cols(stage[0], 0)), None), 1: (by_head(cols(stage[0], 1)), None),
                2: (by_head(cols(stage[1], 0)), None), 3: (by_head(cols(stage[1], 1)), None),
                4: cols(vbig, 0), 5: cols(vbig, 1),
                6: (half_pairs(stage[0], 0), None), 7: (half_pairs(stage[0], 1), None),
                8: None, 9: (by_head(stk[0]), vsm[0]), 10: (by_head(stk[1]), vsm[1])})
        TURNS = {"qa": (0, None, "dve", 2), "ka": (2, "b", "dve", 3),
                 "qb": (1, None, "act", 2), "kb": (0, None, "act", 4),
                 "qc": (0, None, "dve", 5), "kc": (1, None, "dve", 7),
                 "qd": (0, None, "dve", 9), "ks": (2, "a", "dve", 10), "kw": (3, "b", "dve", 11)}
        TDST = {"qa": (qT[0], qk_g[:, 0:1]), "ka": (kTp[0], qk_g[:, 1:2]), "qb": (qT[1], 0.125), "kb": (kT, None),
                "qc": (qT[0], qk_g[:, 2:3]), "kc": (kT, qk_g[:, 3:4]), "qd": (qT[1], qk_g[:, 4:5]),
                "ks": (kTp[0], qk_g[:, 6:7]), "kw": (kTp[1], qk_g[:, 7:8])}

        def tok(a, k):
            return a.rearrange("q (p k) -> q k p", k=KD)[:, k, :]

        def slot_of(n):
            return n % RING

        def landings(n):
            here = [m for m in range(slot_of(n), n + 1, RING)
                    if m < U_MOE0 - 1 or U_OD_IN <= m < U_MOE1 and m != U_CMP]
            return 16 * len(here)

        def released(n):
            if n < U_EV_OUT:
                return pr_full, n + 1
            if n == U_MOE0 - 1:
                return released(n - RING)
            if n < U_MOE0:
                return wo_used, n - U_EV_OUT + 1
            if n < U_CMP:
                return pr_full, EV_UNITS + n - U_OD_IN + 1
            if n == U_CMP:
                return cmp_full, CF_COMPRESSED
            return wo_used, OUT_UNITS + n - U_OD_OUT + 1

        def seconds(v):
            return v.rearrange("p (h q d) -> p h q d", h=4, q=NT)

        class Chain:
            def __init__(self, eng, s, before=0):
                self.eng, self.s, self.n, self.before = eng, s, 0, before

            def count(self, ins):
                self.n += 1
                ins.then_inc(self.s, 1)

            def wait(self):
                self.eng.wait_ge(self.s, self.before + self.n)

            def __call__(self, ins):
                self.count(ins)
                self.wait()

        block = ctx.enter_context(nc.Block())

        def col(v):
            return v.rearrange("(p k) -> p k", k=KD)

        @block.sync
        def _(sp):
            for t in range(NT):
                sp.dma_start(xs[:, t, :], x[0, t * P:(t + 1) * P, :]).then_inc(x_landed, 16)
            sp.dma_start(g_col[:, 0, :], col(ev_norm[0]), allow_slow_non_contiguous=True).then_inc(gains_landed, 16)

            def load(n, src, shape, after_moe=None):
                if after_moe is not None and n - RING < U_MOE0 + NE * PER_EXPERT:
                    nb = after_moe
                    sp.wait_ge(gu_full[0] if (n - U_MOE0) % RING < 2 * GROUPS else y_full[0], nb)
                elif n >= RING:
                    sp.wait_ge(*released(n - RING))
                dst = ring[:, slot_of(n), :].rearrange("p (a b) -> p a b", a=shape)
                sp.dma_start(dst, src).then_inc(landed[slot_of(n)], 16)

            def head_gains():
                sp.dma_start(sink[:], ev_sink.broadcast_to([P, 8])).then_inc(gains2_landed, 16)
                for half in range(2):
                    r = slice(half * DH, half * DH + DH)
                    for c, v in ((0, ev_q_norm), (1, ev_k_norm), (2, od_c_q_norm), (3, od_c_k_norm),
                                 (4, od_d_q_norm), (5, od_d_k_norm[0])):
                        sp.dma_start(qk_g[r, c:c + v.shape[0]], v.rearrange("a d -> d a"),
                                     allow_slow_non_contiguous=True).then_inc(gains2_landed, 16)

            def proj_units(u0, w, units, after_moe=None):
                wv = w[0].rearrange("(p k) n -> p k n", k=KD)
                for u in range(units):
                    load(u0 + u, wv[:, :, u * UC:(u + 1) * UC], KD, after_moe)
                    if u0 + u == 3:
                        head_gains()

            def out_units(u0, w):
                for u in range(OUT_UNITS):
                    load(u0 + u, w[0, u * 2 * P:(u + 1) * 2 * P, :].rearrange("(k p) n -> p k n", p=P), 2)

            def expert(l, e, c):
                one = bass.ds(l * NE + e, 1)
                if c < 2:
                    w = (moe_w_gate, moe_w_up)[c].rearrange("l e (p k) n -> (l e) p k n", k=KD)
                else:
                    w = moe_w_down.rearrange("l e (k p) n -> (l e) p k n", p=P)
                return w[one].rearrange("o p k n -> p (o k) n")

            def expert_dst(l, i):
                return ring[:, slot_of(U_MOE[l] + i), :].rearrange("p (a b) -> p a b", a=KD if i < 2 * GROUPS else KF)

            def part(i):
                return (i // 2, i % 2) if i < 2 * GROUPS else (i - 2 * GROUPS, 2)

            def moe_units(l):
                beside = False
                for i in range(BATCH):
                    free, count = released(U_MOE[l] + i - RING)
                    if free is wo_used and not beside:
                        sp.wait_ge(wo_used, OUT_UNITS * l + 1)
                        for j, c in enumerate(SIDE):
                            g, which = part(c)
                            dst = side_down[:] if which == 2 else side_pair[:, j, :]
                            sp.dma_start(dst.rearrange("p (a b) -> p a b", a=KF if which == 2 else KD),
                                         expert(l, GROUPS + g, which)).then_inc(side_landed, 16)
                        beside = True
                    sp.wait_ge(free, count)
                    g, c = part(i)
                    sp.dma_start(expert_dst(l, i), expert(l, g, c)).then_inc(moe_landed[l][i], 16)
                for i in range(BATCH):
                    if i not in SIDE:
                        g, c = part(i)
                        sp.wait_ge(y_full[l] if c == 2 else gu_full[l], 1)
                        sp.dma_start(expert_dst(l, i), expert(l, GROUPS + g, c)).then_inc(moe_landed[l][i], 16)
                with sp.Fori(2, OWN) as b:
                    for i in range(BATCH):
                        g, c = part(i)
                        sp.wait_ge(y_full[l] if c == 2 else gu_full[l], b)
                        sp.dma_start(expert_dst(l, i), expert(l, b * GROUPS + g, c)).then_inc(moe_landed[l][i], 16)
                sp.wait_ge(list_ready, l + 1)
                nb = sp.value_load(nb_i[0:1, 0:1], min_val=OWN, max_val=MAXB)
                with sp.If(nb - OWN):
                    with sp.Fori(OWN, nb) as b:
                        ids = [sp.value_load(ove_i[0:1, bass.ds((b - OWN) * GROUPS + g, 1)], min_val=0, max_val=NE - 1)
                               for g in range(GROUPS)]
                        for i in range(BATCH):
                            g, c = part(i)
                            sp.wait_ge(y_full[l] if c == 2 else gu_full[l], b)
                            sp.dma_start(expert_dst(l, i), expert(l, ids[g], c)).then_inc(moe_landed[l][i], 16)
                return nb

            proj_units(U_EV_IN, ev_w_in, EV_UNITS)
            out_units(U_EV_OUT, ev_w_out)
            nb = moe_units(0)
            proj_units(U_OD_IN, od_w_in, OD_UNITS, nb)
            sp.wait_ge(y_full[0], nb)
            cw = od_cmp_w[0].rearrange("w (h l) d e -> h d w l e", h=2)
            for h in range(2):
                for w in range(2):
                    dst = ring[h * DH:(h + 1) * DH, slot_of(U_CMP), w * NCMP * DH:(w + 1) * NCMP * DH]
                    sp.dma_start(dst.rearrange("p (l e) -> p l e", l=NCMP), cw[h, :, w]).then_inc(cmp_landed, 16)
            out_units(U_OD_OUT, od_w_out)
            moe_units(1)
            for t in range(NT):
                sp.wait_ge(x_ready, 3 * NT + t + 1)
                sp.dma_start(out[0, t * P:(t + 1) * P, :], xs[:, t, :]).then_inc(stored, 16)
            sp.wait_ge(stored, 16 * NT)

        @block.gpsimd
        def _(pool):
            g = nc.gpsimd
            chain = Chain(pool, pool_chain)

            g.memset(eps_t[:], EPS).then_inc(consts, 1)
            g.memset(one_t[:], 1.0).then_inc(consts, 1)
            g.memset(ones[:], 1.0).then_inc(consts, 1)
            chain(g.memset(ident[:], 0.0))
            g.affine_select(out=ident[:], in_=ident[:], compare_op=ALU.not_equal, fill=1.0, base=0,
                            pattern=[[-1, P]], channel_multiplier=1).then_inc(consts, 1)
            chain(g.memset(before[:], 1.0))
            g.affine_select(out=before[:], in_=before[:], compare_op=ALU.is_gt, fill=0.0, base=0,
                            pattern=[[1, P]], channel_multiplier=-1).then_inc(consts, 1)

            g.iota(first_q[:], pattern=[[TILE, NE]], base=0, channel_multiplier=0,
                   allow_small_or_imprecise_dtypes=True).then_inc(consts, 1)
            g.iota(first_far[:], pattern=[[TILE, NE]], base=TILE - NE * TILE, channel_multiplier=0,
                   allow_small_or_imprecise_dtypes=True).then_inc(consts, 1)
            g.iota(iota_j[:], pattern=[[1, MAXOVER]], base=0, channel_multiplier=0,
                   allow_small_or_imprecise_dtypes=True).then_inc(consts, 1)
            g.iota(steps7[:], pattern=[[TILE, S // TILE - 1]], base=TILE, channel_multiplier=0,
                   allow_small_or_imprecise_dtypes=True).then_inc(consts, 1)
            g.iota(iota_s[:], pattern=[[1, P]], base=0, channel_multiplier=0,
                   allow_small_or_imprecise_dtypes=True).then_inc(consts, 1)
            g.iota(iota8[:], pattern=[[0, NT], [1, EG]], base=-100, channel_multiplier=0,
                   allow_small_or_imprecise_dtypes=True).then_inc(consts, 1)
            g.iota(iota_e[:], pattern=[[1, NE]], base=0, channel_multiplier=0,
                   allow_small_or_imprecise_dtypes=True).then_inc(consts, 1)

            def bias_table(windowed):
                chain(g.iota(btab[:, 7, 0:P], pattern=[[-1, P]], base=0, channel_multiplier=1,
                             allow_small_or_imprecise_dtypes=True))
                chain(g.iota(btab[:, 7, P:SC], pattern=[[-1, S]], base=P, channel_multiplier=1,
                             allow_small_or_imprecise_dtypes=True))
                for h in range(8):
                    chain(g.tensor_scalar(btab[:, h, :], btab[:, 7, :], -SLOPES[h], None, ALU.mult))
                for a, n, base in ((0, P, 0), (P, S, P)):
                    v = btab[:, :, a:a + n]
                    chain(g.affine_select(out=v, in_=v, compare_op=ALU.is_ge,
                                          fill=NEG, base=base, pattern=[[0, 8], [-1, n]], channel_multiplier=1))
                if windowed:
                    chain(g.affine_select(out=btab[:, :, P:SC], in_=btab[:, :, P:SC], compare_op=ALU.is_gt,
                                          fill=NEG, base=0, pattern=[[0, 8], [1, S]], channel_multiplier=-1))

            bias_table(True)
            chain(g.memset(smask[:], 0.0))
            chain(g.affine_select(out=smask[:, 0:P], in_=smask[:, 0:P], compare_op=ALU.is_gt, fill=NEG,
                                  base=0, pattern=[[-1, P]], channel_multiplier=1))
            chain(g.affine_select(out=smask[:, P:SC], in_=smask[:, P:SC], compare_op=ALU.is_gt, fill=NEG,
                                  base=P, pattern=[[-1, S]], channel_multiplier=1))
            chain(g.memset(sreset[:], 1.0))
            g.memset(sreset[:, P - 1:P], 0.0).then_inc(tables, 1)
            pool.wait_ge(gains2_landed, 16 * N_HEAD_GAINS)
            for c in (0, 2, 4):
                g.tensor_scalar(qk_g[:, c:c + 1], qk_g[:, c:c + 1], 0.125, None, ALU.mult).then_inc(consts, 1)

            def stick_args():
                for n in range(8):
                    b = n % 2
                    pool.wait_ge(suffix_ready, n + 1)
                    g.tensor_tensor(la[b], s_sb[(n + 8) % 3], cu[b], ALU.subtract).then_inc(arg_ready, 1)

            def batch_weights(l):
                def one(b, before, first):
                    ch = Chain(pool, loop_pool[l], before)
                    if not first:
                        pool.wait_ge(ct_full[l], b)
                        ch(g.tensor_tensor(p_q, p_q, places, ALU.subtract))
                        g.sem_inc(places_moved, 1)
                    for t in range(NT):
                        for dst, q, w in ((comb, 0, r_m1), (otmp_m, 1, r_m2)):
                            last = g.tensor_scalar(dst[:, t, :], iota_s[:], p_q[:, q, t:t + 1], w[:, t:t + 1],
                                                   ALU.is_equal, ALU.mult)
                            if not (t == NT - 1 and q == 1):
                                ch.count(last)
                    ch(last)
                    g.tensor_tensor(comb, comb, otmp_m, ALU.add).then_inc(c_ready[l], 1)
                    return ch.n

                pool.wait_ge(q_ready[l], 1)
                chain(g.tensor_copy(p_q, r_q))
                chain(g.memset(places, float(P)))
                g.sem_inc(c_copied, 1)
                done = one(0, 0, True)
                pool.wait_ge(list_ready, l + 1)
                nb = pool.value_load(nb_i[0:1, 0:1], min_val=OWN, max_val=MAXB)
                with pool.Fori(1, nb) as b:
                    per = done + 1
                    assert one(b, b * per - 1, False) == per

            def cmp_tables():
                chain(g.iota(ctab.rearrange("p t a b n -> p t (a b) n"),
                             pattern=[[P, NT], [0, 8], [-CSTEP, NCMP]], base=-(CLEN - 1),
                             channel_multiplier=1, allow_small_or_imprecise_dtypes=True))
                for pr in range(4):
                    for kv in range(2):
                        v = ctab[:, :, pr, kv, :]
                        chain(g.tensor_scalar(v, v, -SLOPES[kv * 4 + pr], None, ALU.mult))
                chain(g.memset(cmask, 1.0))
                for a, fill in ((ctab, NEG), (cmask, 0.0)):
                    for t in range(NT):
                        v = a[:, t].rearrange("p a b n -> p (a b) n")
                        chain(g.affine_select(out=v, in_=v, compare_op=ALU.is_ge, fill=fill,
                                              base=P * t - (CLEN - 1), pattern=[[0, 8], [-CSTEP, NCMP]],
                                              channel_multiplier=1))
                    chain(g.memset(a.rearrange("p t a b n -> p (t a b) n")[:, :, NCMP - 1:NCMP], fill))
                pool.wait_ge(consts, N_CONST)
                for a in range(4):
                    chain(g.tensor_copy(spread[0:32, a, :], ident[0:32, 0:32]))
                chain(g.memset(blk, 1.0))
                chain(g.affine_select(out=blk, in_=blk, compare_op=ALU.is_ge, fill=0.0, base=0,
                                      pattern=[[-NCMP, 8]], channel_multiplier=1))
                g.affine_select(out=blk, in_=blk, compare_op=ALU.is_ge, fill=0.0, base=NCMP - 1,
                                pattern=[[NCMP, 8]], channel_multiplier=-1).then_inc(tables, 1)

            stick_args()
            batch_weights(0)
            pool.wait_ge(x_ready, 2 * NT)
            bias_table(False)
            cmp_tables()
            batch_weights(1)

        @block.tensor
        def _(pe):
            T = nc.tensor
            turns = {"a": 0, "b": 0}
            units, drains = [0], []
            nd = {"act": 0, "dve": 0}
            job = {"s": 0, "t": 0, "v": 0}

            def turn(which, pieces):
                full, free, bk = (ta_full, ta_free, 2) if which == "a" else (tb_full, tb_free, 3)
                if turns[which]:
                    pe.wait_ge(free, turns[which])
                for c, v in pieces:
                    k, m = v.shape[0], 1
                    for e in v.shape[1:]:
                        m *= e
                    last = T.transpose(bank[bk][0:m, c:c + k], v, ident[0:k, 0:k])
                last.then_inc(full, 1)
                turns[which] += 1

            def turned():
                pe.wait_ge(ta_free, turns["a"])
                pe.wait_ge(tb_free, turns["b"])

            def keep_warm(n, bk):
                for _ in range(n):
                    T.matmul(bank[bk][:], ones[:], ones[:].unsqueeze(1).broadcast_to([P, 4, P]), start=True, stop=True)

            def norm_turn(n):
                if n == 0:
                    pe.wait_ge(consts, N_CONST_A)
                keep_warm(WARM_NORM[n], (7, 7, 0, 7)[n])
                src = xn
                if n % 2:
                    src = xs
                    pe.wait_ge(x_ready, NT * n)
                else:
                    pe.wait_ge(xn_ready, NT * (n + 1))
                if n == 1:
                    pe.wait_ge(late_landed, 16 * N_LATE)
                for b in range(4):
                    turn("ab"[b % 2], [(kk * S + t * P, tok(src[:, t, :], 2 * b + kk))
                                       for kk in range(2) for t in range(NT)])
                turned()

            def project(n, who):
                if units[0] >= 2:
                    pe.wait_ge(*drains[units[0] - 2])
                pe.wait_ge(landed[slot_of(n)], landings(n))
                w = ring[:, slot_of(n), :].rearrange("p (k c) -> p k c", k=KD)
                for t in range(NT):
                    for k in range(KD):
                        last = T.matmul(bank[units[0] % 2][:, t * UC:(t + 1) * UC], hT[:, k, t * P:(t + 1) * P],
                                        w[:, k, :], start=(k == 0), stop=(k == KD - 1))
                last.then_inc(pr_full, 1)
                units[0] += 1
                nd[who] += 1
                drains.append((pr_act if who == "act" else pr_dve, nd[who]))

            def qk_of(kind, h):
                if kind in "BC":
                    r = slice(DH * (h % 2), DH * (h % 2) + DH)
                    return (qT[1] if kind == "B" else qT[0])[r, h // 2, :], kT[r, h // 2, :]
                r = slice(DH * (h // 4), DH * (h // 4) + DH)
                k = kTp[1] if kind == "W" else kTp[0]
                return (qT[0] if kind == "A" else qT[1])[r, h % 4, :], k[r, :]

            def v_of(kind, h, t):
                if kind in "BC":
                    return vbig[:, t, h * DH:(h + 1) * DH]
                return vsm[kind == "W"][:, t, (h // 4) * DH:(h // 4 + 1) * DH]

            def scores(kind, h):
                n = job["s"]
                if n >= 2:
                    pe.wait_ge(sc_free, n - 1)
                if n in V_THERE:
                    turned()
                q, k = qk_of(kind, h)
                b = bank[4 + n % 2]
                T.matmul(b[:, 0:P], q[:, 0:P], k[:, 0:P], start=True, stop=True)
                T.matmul(b[:, P:SC], q[:, P:S], k[:, 0:S], start=True, stop=True).then_inc(sc_full, 1)
                job["s"] += 1

            def turn_p(kind):
                n = job["t"]
                pe.wait_ge(*((p_ready, PR[n]) if kind == "B" else (ps_ready, NMN[n])))
                if n:
                    pe.wait_ge(pt_ready, n)
                for c in range(3):
                    last = T.transpose(bank[6][:, c * P:(c + 1) * P], p_sb[n % 3][:, c * P:(c + 1) * P], ident[:])
                last.then_inc(pt_full, 1)
                job["t"] += 1

            def values(kind, h):
                n = job["v"]
                pe.wait_ge(pt_ready, n + 2)
                if GROUP_FIRST[n] and n:
                    pe.wait_ge(o_ready, GROUPS_BEFORE[n])
                if n == len(JOBS[0]):
                    pe.wait_ge(gate_ready, 1)
                if n in V_THERE:
                    who, count = V_THERE[n]
                    pe.wait_ge(pr_dve if who == "dve" else pr_act, count)
                if kind == "W" and h == 1:
                    turned()
                pair = (h - 1, h)
                o = [bank[7][DH * i:DH * i + DH, (h % 4) // 2 * S:(h % 4) // 2 * S + S] for i in range(2)]
                pt = [pT[(n + i) % 3] for i in range(2)]
                for i in range(2):
                    T.matmul(o[i], v_of(kind, pair[i], 0), pt[i][:, 0:2 * P], start=(kind != "W" and h % 4 < 2),
                             stop=True, skip_group_check=True)
                last = [T.matmul(o[i][:, P:S], v_of(kind, pair[i], 1), pt[i][:, 2 * P:3 * P], start=False, stop=True,
                                 skip_group_check=True) for i in range(2)]
                if kind == "W":
                    last = [T.matmul(o[i], v_blk[:, pair[i] % 4 * 2 + h // 4, :], pcT.rearrange("p t q -> p (t q)"),
                                     start=False, stop=True, skip_group_check=True) for i in range(2)]
                for ins in last:
                    ins.then_inc(o_full, 1)
                job["v"] += 2

            def step(layer, i, kt):
                jobs = JOBS[layer]
                if i < len(jobs):
                    scores(*jobs[i])
                if kt is not None:
                    out_both(layer, kt)
                if 0 <= i - 2 < len(jobs):
                    turn_p(jobs[i - 2][0])
                if 0 <= i - SKEW < len(jobs) and jobs[i - SKEW][1] % 2:
                    values(*jobs[i - SKEW])

            def pairs(src, ps):
                return [(i * S + t * P, src[:, t, pr * P:(pr + 1) * P]) for i, pr in enumerate(ps) for t in range(NT)]

            def turn_qk(what):
                src, which, who, count = TURNS[what]
                pe.wait_ge(pr_act if who == "act" else pr_dve, count)
                if src in (2, 3):
                    turn(which, pairs(stk[src - 2], [0]))
                else:
                    turn("a", pairs(stage[src], [0, 1]))
                    turn("b", pairs(stage[src], [2, 3]))

            def cmp_stage(k):
                w = ring[:, slot_of(U_CMP), :].rearrange("p (w l e) -> p w l e", w=2, l=NCMP)
                if k == "pos":
                    pe.wait_ge(late_landed, 16 * N_LATE)
                    turn("a", [(c * NCMP, pos_in[:, c, :]) for c in range(2)])
                elif k == "in":
                    pe.wait_ge(pr_act, nd["act"])
                    pe.wait_ge(pr_dve, nd["dve"])
                    for c in range(2):
                        for h in range(2):
                            for t in range(NT):
                                v = cin[:, t, 2 * c + h].rearrange("p a d -> p (a d)")
                                last = T.transpose(bank[c][:, h * S + t * P:h * S + (t + 1) * P],
                                                   v, ident[:])
                    last.then_inc(cmp_full, 1)
                elif k == "compress":
                    pe.wait_ge(cmp_landed, 4 * 16)
                    pe.wait_ge(cmp_dve, CD_T2)
                    tk, tv = (a.rearrange("p h (n l) -> p l (h n)", l=CSTEP) for a in t2)
                    for l in range(NCMP):
                        T.matmul(bank[0][0:32, 0:DH], tk[:, l], w[:, 0, l, :], start=(l == 0), stop=(l == NCMP - 1))
                    for l in range(NCMP):
                        last = T.matmul(bank[1][0:32, 0:DH], tv[:, l],
                                        w[:, 1, l, :], start=(l == 0), stop=(l == NCMP - 1))
                    last.then_inc(cmp_full, 1)
                elif k == "keys":
                    pe.wait_ge(cmp_dve, CD_KEYS)
                    turn("a", [(0, kc_b[0:32].rearrange("p a d -> p (a d)"))])
                    pe.wait_ge(cmp_act, 1)
                    T.matmul(bank[1][:, 0:DH], spread[0:32].rearrange("p a b -> p (a b)"), vc[0:32, :],
                             start=True, stop=True).then_inc(cmp_full, 1)
                elif k == "scores":
                    turned()
                    for t in range(NT):
                        for pr in range(4):
                            last = T.matmul(bank[0][:, t * P + pr * 32:t * P + (pr + 1) * 32],
                                            qT[1][:, pr, t * P:(t + 1) * P], kcT[:], start=True, stop=True)
                    last.then_inc(cmp_full, 1)
                elif k == "p":
                    pe.wait_ge(cmp_dve, CD_P)
                    turn("a", [(t * P, cs[:, t].rearrange("p a b n -> p (a b n)")) for t in range(NT)])

            def out_there(layer, u):
                pe.wait_ge(o_ready, 4 * layer + u + 1)
                n = (U_EV_OUT, U_OD_OUT)[layer] + u
                pe.wait_ge(landed[slot_of(n)], landings(n))

            def out_tile(layer, kt, t):
                w = ring[:, slot_of((U_EV_OUT, U_OD_OUT)[layer] + kt // 2), :].rearrange("p (k c) -> p k c", k=2)
                for hf in range(2):
                    last = T.matmul(bank[2 * t + hf][:], oT[:, kt, t * P:(t + 1) * P],
                                    w[:, kt % 2, hf * 512:(hf + 1) * 512], start=(kt == 0), stop=True,
                                    skip_group_check=True)
                return last

            def out_both(layer, kt):
                if kt == 0:
                    turned()
                    pe.wait_ge(pr_act, nd["act"])
                    pe.wait_ge(pr_dve, nd["dve"])
                if kt % 2 == 0:
                    out_there(layer, kt // 2)
                for t in range(NT):
                    last = out_tile(layer, kt, t)
                if kt % 2:
                    last.then_inc(wo_used, 1)

            def mixer(layer):
                norm_turn(2 * layer)
                if layer:
                    for t in range(NT):
                        for k in range(KD):
                            last = T.matmul(bank[7][:, t * 32:t * 32 + GATES], hT[:, k, t * P:(t + 1) * P], w_gd[:, k, :],
                                            start=(k == 0), stop=(k == KD - 1))
                    last.then_inc(gate_full, 1)
                for what, *arg in ORDER[layer]:
                    if what == "unit":
                        project((U_EV_IN, U_OD_IN)[layer] + arg[0], arg[1])
                    elif what == "turn":
                        turn_qk(arg[0])
                    elif what == "cmp":
                        cmp_stage(arg[0])
                    elif what == "steps":
                        for i in range(arg[0], arg[1]):
                            step(layer, i, arg[2] if len(arg) > 2 else None)
                u = OUT_UNITS - 1
                out_there(layer, u)
                for t in range(NT):
                    for kt in (2 * u, 2 * u + 1):
                        last = out_tile(layer, kt, t)
                    last.then_inc(wo_used if t else mix_tile, 1)

            def moe(l):
                norm_turn(2 * l + 1)
                for t in range(NT):
                    for k in range(KD):
                        last = T.matmul(bank[0][:, t * 64:t * 64 + NG + NE], hT[:, k, t * P:(t + 1) * P], w_rt[:, l, k, :],
                                        start=(k == 0), stop=(k == KD - 1))
                last.then_inc(rt_full, 1)
                keep_warm(WARM_CHOICE, 7)
                pe.wait_ge(rt_mask, l + 1)
                m0, m1, c = mask[:, 0, :], mask[:, 1, :], bank[1]
                T.matmul(c[:, 0:NE], before[:], m0, start=True, stop=True)
                T.matmul(c[:, NE:2 * NE], ones[:], m0, start=True, stop=False)
                T.matmul(c[:, NE:2 * NE], before[:], m1, start=False, stop=True)
                T.matmul(c[:, 2 * NE:3 * NE], ones[:], m0, start=True, stop=False)
                T.matmul(c[:, 2 * NE:3 * NE], ones[:], m1, start=False, stop=True).then_inc(rt_full, 1)

                def gather(b):
                    pe.wait_ge(b_ready[l], b + 1)
                    for k in range(KD):
                        for t in range(NT):
                            last = T.matmul(bank[2 + k // 4][:, (k % 4) * P:(k % 4 + 1) * P], tok(xn[:, t, :], k),
                                            oneh[:, t, :], start=(t == 0), stop=(t == NT - 1))
                        if k % 4 == 3:
                            last.then_inc(ga_full[l], 1)

                def there(i, b, first, side):
                    if side and i in SIDE:
                        pe.wait_ge(side_landed, 16 * len(SIDE) * (l + 1))
                    elif i in SIDE and not first:
                        pe.wait_ge(moe_landed[l][i], 16 * b)
                    else:
                        pe.wait_ge(moe_landed[l][i], 16 * (b + 1))

                def batch(b, first=False, side=False):
                    if not first:
                        pe.wait_ge(hid_ready[l], b)
                    for k in range(KD):
                        if k % 4 == 0:
                            pe.wait_ge(xt_ready[l], 2 * b + k // 4 + 1)
                        for g in range(GROUPS):
                            if k == 0:
                                there(2 * g, b, first, side)
                                there(2 * g + 1, b, first, side)
                            s = slot_of(U_MOE[l] + 2 * g)
                            w = side_pair if side and g == 0 else ring[:, s:s + 2, :]
                            w = w.rearrange("p u (k c) -> p u k c", k=KD)[:, :, k, :]
                            last = T.matmul(bank[0][g * TILE:(g + 1) * TILE, :], xt[:, k, g * TILE:(g + 1) * TILE], w,
                                            start=(k == 0), stop=(k == KD - 1))
                    last.then_inc(gu_full[l], 1)
                    pe.wait_ge(c_ready[l], b + 1)
                    if not first:
                        pe.wait_ge(ht_ready[l], b)
                    for t in range(NT):
                        last = T.transpose(bank[1][:, (2 + t) * P:(3 + t) * P], comb[:, t, :], ident[:])
                    last.then_inc(ct_full[l], 1)
                    if not first:
                        pe.wait_ge(y_act[l], b)
                        pe.wait_ge(y_dve[l], b)
                    gather(b + 1)
                    pe.wait_ge(hid_ready[l], b + 1)
                    pe.wait_ge(ct_ready[l], b + 1)
                    for k in range(KF):
                        last = T.transpose(bank[1][:, k * P:(k + 1) * P], hid[:, k * P:(k + 1) * P], ident[:])
                    last.then_inc(ht_full[l], 1)
                    pe.wait_ge(ht_ready[l], b + 1)
                    pe.wait_ge(xt_ready[l], 2 * b + 4)
                    for k in range(KF):
                        for hf in range(2):
                            for g in range(GROUPS):
                                if k == 0 and hf == 0:
                                    there(2 * GROUPS + g, b, first, side)
                                w = side_down[:] if side and g == 0 else ring[:, slot_of(U_MOE[l] + 2 * GROUPS + g), :]
                                w = w.rearrange("p (k c) -> p k c", k=KF)
                                last = T.matmul(bank[2 + hf][g * TILE:(g + 1) * TILE, :], hidT[:, k, g * TILE:(g + 1) * TILE],
                                                w[:, k, hf * 512:(hf + 1) * 512], start=(k == 0), stop=(k == KF - 1))
                    last.then_inc(y_full[l], 1)
                    pe.wait_ge(y_act[l], b + 1)
                    pe.wait_ge(y_dve[l], b + 1)
                    for t in range(NT):
                        for hf in range(2):
                            last = T.matmul(bank[4 + 2 * t + hf][:], combT[:, t, :], yb[:, hf * 512:(hf + 1) * 512],
                                            start=first, stop=True, skip_group_check=True)
                    last.then_inc(added[l], 1)

                keep_warm(WARM_PLACES, 7)
                pe.wait_ge(xn_ready, NT * (2 * l + 2))
                gather(0)
                batch(0, first=True)
                batch(1, side=True)
                pe.wait_ge(list_ready, l + 1)
                nb = pe.value_load(nb_i[0:1, 0:1], min_val=OWN, max_val=MAXB)
                with pe.Fori(2, nb) as b:
                    batch(b)

            mixer(0)
            moe(0)
            mixer(1)
            moe(1)

        @block.scalar
        def _(act):
            A = nc.scalar
            chain = Chain(act, act_chain)
            n_a, unit, n_act, n_sq, job = [0], [0], [0], [0], [0]
            A.preload_act_table_set("natural_log_exp_and_others")

            def late_loads():
                loads = [(g_col[:, n, :], col(v)) for n, v in ((1, moe_norm[0]), (2, od_norm[0]), (3, moe_norm[1]))]
                loads.append((w_gd[:], od_w_in[0, :, OD_UNITS * UC:].rearrange("(p k) n -> p k n", k=KD)))
                for l in range(2):
                    loads += [(w_rt[:, l, :, 0:NG], moe_w_grp[l].rearrange("(p k) n -> p k n", k=KD)),
                              (w_rt[:, l, :, NG:], moe_w_exp[l].rearrange("(p k) n -> p k n", k=KD)),
                              (b_rt[:, l, 0:NG], moe_b_grp[l:l + 1].broadcast_to([P, NG])),
                              (b_rt[:, l, NG:], moe_b_exp[l:l + 1].broadcast_to([P, NE])),
                              (pos_in[:, l, :].rearrange("l (h d) -> l h d", h=2),
                               od_cmp_pos[0, l].rearrange("(h l) d -> l h d", h=2))]
                assert len(loads) == N_LATE
                for dst, src in loads:
                    act.dma_start(dst, src, allow_slow_non_contiguous=True).then_inc(late_landed, 16)

            def rms(n):
                junk = junk_m if n % 2 else stage[0].rearrange("p a b -> p (a b)")
                for t in range(NT):
                    act.wait_ge(*((x_landed, 16 * NT) if n == 0 else (x_ready, NT * (n - 1) + t + 1)))
                    chain(A.activation(junk, xs[:, t, :], ACT.Square, accum_out=ssq[:, t:t + 1]))
                    if t == 0 and n % 2:
                        norm_drain(n)
                if n == 0:
                    act.wait_ge(consts, N_CONST_A)
                chain(A.activation(lnr[:], ssq[:], ACT.Ln, bias=eps_t[:], scale=1.0 / D))
                A.activation(rstd[:], lnr[:], ACT.Exp, scale=-0.5).then_inc(rstd_ready, 1)

            def drain_a(dst, scale=None, cols=512, rows=P, split=1):
                n_a[0] += 1
                act.wait_ge(ta_full, n_a[0])
                w = cols // split
                for i in range(split):
                    src = bank[2][0:rows, i * w:(i + 1) * w]
                    s = scale[i] if isinstance(scale, list) else scale
                    d = dst[i] if split > 1 else dst
                    if s is None:
                        last = A.copy(d, src)
                    else:
                        last = A.mul(d, src, s)
                last.then_inc(ta_free, 1)

            def norm_drain(n):
                act.wait_ge(*((gains_landed, 16) if n == 0 else (late_landed, 16 * N_LATE)))
                for b in (0, 2):
                    drain_a([hT[:, 2 * b + kk, :] for kk in range(2)],
                            [g_col[:, n, 2 * b + kk:2 * b + kk + 1] for kk in range(2)], split=2)

            def squares(normed):
                n_sq[0] += 1
                n = n_sq[0]
                if n > 1:
                    act.wait_ge(ms_ready, n - 1)
                w = normed * DH
                b = bank[unit[0] % 2][:].rearrange("p (t c) -> p t c", t=NT)
                A.activation(sq[:, :, 0:normed, :].rearrange("p t h d -> p t (h d)"), b[:, :, 0:w],
                             ACT.Square).then_inc(sq_ready, 1)
                act.wait_ge(ms_ready, n)
                chain(A.activation(lq[:, :, 0:normed], red[:, :, 0:normed], ACT.Ln, bias=eps_t[:], scale=1.0 / DH))
                A.activation(rq[:, :, 0:normed], lq[:, :, 0:normed], ACT.Exp, scale=-0.5).then_inc(rq_ready, 1)

            def step(jobs, i, first):
                if i < len(jobs) and jobs[i][0] == "B":
                    n, b = i - 8, i % 2
                    act.wait_ge(sc_free, first + i + 1)
                    if n >= 2:
                        act.wait_ge(suffix_ready, n - 1)
                    chain(A.activation(ea[b], s_sb[(first + i) % 3], ACT.Abs))
                    chain(A.activation(ea[b], ea[b], ACT.Exp, scale=-1.0))
                    A.activation(ea[b], ea[b], ACT.Ln, bias=one_t[:]).then_inc(ln_ready, 1)
                elif i < len(jobs):
                    n = first + i
                    act.wait_ge(nm_ready, NMN[n])
                    if n >= 3:
                        act.wait_ge(pt_full, n - 2)
                    for q, (a, b) in enumerate(((0, P), (P, SC))):
                        A.activation(p_sb[n % 3][:, a:b], s_sb[n % 3][:, a:b], ACT.Exp, bias=nm[:, i, q:q + 1],
                                     accum_out=den[:, i, q:q + 1]).then_inc(p_ready, 1)
                if 0 <= i - 1 < len(jobs) and jobs[i - 1][0] == "B":
                    n = first + i - 1
                    act.wait_ge(arg_ready, i - 1 - 8 + 1)
                    act.wait_ge(pt_full, n - 2)
                    A.activation(p_sb[n % 3], la[n % 2], ACT.Exp).then_inc(p_ready, 1)
                if i < len(jobs) and jobs[i][0] == "A":
                    act.wait_ge(es_in, i + 1)
                    A.activation(es[:, i, :], es[:, i, :], ACT.Exp).then_inc(es_out, 1)
                if 0 <= i - 2 < len(jobs) and jobs[i - 2][0] != "B":
                    n = first + i - 2
                    act.wait_ge(pt_full, n + 1)
                    if n >= 3:
                        act.wait_ge(o_full, n - 2)
                    A.copy(pT[n % 3], bank[6][:, 0:SC]).then_inc(pt_ready, 1)
                if 0 <= i - SKEW < len(jobs) and jobs[i - SKEW] in (("B", 3), ("B", 7)):
                    n, k = first + i - SKEW, 4 + jobs[i - SKEW][1] // 4 * 2
                    act.wait_ge(o_full, n + 1)
                    A.copy(oT[:, k:k + 2, :].rearrange("p k s -> p (k s)"), bank[7][:]).then_inc(o_ready, 1)

            def drain_cmp(k):
                if k == "pos":
                    drain_a(posT.rearrange("p w l -> p (w l)"), cols=2 * NCMP)
                elif k == "compress":
                    act.wait_ge(cmp_full, CF_COMPRESSED)
                    A.copy(vc[0:32, :], bank[1][0:32, 0:DH]).then_inc(cmp_act, 1)
                    chain(A.activation(kc_n[0:32, :], bank[0][0:32, 0:DH], ACT.Square, accum_out=csm[0:32, 0:1]))
                    chain(A.activation(csm[0:32, 1:2], csm[0:32, 0:1], ACT.Ln, bias=eps_t[0:32, :], scale=1.0 / DH))
                    A.activation(csm[0:32, 2:3], csm[0:32, 1:2], ACT.Exp, scale=-0.5).then_inc(cmp_act, 1)
                elif k == "keys":
                    drain_a(kcT[:], qk_g[:, 5:6], cols=32)
                elif k == "scores":
                    act.wait_ge(cmp_dve, CD_ARG)
                    A.activation(cs, cs, ACT.Exp).then_inc(cmp_act, 1)
                elif k == "p":
                    drain_a(pcT.rearrange("p t q -> p (t q)"), cols=NT * P)

            def mixer(layer):
                rms(2 * layer)
                norm_drain(2 * layer)
                if layer == 0:
                    late_loads()
                else:
                    act.wait_ge(gate_full, 1)
                    v = bank[7][:, 0:64].rearrange("p (t c) -> p t c", t=NT)[:, :, 0:GATES]
                    A.activation(gates.rearrange("p t h c -> p t (h c)"), v, ACT.Exp, scale=-1.0).then_inc(gate_exp, 1)
                first = layer * len(JOBS[0])
                for what, *arg in DRAIN_ORDER[layer]:
                    if what == "unit":
                        act.wait_ge(pr_full, unit[0] + 1)
                        if arg[1] == "dve":
                            squares(arg[2])
                        else:
                            dst = DST[layer][arg[0]]
                            if arg[0] in (5, 6) and layer == 0:
                                act.wait_ge(ta_full, T_QA_A)
                                act.wait_ge(tb_full, T_QA_B)
                            v = bank[unit[0] % 2][:]
                            if dst is None:
                                v = v.rearrange("p (t h d) -> p t h d", t=NT, h=4)
                                A.copy(cin[:, :, :, 0, :], v)
                                A.copy(cin[:, :, :, 1, :], v).then_inc(pr_act, 1)
                            else:
                                A.copy(dst, v.rearrange("p (t c) -> p t c", t=NT)).then_inc(pr_act, 1)
                        unit[0] += 1
                    elif what == "turn":
                        if arg[0] == "qa":
                            act.wait_ge(consts, N_CONST)
                        src, which, who, count = TURNS[arg[0]]
                        dst, scale = TDST[arg[0]]
                        if src < 2:
                            drain_a(dst[:, 0:2, :].rearrange("p a b -> p (a b)"), scale)
                        elif which == "a":
                            drain_a(dst, scale, cols=S)
                    elif what == "cmp":
                        drain_cmp(arg[0])
                    elif what == "steps":
                        for i in range(arg[0], arg[1]):
                            step(JOBS[layer], i, first)

            def moe(l):
                rms(2 * l + 1)
                act.wait_ge(rt_gs, l + 1)
                A.activation(ge, ge, ACT.Exp).then_inc(rt_ge, 1)
                act.wait_ge(rt_ws, l + 1)
                A.activation(r_s, r_s, ACT.Exp).then_inc(rt_we, 1)

                def batch(b):
                    act.wait_ge(gu_full[l], b + 1)
                    A.activation(en, bank[0][:, 0:FF], ACT.Exp, scale=-1.0).then_inc(en_ready[l], 1)
                    act.wait_ge(ct_full[l], b + 1)
                    A.copy(combT.rearrange("p t q -> p (t q)"), bank[1][:, 2 * P:4 * P]).then_inc(ct_ready[l], 1)
                    act.wait_ge(ht_full[l], b + 1)
                    A.copy(hidT.rearrange("p k q -> p (k q)"), bank[1][:, 0:2 * P]).then_inc(ht_ready[l], 1)
                    act.wait_ge(y_full[l], b + 1)
                    A.copy(yb[:, 0:512], bank[2][:]).then_inc(y_act[l], 1)

                batch(0)
                act.wait_ge(list_ready, l + 1)
                nb = act.value_load(nb_i[0:1, 0:1], min_val=OWN, max_val=MAXB)
                with act.Fori(1, nb) as b:
                    batch(b)

            mixer(0)
            moe(0)
            mixer(1)
            moe(1)

        @block.vector
        def _(dve):
            V = nc.vector
            chain = Chain(dve, dve_chain)
            n_b, unit, n_sq = [0], [0], [0]

            def normed(n):
                dve.wait_ge(rstd_ready, n + 1)
                for t in range(NT):
                    V.tensor_scalar(xn[:, t, :], xs[:, t, :], rstd[:, t:t + 1], None, ALU.mult).then_inc(xn_ready, 1)

            def drain_b(dst, scale=None, cols=512, split=1):
                n_b[0] += 1
                dve.wait_ge(tb_full, n_b[0])
                w = cols // split
                for i in range(split):
                    src = bank[3][:, i * w:(i + 1) * w]
                    s = scale[i] if isinstance(scale, list) else scale
                    d = dst[i] if split > 1 else dst
                    if s is None:
                        last = V.tensor_copy(d, src)
                    else:
                        last = V.tensor_scalar(d, src, s, None, ALU.mult)
                last.then_inc(tb_free, 1)

            def norm_drain(n):
                dve.wait_ge(*((gains_landed, 16) if n == 0 else (late_landed, 16 * N_LATE)))
                for b in (1, 3):
                    drain_b([hT[:, 2 * b + kk, :] for kk in range(2)],
                            [g_col[:, n, 2 * b + kk:2 * b + kk + 1] for kk in range(2)], split=2)

            def normed_unit(layer, u, heads):
                n_sq[0] += 1
                n = n_sq[0]
                dve.wait_ge(sq_ready, n)
                V.tensor_reduce(red[:, :, 0:heads], sq[:, :, 0:heads, :], AX, ALU.add).then_inc(ms_ready, 1)
                b = bank[unit[0] % 2][:].rearrange("p (t h d) -> p t h d", t=NT, h=4)
                dst, rest = DST[layer][u]
                if layer == 1 and u in (6, 7):
                    dve.wait_ge(ta_full, T_QC_A)
                    dve.wait_ge(tb_full, T_QC_B)
                if heads < 4:
                    V.tensor_copy(rest, bank[unit[0] % 2][:].rearrange("p (t c) -> p t c", t=NT)[:, :, heads * DH:])
                dve.wait_ge(rq_ready, n)
                V.tensor_tensor(dst, b[:, :, 0:heads, :], rq[:, :, 0:heads].unsqueeze(3).broadcast_to([P, NT, heads, DH]),
                                ALU.mult).then_inc(pr_dve, 1)

            def step(jobs, i, layer):
                first = layer * len(JOBS[0])
                if i < len(jobs):
                    kind, h = jobs[i]
                    n = first + i
                    dve.wait_ge(sc_full, n + 1)
                    if n >= 3:
                        dve.wait_ge(p_ready, PR[n - 3])
                    b = bank[4 + n % 2]
                    if kind == "B":
                        V.tensor_tensor(s_sb[n % 3], b[:, 0:SC], smask[:], ALU.add).then_inc(sc_free, 1)
                    else:
                        V.tensor_tensor_reduce(s_sb[n % 3][:, 0:P], b[:, 0:P], btab[:, h, 0:P], 1.0, 3 * NEG,
                                               ALU.add, ALU.max, mx[:, i, 0:1])
                        V.tensor_tensor_reduce(s_sb[n % 3][:, P:SC], b[:, P:SC], btab[:, h, P:SC], 1.0, 3 * NEG,
                                               ALU.add, ALU.max, mx[:, i, 1:2]).then_inc(sc_free, 1)
                        dve.wait_ge(sc_free, n + 1)
                        if kind == "A":
                            V.tensor_scalar(nm[:, i, :], mx[:, i, :], sink[:, h:h + 1], -1.0,
                                            ALU.max, ALU.mult).then_inc(nm_ready, 1)
                            dve.wait_ge(nm_ready, NMN[n])
                            V.tensor_scalar(es[:, h, :], nm[:, i, :], sink[:, h:h + 1], None, ALU.add).then_inc(es_in, 1)
                        else:
                            V.tensor_scalar(nm[:, i, :], mx[:, i, :], -1.0, None, ALU.mult).then_inc(nm_ready, 1)
                if 0 <= i - 1 < len(jobs) and jobs[i - 1][0] == "B":
                    m, b = i - 1 - 8, (i - 1) % 2
                    dve.wait_ge(ln_ready, m + 1)
                    chain(V.scalar_tensor_tensor(out=la[b], in0=s_sb[(first + i - 1) % 3], scalar=0.0, in1=ea[b], op0=ALU.max, op1=ALU.add))
                    V.tensor_tensor_scan(cu[b][:, ::-1], sreset[:, ::-1], la[b][:, ::-1], 0.0,
                                         ALU.mult, ALU.add).then_inc(suffix_ready, 1)
                if 0 <= i - 1 < len(jobs) and jobs[i - 1][0] != "B":
                    over_sums(jobs, i - 1, first)
                if 0 <= i - 2 < len(jobs) and jobs[i - 2][0] == "B":
                    n = first + i - 2
                    dve.wait_ge(pt_full, n + 1)
                    if n >= 3:
                        dve.wait_ge(o_full, n - 2)
                    V.tensor_copy(pT[n % 3], bank[6][:, 0:SC]).then_inc(pt_ready, 1)
                if 0 <= i - SKEW < len(jobs):
                    (kind, h), n = jobs[i - SKEW], first + i - SKEW
                    if kind != "B" and GROUP_LAST[n]:
                        k = (4 if kind == "W" else 0) + h // 4 * 2
                        dve.wait_ge(o_full, n + 1)
                        V.tensor_copy(oT[:, k:k + 2, :].rearrange("p k s -> p (k s)"), bank[7][:]).then_inc(o_ready, 1)

            def over_sums(jobs, i, first):
                n, (kind, h) = first + i, jobs[i]
                dve.wait_ge(p_ready, PR[n])
                d, c = den[:, i, :], cf[:, i, :]
                if kind == "A":
                    dve.wait_ge(es_out, h + 1)
                    chain(V.tensor_tensor(d, d, es[:, h, :], ALU.add))
                chain(V.reciprocal(c, d))
                if kind in "LW":
                    chain(V.tensor_tensor(c, c, gates[:, :, h, 1 if kind == "L" else 2], ALU.mult))
                p = p_sb[n % 3]
                V.tensor_scalar(p[:, 0:P], p[:, 0:P], c[:, 0:1], None, ALU.mult)
                V.tensor_scalar(p[:, P:SC], p[:, P:SC], c[:, 1:2], None, ALU.mult).then_inc(ps_ready, 1)

            def cmp_stage(k):
                if k == "in":
                    dve.wait_ge(cmp_full, 1)
                    dve.wait_ge(ta_free, T_POS)
                    for c in range(2):
                        lo = bank[c][0:DH, :].rearrange("p (m l) -> p m l", l=CSTEP)
                        V.tensor_tensor(t2[c][0:DH].rearrange("p h (n l) -> p (h n) l", l=CSTEP), lo,
                                        posT[0:DH, c, :].unsqueeze(1).broadcast_to([DH, 32, CSTEP]), ALU.add)
                        hi = bank[c][DH:P, :].rearrange("p (h n l) -> p h n l", h=2, l=CSTEP)[:, :, 1:, :]
                        dst = t2[c][DH:P].rearrange("p h (n l) -> p h n l", l=CSTEP)
                        V.tensor_tensor(dst[:, :, 0:NCMP - 1, :], hi,
                                        posT[DH:P, c, :].unsqueeze(1).unsqueeze(1).broadcast_to([DH, 2, NCMP - 1, CSTEP]),
                                        ALU.add)
                        last = V.memset(dst[:, :, NCMP - 1, :], 0.0)
                    last.then_inc(cmp_dve, 1)
                elif k == "compress":
                    dve.wait_ge(cmp_act, 2)
                    dve.wait_ge(tables, 2)
                    chain(V.tensor_scalar(kc_n[0:32, :], bank[0][0:32, 0:DH], csm[0:32, 2:3], None, ALU.mult))
                    V.tensor_tensor(kc_b[0:32], kc_n[0:32].unsqueeze(1).broadcast_to([32, 2, DH]),
                                    blk[0:32, 0:2].unsqueeze(2).broadcast_to([32, 2, DH]), ALU.mult).then_inc(cmp_dve, 1)
                elif k == "keys":
                    dve.wait_ge(cmp_full, 3)
                    V.tensor_tensor(v_blk, bank[1][:, 0:DH].unsqueeze(1).broadcast_to([P, 8, DH]),
                                    blk.unsqueeze(2).broadcast_to([P, 8, DH]), ALU.mult).then_inc(cmp_dve, 1)
                elif k == "scores":
                    dve.wait_ge(cmp_full, 4)
                    c3 = cs.rearrange("p t a b n -> p (t a b) n")
                    bc = [P, NT * 8, NCMP]
                    flat = [v.rearrange("p t h -> p (t h)") for v in (cmx, cden, cz, ccf)]
                    chain(V.tensor_tensor(cs.rearrange("p t a b n -> p (t a b n)"), bank[0][:, 0:NT * P],
                                          ctab.rearrange("p t a b n -> p (t a b n)"), ALU.add))
                    chain(V.tensor_reduce(flat[0], c3, AX, ALU.max))
                    V.tensor_tensor(c3, c3, flat[0].unsqueeze(2).broadcast_to(bc), ALU.subtract).then_inc(cmp_dve, 1)
                elif k == "norm":
                    c3 = cs.rearrange("p t a b n -> p (t a b) n")
                    bc = [P, NT * 8, NCMP]
                    flat = [v.rearrange("p t h -> p (t h)") for v in (cmx, cden, cz, ccf)]
                    dve.wait_ge(cmp_act, 3)
                    chain(V.tensor_tensor(c3, c3, cmask.rearrange("p t a b n -> p (t a b) n"), ALU.mult))
                    chain(V.tensor_reduce(flat[1], c3, AX, ALU.add))
                    chain(V.tensor_scalar(flat[2], flat[1], 0.0, None, ALU.is_equal))
                    chain(V.tensor_tensor(flat[1], flat[1], flat[2], ALU.add))
                    chain(V.reciprocal(flat[3], flat[1]))
                    gt = gates[:, :, :, 0].rearrange("p t (b a) -> p t a b", b=2)
                    v = ccf.rearrange("p t (a b) -> p t a b", a=4)
                    chain(V.tensor_tensor(v, v, gt, ALU.mult))
                    V.tensor_tensor(c3, c3, flat[3].unsqueeze(2).broadcast_to(bc), ALU.mult).then_inc(cmp_dve, 1)

            def add_out(t, first_bank):
                for hf in range(2):
                    v = xs[:, t, hf * 512:(hf + 1) * 512]
                    last = V.tensor_tensor(v, v, bank[first_bank + 2 * t + hf][:], ALU.add)
                last.then_inc(x_ready, 1)

            def mixer(layer):
                normed(2 * layer)
                norm_drain(2 * layer)
                if layer:
                    dve.wait_ge(gate_exp, 1)
                    v = gates.rearrange("p t h c -> p (t h c)")
                    chain(V.tensor_scalar(v, v, 1.0, None, ALU.add))
                    V.reciprocal(v, v).then_inc(gate_ready, 1)
                waited = False
                for what, *arg in DRAIN_ORDER[layer]:
                    if what == "unit":
                        if arg[1] == "dve":
                            normed_unit(layer, arg[0], arg[2])
                        unit[0] += 1
                    elif what == "turn":
                        if arg[0] == "qa":
                            dve.wait_ge(consts, N_CONST)
                        src, which, who, count = TURNS[arg[0]]
                        dst, scale = TDST[arg[0]]
                        if src < 2:
                            drain_b(dst[:, 2:4, :].rearrange("p a b -> p (a b)"), scale)
                        elif which == "b":
                            drain_b(dst, scale, cols=S)
                    elif what == "cmp":
                        cmp_stage(arg[0])
                    elif what == "steps":
                        if not waited:
                            dve.wait_ge(tables, layer + 1)
                            waited = True
                        for i in range(arg[0], arg[1]):
                            step(JOBS[layer], i, layer)
                dve.wait_ge(mix_tile, layer + 1)
                add_out(0, 0)
                dve.wait_ge(wo_used, OUT_UNITS * (layer + 1))
                add_out(1, 0)

            def first_max(p, width, mxv, eq, idx, oh):
                iota = iota8[:, :, 0:width]
                chain(V.tensor_reduce(mxv, p, AX, ALU.max))
                for t in range(NT):
                    chain.count(V.scalar_tensor_tensor(out=eq[:, t, :], in0=p[:, t, :], scalar=mxv[:, t:t + 1],
                                                       in1=iota[:, t, :], op0=ALU.is_equal, op1=ALU.mult))
                chain.wait()
                chain(V.tensor_reduce(idx, eq, AX, ALU.min))
                chain(V.tensor_tensor(oh, iota, idx.unsqueeze(2).broadcast_to([P, NT, width]), ALU.is_equal))

            def route(l):
                n36 = NG + NE
                dve.wait_ge(rt_full, 2 * l + 1)
                v = bank[0][:, 0:NT * 64].rearrange("p (t c) -> p t c", t=NT)[:, :, 0:n36]
                for t in range(NT):
                    chain.count(V.scalar_tensor_tensor(out=lg[:, t, :], in0=v[:, t, :], scalar=rstd[:, t:t + 1],
                                                       in1=b_rt[:, l, :], op0=ALU.mult, op1=ALU.add))
                chain.wait()
                gl = lg[:, :, 0:NG]
                first_max(gl, NG, r_gm, g_eq, r_i, g_oh)
                V.tensor_tensor(ge, gl, r_gm.unsqueeze(2).broadcast_to([P, NT, NG]), ALU.subtract).then_inc(rt_gs, 1)
                el = lg[:, :, NG:].rearrange("p t (g e) -> p t g e", g=NG)
                w4 = wtmp.rearrange("p t (g e) -> p t g e", g=NG)
                goh = g_oh.unsqueeze(3).broadcast_to([P, NT, NG, EG])
                chain(V.tensor_tensor(w4, el, goh, ALU.mult))
                chain(V.tensor_reduce(we, w4.rearrange("p t g e -> p t e g"), AX, ALU.add))
                first_max(we, EG, r_m1, e_eq, r_i, oh1)
                chain(V.scalar_tensor_tensor(out=we, in0=oh1, scalar=3 * NEG, in1=we, op0=ALU.mult, op1=ALU.add))
                first_max(we, EG, r_m2, e_eq, r_i, oh2)
                V.tensor_tensor(r_s, r_m2, r_m1, ALU.subtract).then_inc(rt_ws, 1)
                for j, oh in enumerate((oh1, oh2)):
                    chain.count(V.tensor_tensor(f12[:, j].rearrange("p t (g e) -> p t g e", g=NG), goh,
                                                oh.unsqueeze(2).broadcast_to([P, NT, NG, EG]), ALU.mult))
                chain.wait()
                V.tensor_tensor(mask, f12[:, 0], f12[:, 1], ALU.add).then_inc(rt_mask, 1)
                dve.wait_ge(rt_ge, l + 1)
                chain(V.tensor_reduce(r_pg, ge, AX, ALU.add))
                dve.wait_ge(rt_we, l + 1)
                chain(V.tensor_scalar(r_ws, r_s, 1.0, None, ALU.add))
                chain(V.tensor_tensor(r_ws, r_ws, r_pg, ALU.mult))
                chain(V.reciprocal(r_m1, r_ws))
                chain(V.tensor_tensor(r_m2, r_m1, r_s, ALU.mult))
                dve.wait_ge(rt_full, 2 * l + 2)
                n7 = S // TILE - 1
                bc = [P, NT, NE]
                rank = bank[1][:, 0:2 * NE].rearrange("p (t e) -> p t e", t=NT)
                chain.count(V.tensor_tensor(qe, rank, first_q[:].unsqueeze(1).broadcast_to(bc), ALU.add))
                chain(V.tensor_tensor(cmp7, bank[1][:, 2 * NE:3 * NE].unsqueeze(2).broadcast_to([P, NE, n7]),
                                      steps7[:].unsqueeze(1).broadcast_to([P, NE, n7]), ALU.is_gt))
                chain(V.tensor_reduce(tov, cmp7, AX, ALU.add))
                chain(V.tensor_tensor_scan(vin, ones[:, 0:NE], tov, 0.0, ALU.mult, ALU.add))
                chain(V.tensor_tensor(vex, vin, tov, ALU.subtract))
                chain(V.scalar_tensor_tensor(out=dq, in0=vex, scalar=float(TILE), in1=first_far[:],
                                             op0=ALU.mult, op1=ALU.subtract))
                chain(V.scalar_tensor_tensor(out=over, in0=rank, scalar=float(TILE), in1=dq.unsqueeze(1).broadcast_to(bc),
                                             op0=ALU.is_ge, op1=ALU.mult))
                chain(V.tensor_tensor(qe, qe, over, ALU.add))
                for j in range(2):
                    chain.count(V.tensor_tensor(f12[:, j], f12[:, j], qe, ALU.mult))
                chain.wait()
                V.tensor_reduce(r_q, f12, AX, ALU.add).then_inc(q_ready[l], 1)

            def batch_list():
                bc = [P, MAXOVER, NE]

                def row(v):
                    return v.unsqueeze(1).broadcast_to(bc)
                j = iota_j[:].unsqueeze(2).broadcast_to(bc)
                chain(V.tensor_tensor(ov[0], j, row(vex), ALU.is_ge))
                chain(V.tensor_tensor(ov[1], j, row(vin), ALU.is_lt))
                chain(V.tensor_tensor(ov[2], ov[0], ov[1], ALU.mult))
                chain(V.tensor_tensor(ov[0], ov[2], row(iota_e[:]), ALU.mult))
                chain(V.tensor_reduce(ovr, ov[0], AX, ALU.add))
                chain(V.tensor_copy(ove_i[:], ovr))
                chain(V.tensor_tensor(nb_f, vin[:, NE - 1:NE].broadcast_to([P, GROUPS]),
                                      iota_j[:, 0:MAXOVER:GROUPS], ALU.is_gt))
                chain(V.tensor_reduce(nb_s, nb_f, AX, ALU.add))
                V.tensor_scalar(nb_i[:], nb_s, float(OWN), None, ALU.add).then_inc(list_ready, 1)

            def moe(l):
                norm_drain(2 * l + 1)
                normed(2 * l + 1)
                route(l)

                def onehots(b, ch, first=False):
                    if not first:
                        ch(V.tensor_scalar(r_q, r_q, float(-P), None, ALU.add))
                    for t in range(NT):
                        ch.count(V.tensor_scalar(ctmp[:, t, :], iota_s[:], r_q[:, 1, t:t + 1], None, ALU.is_equal))
                    ch.wait()
                    for t in range(NT):
                        last = V.scalar_tensor_tensor(out=oneh[:, t, :], in0=iota_s[:], scalar=r_q[:, 0, t:t + 1],
                                                      in1=ctmp[:, t, :], op0=ALU.is_equal, op1=ALU.add)
                    last.then_inc(b_ready[l], 1)

                def inputs(b):
                    for hf in range(2):
                        dve.wait_ge(ga_full[l], 2 * b + hf + 1)
                        V.tensor_tensor(xt[:, 4 * hf:4 * hf + 4, :], bank[2 + hf][:].rearrange("p (k q) -> p k q", k=4),
                                        g_col[:, 2 * l + 1, 4 * hf:4 * hf + 4].unsqueeze(2).broadcast_to([P, 4, P]),
                                        ALU.mult).then_inc(xt_ready[l], 1)

                def batch(b, before):
                    ch = Chain(dve, loop_dve[l], before)
                    dve.wait_ge(ga_full[l], 2 * b + 2)
                    onehots(b + 1, ch)
                    dve.wait_ge(en_ready[l], b + 1)
                    ch(V.tensor_scalar(en, en, 1.0, None, ALU.add))
                    ch(V.reciprocal(en, en))
                    ch(V.tensor_tensor(en, en, bank[0][:, 0:FF], ALU.mult))
                    V.tensor_tensor(hid, en, bank[0][:, FF:], ALU.mult).then_inc(hid_ready[l], 1)
                    inputs(b + 1)
                    dve.wait_ge(y_full[l], b + 1)
                    V.tensor_copy(yb[:, 512:], bank[3][:]).then_inc(y_dve[l], 1)
                    return ch.n

                dve.wait_ge(q_ready[l], 1)
                onehots(0, chain, first=True)
                inputs(0)
                batch_list()
                dve.wait_ge(c_copied, l + 1)
                per = batch(0, 0)
                nb = dve.value_load(nb_i[0:1, 0:1], min_val=OWN, max_val=MAXB)
                with dve.Fori(1, nb) as b:
                    batch(b, b * per)
                dve.wait_ge(added[l], nb)
                for t in range(NT):
                    add_out(t, 4)

            mixer(0)
            moe(0)
            mixer(1)
            moe(1)


_INS = ['x', 'ev_norm', 'ev_w_in', 'ev_q_norm', 'ev_k_norm', 'ev_sink', 'ev_w_out',
        'od_norm', 'od_w_in', 'od_c_q_norm', 'od_c_k_norm', 'od_d_q_norm', 'od_d_k_norm',
        'od_cmp_pos', 'od_cmp_w', 'od_w_out',
        'moe_norm', 'moe_w_grp', 'moe_b_grp', 'moe_w_exp', 'moe_b_exp', 'moe_w_gate', 'moe_w_up', 'moe_w_down']
_OUTS = [((1, S, D), 'float32')]


def kernel(**inputs):
    import numpy as _np
    import concourse.bacc as _bacc
    from concourse import mybir as _mybir
    from concourse.bass_utils import run_bass_kernel_spmd as _run

    nc = _bacc.Bacc("TRN2", target_bir_lowering=False, num_devices=1)
    arrays, args = {}, []
    for name in _INS:
        a = _np.ascontiguousarray(inputs[name])
        arrays[f"in_{name}_dram"] = a
        args.append(nc.dram_tensor(f"in_{name}_dram", a.shape, _mybir.dt.from_np(a.dtype), kind="ExternalInput").ap())
    for i, (shape, dtype) in enumerate(_OUTS):
        dt = _mybir.dt.from_np(_np.dtype(dtype))
        args.append(nc.dram_tensor(f"out_{i}_dram", shape, dt, kind="ExternalOutput").ap())
    program(nc, *args)
    r = _run(nc, [arrays], core_ids=[0])
    got = tuple(r.results[0][f"out_{i}_dram"] for i in range(len(_OUTS)))
    return got[0]
```
